# Optimizing a Trainium2 kernel written in Bass

```python
import jax, jax.numpy as jnp
from jax import lax
import numpy as np
import math

D_MODEL = 1024
BATCH = 1
SEQ = 512
DEPTH = 2

GRID_W = 64
CTX_LEN = 256
N_EVEN = (DEPTH + 1) // 2
N_ODD = DEPTH // 2
RMS_EPS = 1e-6

POOL_WIDTH = D_MODEL // 2
POOL_WINDOWS = (2, 4, 8, 16)
POOL_GROUP = POOL_WIDTH // len(POOL_WINDOWS)
HG_WIDTH = D_MODEL // 2
HG_HEAD_DIM = 128
HG_HEADS = HG_WIDTH // HG_HEAD_DIM
HG_CHUNK = 64
AB_IN = POOL_WIDTH + 5 * HG_WIDTH
AB_MIX = POOL_WIDTH + HG_WIDTH
ATT_HEAD_DIM = 128
ATT_HEADS = D_MODEL // ATT_HEAD_DIM
ATT_KV_HEADS = 2
ATT_GROUP = ATT_HEADS // ATT_KV_HEADS
ATT_IN = (ATT_HEADS + 2 * ATT_KV_HEADS) * ATT_HEAD_DIM
Q_BLOCK = 128
ROPE_THETA = 10000.0
FFN_HIDDEN = ((8 * D_MODEL + 3 * 256 - 1) // (3 * 256)) * 256


F32 = jnp.float32

def rmsnorm(x, g):
    xf = x.astype(F32)
    y = xf * lax.rsqrt(jnp.mean(xf * xf, axis=-1, keepdims=True) + RMS_EPS)
    return (y * g.astype(F32)).astype(x.dtype)

def flip(a):
    return a[:, ::-1]

def swiglu(h, w_in, w_out):
    a, b = jnp.split(h @ w_in, 2, axis=-1)
    return (jax.nn.silu(a) * b) @ w_out

def grid_rope(x):
    L = x.shape[1]
    rows = L // GRID_W
    row = jnp.repeat(jnp.arange(rows, dtype=F32), GRID_W)
    col = jnp.tile(jnp.arange(GRID_W, dtype=F32), rows)
    n_freq = ATT_HEAD_DIM // 4
    inv = ROPE_THETA ** (-jnp.arange(n_freq, dtype=F32) / n_freq)

    def rot(xa, pos):
        ang = pos[:, None] * inv[None, :]
        cos = jnp.cos(ang)[:, None, :]
        sin = jnp.sin(ang)[:, None, :]
        x1, x2 = jnp.split(xa, 2, axis=-1)
        return jnp.concatenate([x1 * cos - x2 * sin, x2 * cos + x1 * sin], axis=-1)

    xf = x.astype(F32)
    half = ATT_HEAD_DIM // 2
    return jnp.concatenate([rot(xf[..., :half], row), rot(xf[..., half:], col)], axis=-1).astype(x.dtype)

def multiscale_pool(u, pool_w, pool_scale):
    Bn, Ln, _ = u.shape
    cs = jnp.pad(jnp.cumsum(u.astype(F32), axis=1), ((0, 0), (1, 0), (0, 0)))
    t = jnp.arange(Ln)
    groups = []
    for gi, w in enumerate(POOL_WINDOWS):
        lo = jnp.clip(t - w // 2, 0, Ln)
        hi = jnp.clip(t - w // 2 + w, 0, Ln)
        sl = slice(gi * POOL_GROUP, (gi + 1) * POOL_GROUP)
        csg = cs[..., sl]
        mean = (csg[:, hi] - csg[:, lo]) / (hi - lo).astype(F32)[None, :, None]
        groups.append(mean - u[..., sl].astype(F32))
    y = jnp.stack(groups, axis=2).astype(u.dtype)
    y = jnp.einsum('blgc,gcd->blgd', y, pool_w).reshape(Bn, Ln, POOL_WIDTH)
    return y * pool_scale

def hgrn_scan(q, k, v, logf, s0):
    Bn, Ln, H, _ = q.shape
    dv = v.shape[-1]
    n = Ln // HG_CHUNK

    def chunks(a):
        return jnp.moveaxis(a.reshape(Bn, n, HG_CHUNK, H, a.shape[-1]), 1, 0)

    causal = jnp.tril(jnp.ones((HG_CHUNK, HG_CHUNK), dtype=bool))[None, :, :, None, None]

    def step(S, inp):
        qc, kc, vc, gc = inp
        b = jnp.cumsum(gc, axis=1)
        dec = jnp.exp(jnp.where(causal, b[:, :, None] - b[:, None, :], -jnp.inf))
        a = jnp.einsum('bthd,btshd->btsh', qc, dec * kc[:, None])
        o = jnp.einsum('btsh,bshe->bthe', a, vc) + jnp.einsum('bthd,bhde->bthe', qc * jnp.exp(b), S)
        b_last = b[:, -1]
        S = jnp.exp(b_last)[..., None] * S + jnp.einsum('bshd,bshe->bhde', kc * jnp.exp(b_last[:, None] - b), vc)
        return S, o

    s_fin, o = lax.scan(step, s0, (chunks(q), chunks(k), chunks(v), chunks(logf)))
    return jnp.moveaxis(o, 0, 1).reshape(Bn, Ln, H, dv), s_fin

def pool_hgrn_mixer(h_lat, h_ctx, w_in, w_out, pool_w, pool_scale, lb, onorm_g, need_ctx):
    def project(h):
        z = h @ w_in
        Bn, Ln = z.shape[:2]
        u = z[..., :POOL_WIDTH]
        q, zf, zb, v, g = jnp.split(z[..., POOL_WIDTH:], 5, axis=-1)
        heads = lambda a: a.reshape(Bn, Ln, HG_HEADS, HG_HEAD_DIM).astype(F32)
        return u, heads(jax.nn.silu(q)), heads(zf), heads(zb), heads(v), g

    def gate(z, lb_dir):
        f = lb_dir + (1.0 - lb_dir) * jax.nn.sigmoid(z)
        return 1.0 - f, jnp.log(f)

    lb_f = lb[0].reshape(HG_HEADS, HG_HEAD_DIM)
    lb_b = lb[1].reshape(HG_HEADS, HG_HEAD_DIM)
    u_c, q_c, zf_c, zb_c, v_c, g_c = project(h_ctx)
    u_l, q_l, zf_l, zb_l, v_l, g_l = project(h_lat)
    k_cf, lf_cf = gate(zf_c, lb_f)
    k_cb, lf_cb = gate(zb_c, lb_b)
    k_lf, lf_lf = gate(zf_l, lb_f)
    k_lb, lf_lb = gate(zb_l, lb_b)

    s0 = jnp.zeros((h_ctx.shape[0], HG_HEADS, HG_HEAD_DIM, HG_HEAD_DIM), F32)
    o_cf, s_f = hgrn_scan(q_c, k_cf, v_c, lf_cf, s0)
    o_cb, s_b = hgrn_scan(flip(q_c), flip(k_cb), flip(v_c), flip(lf_cb), s0)
    o_lf, _ = hgrn_scan(q_l, k_lf, v_l, lf_lf, s_f)
    o_lb, _ = hgrn_scan(flip(q_l), flip(k_lb), flip(v_l), flip(lf_lb), s_b)

    def readout(o_sum, g, u):
        Bn, Ln = g.shape[:2]
        o = rmsnorm(o_sum, onorm_g).reshape(Bn, Ln, HG_WIDTH).astype(g.dtype) * jax.nn.silu(g)
        return jnp.concatenate([multiscale_pool(u, pool_w, pool_scale), o], axis=-1) @ w_out

    y_lat = readout(o_lf + flip(o_lb), g_l, u_l)
    y_ctx = readout(o_cf + flip(o_cb), g_c, u_c) if need_ctx else None
    return y_lat, y_ctx

def gqa_mixer(h_lat, h_ctx, w_in, w_out, qn_g, kn_g, need_ctx):
    dh = ATT_HEAD_DIM

    def project(h):
        z = h @ w_in
        Bn, Ln = z.shape[:2]
        q = z[..., :ATT_HEADS * dh].reshape(Bn, Ln, ATT_HEADS, dh)
        k = z[..., ATT_HEADS * dh:(ATT_HEADS + ATT_KV_HEADS) * dh].reshape(Bn, Ln, ATT_KV_HEADS, dh)
        v = z[..., (ATT_HEADS + ATT_KV_HEADS) * dh:].reshape(Bn, Ln, ATT_KV_HEADS, dh)
        return rmsnorm(q, qn_g), rmsnorm(k, kn_g), v

    Bn, L, _ = h_lat.shape
    Lc = h_ctx.shape[1]
    q_l, k_l, v_l = project(h_lat)
    q_c, k_c, v_c = project(h_ctx)
    q_l = grid_rope(q_l)
    k_l = grid_rope(k_l)
    k_all = jnp.concatenate([k_l, k_c], axis=1)
    v_all = jnp.concatenate([v_l, v_c], axis=1)
    scale = dh ** -0.5

    def attend(qb, k, v):
        s = jnp.einsum('bqhgd,bkhd->bhgqk', qb, k, preferred_element_type=F32) * scale
        p = jax.nn.softmax(s, axis=-1).astype(v.dtype)
        return jnp.einsum('bhgqk,bkhd->bqhgd', p, v)

    q_blocks = jnp.moveaxis(q_l.reshape(Bn, L // Q_BLOCK, Q_BLOCK, ATT_KV_HEADS, ATT_GROUP, dh), 1, 0)
    o = lax.map(lambda qb: attend(qb, k_all, v_all), q_blocks)
    y_lat = jnp.moveaxis(o, 0, 1).reshape(Bn, L, ATT_HEADS * dh) @ w_out
    y_ctx = None
    if need_ctx:
        o_c = attend(q_c.reshape(Bn, Lc, ATT_KV_HEADS, ATT_GROUP, dh), k_c, v_c)
        y_ctx = o_c.reshape(Bn, Lc, ATT_HEADS * dh) @ w_out
    return y_lat, y_ctx

def first_inputs(seed: int = 0) -> dict:
    key = jax.random.key(seed)
    ks = jax.random.split(key, 20)
    D = D_MODEL
    nrm = lambda k, shape, s: jax.random.normal(k, shape, F32) * s
    return {
        "x": nrm(ks[0], (BATCH, SEQ, D), 1.0),
        "c": nrm(ks[1], (BATCH, D), 1.0),
        "ctx": nrm(ks[2], (BATCH, CTX_LEN, D), 1.0),
        "c_ctx": nrm(ks[3], (D,), 1.0),
        "ada_w": nrm(ks[4], (DEPTH, D, 6 * D), 0.5 * D ** -0.5),
        "ada_b": nrm(ks[5], (DEPTH, 6 * D), 0.02),
        "norm_g": 1.0 + nrm(ks[6], (DEPTH, 4, D), 0.02),
        "ab_w_in": nrm(ks[7], (N_EVEN, D, AB_IN), D ** -0.5),
        "ab_w_out": nrm(ks[8], (N_EVEN, AB_MIX, D), AB_MIX ** -0.5),
        "pool_w": nrm(ks[9], (N_EVEN, len(POOL_WINDOWS), POOL_GROUP, POOL_GROUP), POOL_GROUP ** -0.5),
        "pool_scale": 1.0 + nrm(ks[10], (N_EVEN, POOL_WIDTH), 0.1),
        "hg_lower": nrm(ks[11], (N_EVEN + 1, 2, HG_WIDTH), 0.1),
        "hg_onorm_g": 1.0 + nrm(ks[12], (N_EVEN, HG_HEAD_DIM), 0.02),
        "att_w_in": nrm(ks[13], (N_ODD, D, ATT_IN), D ** -0.5),
        "att_w_out": nrm(ks[14], (N_ODD, ATT_HEADS * ATT_HEAD_DIM, D), (ATT_HEADS * ATT_HEAD_DIM) ** -0.5),
        "att_qnorm_g": 1.0 + nrm(ks[15], (N_ODD, ATT_HEAD_DIM), 0.02),
        "att_knorm_g": 1.0 + nrm(ks[16], (N_ODD, ATT_HEAD_DIM), 0.02),
        "ffn_w_in": nrm(ks[17], (DEPTH, D, 2 * FFN_HIDDEN), D ** -0.5),
        "ffn_w_out": nrm(ks[18], (DEPTH, FFN_HIDDEN, D), FFN_HIDDEN ** -0.5),
    }

def first_block(x, c, ctx, c_ctx, ada_w, ada_b, norm_g, ab_w_in, ab_w_out, pool_w, pool_scale,
              hg_lower, hg_onorm_g, att_w_in, att_w_out, att_qnorm_g, att_knorm_g, ffn_w_in, ffn_w_out):
    lb_all = jnp.cumsum(jax.nn.softmax(hg_lower.astype(F32), axis=0), axis=0)
    ctx_s = ctx
    for l in range(DEPTH):
        j = l // 2
        need_ctx = l < DEPTH - 1
        m_lat = (jax.nn.silu(c) @ ada_w[l] + ada_b[l])[:, None]
        m_ctx = jax.nn.silu(c_ctx) @ ada_w[l] + ada_b[l]
        sh1, sc1, g1, sh2, sc2, g2 = jnp.split(m_lat, 6, axis=-1)
        csh1, csc1, cg1, csh2, csc2, cg2 = jnp.split(m_ctx, 6, axis=-1)

        h_lat = rmsnorm(x, norm_g[l, 0]) * (1.0 + sc1) + sh1
        h_ctx = rmsnorm(ctx_s, norm_g[l, 0]) * (1.0 + csc1) + csh1
        if l % 2 == 0:
            y_lat, y_ctx = pool_hgrn_mixer(h_lat, h_ctx, ab_w_in[j], ab_w_out[j], pool_w[j], pool_scale[j],
                                           lb_all[j], hg_onorm_g[j], need_ctx)
        else:
            y_lat, y_ctx = gqa_mixer(h_lat, h_ctx, att_w_in[j], att_w_out[j], att_qnorm_g[j], att_knorm_g[j],
                                     need_ctx)
        x = x + g1 * rmsnorm(y_lat, norm_g[l, 1])
        f_lat = swiglu(rmsnorm(x, norm_g[l, 2]) * (1.0 + sc2) + sh2, ffn_w_in[l], ffn_w_out[l])
        x = x + g2 * rmsnorm(f_lat, norm_g[l, 3])

        if need_ctx:
            ctx_s = ctx_s + cg1 * rmsnorm(y_ctx, norm_g[l, 1])
            f_ctx = swiglu(rmsnorm(ctx_s, norm_g[l, 2]) * (1.0 + csc2) + csh2, ffn_w_in[l], ffn_w_out[l])
            ctx_s = ctx_s + cg2 * rmsnorm(f_ctx, norm_g[l, 3])
    return x


N_A_LAYERS = DEPTH // 2
N_B_LAYERS = DEPTH - N_A_LAYERS
GATED_NORM_EPS = 1e-5

SSM_EXPAND = 2
SSM_D_INNER = SSM_EXPAND * D_MODEL
SSM_HEAD_DIM = 64
SSM_N_HEADS = SSM_D_INNER // SSM_HEAD_DIM
SSM_N_GROUPS = 8
SSM_D_STATE = 128
SSM_CONV = 4
SSM_CHUNK = 128
SSM_CONV_DIM = SSM_D_INNER + 2 * SSM_N_GROUPS * SSM_D_STATE
SSM_IN_DIM = SSM_D_INNER + SSM_CONV_DIM + SSM_N_HEADS

ATT_PATTERNS = ((128, 1), (512, 4), (2048, 16))
ATT_N_GROUPS = len(ATT_PATTERNS)
ATT_HEADS_PER_GROUP = 8
ATT_KV_HEADS_PER_GROUP = 2
ATT_Q_DIM = ATT_N_GROUPS * ATT_HEADS_PER_GROUP * ATT_HEAD_DIM
ATT_KV_DIM = ATT_N_GROUPS * ATT_KV_HEADS_PER_GROUP * ATT_HEAD_DIM
ATT_OUT_DIM = ATT_HEADS_PER_GROUP * ATT_HEAD_DIM
ROPE_DIM = ATT_HEAD_DIM // 4
ROPE_THETA_2 = 500000.0

FFN_DIM = 2816
FFN_CONV = 3


def _rms_norm(x, w, eps=RMS_EPS):
    xf = x.astype(jnp.float32)
    y = xf * lax.rsqrt(jnp.mean(xf * xf, axis=-1, keepdims=True) + eps)
    return (y * w.astype(jnp.float32)).astype(x.dtype)

def _causal_depthwise_conv(x, w):
    width, ch = w.shape
    return lax.conv_general_dilated(
        x, w[:, None, :].astype(x.dtype), window_strides=(1,),
        padding=((width - 1, 0),), dimension_numbers=('NWC', 'WIO', 'NWC'),
        feature_group_count=ch)

def _partial_rotary(x, positions):
    half = ROPE_DIM // 2
    inv_freq = jnp.power(jnp.float32(ROPE_THETA_2), -jnp.arange(0, ROPE_DIM, 2, dtype=jnp.float32) / ROPE_DIM)
    ang = positions.astype(jnp.float32)[:, None] * inv_freq[None, :]
    cos = jnp.cos(ang)[None, :, None, :]
    sin = jnp.sin(ang)[None, :, None, :]
    xf = x.astype(jnp.float32)
    x1, x2, rest = xf[..., :half], xf[..., half:ROPE_DIM], xf[..., ROPE_DIM:]
    out = jnp.concatenate([x1 * cos - x2 * sin, x2 * cos + x1 * sin, rest], axis=-1)
    return out.astype(x.dtype)

def _ssd_chunked(x, dt, a, b_in, c_in):
    bsz, seq, nh, hp = x.shape
    ng, ns = b_in.shape[2], b_in.shape[3]
    hg = nh // ng
    nc, L = seq // SSM_CHUNK, SSM_CHUNK
    xc = (x.astype(jnp.float32) * dt[..., None]).reshape(bsz, nc, L, ng, hg, hp)
    adt = (dt * a).reshape(bsz, nc, L, ng, hg).transpose(0, 1, 3, 4, 2)
    a_cs = jnp.cumsum(adt, axis=-1)
    bc = b_in.astype(jnp.float32).reshape(bsz, nc, L, ng, ns)
    cc = c_in.astype(jnp.float32).reshape(bsz, nc, L, ng, ns)
    tril = jnp.tril(jnp.ones((L, L), dtype=bool))
    seg = a_cs[..., :, None] - a_cs[..., None, :]
    decay = jnp.exp(jnp.where(tril, seg, -jnp.inf))
    cb = jnp.einsum('bclgn,bcsgn->bcgls', cc, bc)
    y_diag = jnp.einsum('bcgls,bcghls,bcsghp->bclghp', cb, decay, xc)
    decay_states = jnp.exp(a_cs[..., -1:] - a_cs)
    states = jnp.einsum('bclgn,bcghl,bclghp->bcghpn', bc, decay_states, xc)
    chunk_decay = jnp.exp(a_cs[..., -1])

    def step(h, inp):
        st, dec = inp
        return h * dec[..., None, None] + st, h

    h0 = jnp.zeros((bsz, ng, hg, hp, ns), jnp.float32)
    _, prev = lax.scan(step, h0, (jnp.moveaxis(states, 1, 0), jnp.moveaxis(chunk_decay, 1, 0)))
    prev = jnp.moveaxis(prev, 0, 1)
    y_off = jnp.einsum('bclgn,bcghpn,bcghl->bclghp', cc, prev, jnp.exp(a_cs))
    return (y_diag + y_off).reshape(bsz, seq, nh, hp)

def _mamba2_mixer(h, w_in, conv_w, conv_b, dt_bias, a_log, d_skip, norm_w, w_out):
    bsz, seq, _ = h.shape
    zxbcdt = h @ w_in.astype(h.dtype)
    z = zxbcdt[..., :SSM_D_INNER]
    xbc = zxbcdt[..., SSM_D_INNER:SSM_D_INNER + SSM_CONV_DIM]
    dt_raw = zxbcdt[..., SSM_D_INNER + SSM_CONV_DIM:]
    xbc = jax.nn.silu(_causal_depthwise_conv(xbc, conv_w) + conv_b.astype(h.dtype))
    gn = SSM_N_GROUPS * SSM_D_STATE
    xs = xbc[..., :SSM_D_INNER].reshape(bsz, seq, SSM_N_HEADS, SSM_HEAD_DIM)
    b_in = xbc[..., SSM_D_INNER:SSM_D_INNER + gn].reshape(bsz, seq, SSM_N_GROUPS, SSM_D_STATE)
    c_in = xbc[..., SSM_D_INNER + gn:].reshape(bsz, seq, SSM_N_GROUPS, SSM_D_STATE)
    dt = jax.nn.softplus(dt_raw.astype(jnp.float32) + dt_bias.astype(jnp.float32))
    a = -jnp.exp(a_log.astype(jnp.float32))
    y = _ssd_chunked(xs, dt, a, b_in, c_in)
    y = y + xs.astype(jnp.float32) * d_skip.astype(jnp.float32)[:, None]
    y = y.reshape(bsz, seq, SSM_D_INNER) * jax.nn.silu(z.astype(jnp.float32))
    yg = y.reshape(bsz, seq, SSM_N_GROUPS, SSM_D_INNER // SSM_N_GROUPS)
    yg = yg * lax.rsqrt(jnp.mean(yg * yg, axis=-1, keepdims=True) + GATED_NORM_EPS)
    y = yg.reshape(bsz, seq, SSM_D_INNER) * norm_w.astype(jnp.float32)
    return y.astype(h.dtype) @ w_out.astype(h.dtype)

def _shared_kv(x, kv_norm, w_kv, positions):
    bsz, seq, _ = x.shape
    kv = (_rms_norm(x, kv_norm) @ w_kv.astype(x.dtype)).reshape(
        bsz, seq, 2, ATT_N_GROUPS * ATT_KV_HEADS_PER_GROUP, ATT_HEAD_DIM)
    k = _partial_rotary(kv[:, :, 0], positions).reshape(bsz, seq, ATT_N_GROUPS, ATT_KV_HEADS_PER_GROUP, ATT_HEAD_DIM)
    v = kv[:, :, 1].reshape(bsz, seq, ATT_N_GROUPS, ATT_KV_HEADS_PER_GROUP, ATT_HEAD_DIM)
    return k, v

def _dilated_group_attention(q, k, v, window, dilation):
    bsz, seq, n_heads, hd = q.shape
    n_kv = k.shape[2]
    rep = n_heads // n_kv
    blk = window // dilation
    n_sub = seq // dilation
    n_blk = -(-n_sub // blk)
    n_pad = n_blk * blk

    def to_blocks(t):
        t = jnp.moveaxis(t.reshape(bsz, n_sub, dilation, *t.shape[2:]), 2, 1)
        pad = [(0, 0)] * t.ndim
        pad[2] = (0, n_pad - n_sub)
        t = jnp.pad(t, pad)
        return t.reshape(bsz, dilation, n_blk, blk, *t.shape[3:])

    def with_prev(t):
        prev = jnp.pad(t[:, :, :-1], ((0, 0), (0, 0), (1, 0), (0, 0), (0, 0), (0, 0)))
        return jnp.concatenate([prev, t], axis=3)

    qb = to_blocks(q.astype(jnp.float32)).reshape(bsz, dilation, n_blk, blk, n_kv, rep, hd)
    kb = with_prev(to_blocks(k.astype(jnp.float32)))
    vb = with_prev(to_blocks(v.astype(jnp.float32)))
    scores = jnp.einsum('brnqhgd,brnshd->brnhgqs', qb, kb) * (hd ** -0.5)
    q_idx = jnp.arange(blk)[:, None]
    s_idx = jnp.arange(2 * blk)[None, :]
    rel = q_idx + blk - s_idx
    band = (rel >= 0) & (rel <= blk)
    has_prev = (jnp.arange(n_blk) > 0)[:, None, None] | (s_idx >= blk)[None]
    mask = band[None] & has_prev
    scores = jnp.where(mask[:, None, None], scores, -jnp.inf)
    m = jnp.max(scores, axis=-1, keepdims=True)
    p = jnp.exp(scores - m)
    denom = jnp.sum(p, axis=-1)
    lse = jnp.transpose(m[..., 0] + jnp.log(denom), (0, 1, 2, 5, 3, 4))
    out = jnp.einsum('brnhgqs,brnshd->brnqhgd', p, vb) / jnp.transpose(denom, (0, 1, 2, 5, 3, 4))[..., None]

    def from_blocks(t):
        t = t.reshape(bsz, dilation, n_pad, n_heads, *t.shape[6:])[:, :, :n_sub]
        return jnp.moveaxis(t, 1, 2).reshape(bsz, seq, n_heads, *t.shape[4:])

    return from_blocks(out), from_blocks(lse)

def _dilated_mixer(h, k_sh, v_sh, w_q, w_o, positions):
    bsz, seq, _ = h.shape
    q = (h @ w_q.astype(h.dtype)).reshape(bsz, seq, ATT_N_GROUPS * ATT_HEADS_PER_GROUP, ATT_HEAD_DIM)
    q = _partial_rotary(q, positions).reshape(bsz, seq, ATT_N_GROUPS, ATT_HEADS_PER_GROUP, ATT_HEAD_DIM)
    outs, lses = [], []
    for g, (window, dilation) in enumerate(ATT_PATTERNS):
        o_g, lse_g = _dilated_group_attention(q[:, :, g], k_sh[:, :, g], v_sh[:, :, g], window, dilation)
        outs.append(o_g)
        lses.append(lse_g)
    wts = jax.nn.softmax(jnp.stack(lses, axis=0), axis=0)
    o = jnp.einsum('gbsh,gbshd->bshd', wts, jnp.stack(outs, axis=0))
    return o.reshape(bsz, seq, ATT_OUT_DIM).astype(h.dtype) @ w_o.astype(h.dtype)

def _conv_ffn(h, w_up, conv_w, w_down):
    u = _causal_depthwise_conv(h @ w_up.astype(h.dtype), conv_w)
    gate, val = u[..., :FFN_DIM], u[..., FFN_DIM:]
    return (jax.nn.silu(gate) * val) @ w_down.astype(h.dtype)

def second_inputs(seed: int = 0) -> dict:
    key = jax.random.key(seed)
    ks = jax.random.split(key, 24)
    f32 = jnp.float32
    out_scale = (2.0 * DEPTH) ** -0.5

    def nrm(k, shape, scale):
        return jax.random.normal(k, shape, f32) * scale

    x = nrm(ks[0], (BATCH, SEQ, D_MODEL), 1.0)
    a_norm = 1.0 + nrm(ks[1], (N_A_LAYERS, D_MODEL), 0.02)
    ssm_w_in = nrm(ks[2], (N_A_LAYERS, D_MODEL, SSM_IN_DIM), D_MODEL ** -0.5)
    ssm_conv_w = nrm(ks[3], (N_A_LAYERS, SSM_CONV, SSM_CONV_DIM), SSM_CONV ** -0.5)
    ssm_conv_b = nrm(ks[4], (N_A_LAYERS, SSM_CONV_DIM), 0.02)
    dt0 = jnp.exp(jax.random.uniform(ks[5], (N_A_LAYERS, SSM_N_HEADS), f32, math.log(1e-3), math.log(1e-1)))
    ssm_dt_bias = dt0 + jnp.log(-jnp.expm1(-dt0))
    ssm_a_log = jnp.log(jax.random.uniform(ks[6], (N_A_LAYERS, SSM_N_HEADS), f32, 1.0, 16.0))
    ssm_d = 1.0 + nrm(ks[7], (N_A_LAYERS, SSM_N_HEADS), 0.02)
    ssm_norm = 1.0 + nrm(ks[8], (N_A_LAYERS, SSM_D_INNER), 0.02)
    ssm_w_out = nrm(ks[9], (N_A_LAYERS, SSM_D_INNER, D_MODEL), SSM_D_INNER ** -0.5 * out_scale)
    kv_norm = 1.0 + nrm(ks[10], (D_MODEL,), 0.02)
    w_kv = nrm(ks[11], (D_MODEL, 2 * ATT_KV_DIM), D_MODEL ** -0.5)
    b_norm = 1.0 + nrm(ks[12], (N_B_LAYERS, D_MODEL), 0.02)
    att_w_q = nrm(ks[13], (N_B_LAYERS, D_MODEL, ATT_Q_DIM), D_MODEL ** -0.5)
    att_w_o = nrm(ks[14], (N_B_LAYERS, ATT_OUT_DIM, D_MODEL), ATT_OUT_DIM ** -0.5 * out_scale)
    ffn_norm = 1.0 + nrm(ks[15], (DEPTH, D_MODEL), 0.02)
    ffn_w_up = nrm(ks[16], (DEPTH, D_MODEL, 2 * FFN_DIM), D_MODEL ** -0.5)
    ffn_conv_w = nrm(ks[17], (DEPTH, FFN_CONV, 2 * FFN_DIM), FFN_CONV ** -0.5)
    ffn_w_down = nrm(ks[18], (DEPTH, FFN_DIM, D_MODEL), FFN_DIM ** -0.5 * out_scale)
    final_norm = 1.0 + nrm(ks[19], (D_MODEL,), 0.02)
    return {'x': x, 'a_norm': a_norm, 'ssm_w_in': ssm_w_in, 'ssm_conv_w': ssm_conv_w,
            'ssm_conv_b': ssm_conv_b, 'ssm_dt_bias': ssm_dt_bias, 'ssm_a_log': ssm_a_log,
            'ssm_d': ssm_d, 'ssm_norm': ssm_norm, 'ssm_w_out': ssm_w_out, 'kv_norm': kv_norm,
            'w_kv': w_kv, 'b_norm': b_norm, 'att_w_q': att_w_q, 'att_w_o': att_w_o,
            'ffn_norm': ffn_norm, 'ffn_w_up': ffn_w_up, 'ffn_conv_w': ffn_conv_w,
            'ffn_w_down': ffn_w_down, 'final_norm': final_norm}

def second_block(x, a_norm, ssm_w_in, ssm_conv_w, ssm_conv_b, ssm_dt_bias, ssm_a_log, ssm_d,
              ssm_norm, ssm_w_out, kv_norm, w_kv, b_norm, att_w_q, att_w_o,
              ffn_norm, ffn_w_up, ffn_conv_w, ffn_w_down, final_norm):
    positions = jnp.arange(x.shape[1], dtype=jnp.int32)
    k_sh, v_sh = None, None
    for layer in range(DEPTH):
        if layer < N_A_LAYERS:
            i = layer
            x = x + _mamba2_mixer(_rms_norm(x, a_norm[i]), ssm_w_in[i], ssm_conv_w[i], ssm_conv_b[i],
                                  ssm_dt_bias[i], ssm_a_log[i], ssm_d[i], ssm_norm[i], ssm_w_out[i])
        else:
            if layer == N_A_LAYERS:
                k_sh, v_sh = _shared_kv(x, kv_norm, w_kv, positions)
            j = layer - N_A_LAYERS
            x = x + _dilated_mixer(_rms_norm(x, b_norm[j]), k_sh, v_sh, att_w_q[j], att_w_o[j], positions)
        x = x + _conv_ffn(_rms_norm(x, ffn_norm[layer]), ffn_w_up[layer], ffn_conv_w[layer], ffn_w_down[layer])
    return _rms_norm(x, final_norm)


def setup_inputs(seed=0):
    out = dict(first_inputs(seed))
    for name, value in second_inputs(seed + 1).items():
        if name != "x":
            out[name + "_2"] = value
    return out


def reference(
    x, c, ctx, c_ctx, ada_w, ada_b, norm_g, ab_w_in, ab_w_out, pool_w, pool_scale, hg_lower,
    hg_onorm_g, att_w_in, att_w_out, att_qnorm_g, att_knorm_g, ffn_w_in, ffn_w_out, a_norm_2,
    ssm_w_in_2, ssm_conv_w_2, ssm_conv_b_2, ssm_dt_bias_2, ssm_a_log_2, ssm_d_2, ssm_norm_2,
    ssm_w_out_2, kv_norm_2, w_kv_2, b_norm_2, att_w_q_2, att_w_o_2, ffn_norm_2, ffn_w_up_2,
    ffn_conv_w_2, ffn_w_down_2, final_norm_2,
):
    x = first_block(
        x, c, ctx, c_ctx, ada_w, ada_b, norm_g, ab_w_in, ab_w_out, pool_w, pool_scale, hg_lower,
        hg_onorm_g, att_w_in, att_w_out, att_qnorm_g, att_knorm_g, ffn_w_in, ffn_w_out,
    )
    return second_block(
        x, a_norm_2, ssm_w_in_2, ssm_conv_w_2, ssm_conv_b_2, ssm_dt_bias_2, ssm_a_log_2,
        ssm_d_2, ssm_norm_2, ssm_w_out_2, kv_norm_2, w_kv_2, b_norm_2, att_w_q_2, att_w_o_2,
        ffn_norm_2, ffn_w_up_2, ffn_conv_w_2, ffn_w_down_2, final_norm_2,
    )


_drawn_inputs = setup_inputs


def setup_inputs(seed=0):
    import zlib

    import numpy as np

    out = dict(_drawn_inputs(seed))
    spreads = {}
    factors = {'norm_g': 2.796,
     'hg_lower': 8.0,
     'hg_onorm_g': 8.0,
     'att_qnorm_g': 8.0,
     'att_knorm_g': 8.0,
     'a_norm_2': 4.427,
     'ssm_conv_b_2': 4.906,
     'ssm_d_2': 200.0,
     'ssm_norm_2': 6.759,
     'kv_norm_2': 8.0,
     'b_norm_2': 8.0,
     'ffn_norm_2': 6.104}
    for name, (base, spread) in spreads.items():
        noise = np.random.default_rng([zlib.crc32(name.encode()), seed]).standard_normal(out[name].shape)
        drawn = base * np.exp(spread * noise) if base else spread * noise
        out[name] = __import__('jax').numpy.asarray(drawn.astype(out[name].dtype))
    for name, factor in factors.items():
        out[name] = (out[name] * factor).astype(out[name].dtype)
    return out
```

```python
import numpy as np
import concourse.bass as bass
from concourse import mybir
from contextlib import ExitStack

P = 128
D = 1024
ND = D // P
TL, TC = 512, 256
TA = TL + TC
HID = 2816
NH = HID // P
EPS = 1e-6
GEPS = 1e-5
RAW, SPL = 4, 2
KC = 11
NBANK = 4
CH = 128
NCH = TA // CH
HEADS = 4
LEVELS = (64, 32, 16, 8, 4, 2, 1)
DI = 2048
NG = 8
NSH = 32
SCALE = float(P) ** -0.5
NEG = -1e30

VEC = {}
_n = 0
for _name, _w in (("ada_b", 96), ("norm_g", 64), ("pool_scale", 4), ("hg_lower", 16), ("onorm", 1), ("qn", 1), ("kn", 1),
                  ("a_norm", 8), ("conv_w", 128), ("conv_b", 32), ("ssm_norm", 16), ("d_skip", 16), ("kv_norm", 8),
                  ("b_norm", 8), ("ffn_norm", 16), ("ffn_conv", 264), ("final_norm", 8), ("dt_bias", 1), ("a_log", 1)):
    VEC[_name] = (_n, _w)
    _n += _w
NVEC = _n

CST = {}
_n = 0
for _name, _w in (("ident", 128), ("rot1", 128), ("rot2", 128), ("cos1", TL), ("sin1", TL), ("cos2", TL), ("sin2", TL),
                  ("hg_mask", 2 * 6 * 128), ("band", 256), ("dil4", 512), ("dil16", 512), ("pool_inv", 4 * TA), ("ssd_mask", 128)):
    CST[_name] = (_n, _w)
    _n += _w
NCST = _n


STOP = None


def upto(taken, n, seed=0):
    return taken[0], taken[1] + n + seed


class Counts:

    def __init__(self, make):
        self.make, self.sems, self.at = make, {}, {}

    def take(self, name, n):
        if name not in self.sems:
            self.sems[name], self.at[name] = self.make(name), 0
        base = self.at[name]
        self.at[name] += n
        return self.sems[name], base


def build(nc, xT, ctxT, cvec, vecs, cst, ada0, ada1, w_ab_in, w_ab_out, w_pool, w_f0u, w_f0d, w_att_in, w_att_out,
          w_f1u, w_f1d, w_ssm, w_dt, w_ssm_out, w_kv, w_q, w_o, w_f2u, w_f2d, w_f3u, w_f3d, out):
    f32, f32r = mybir.dt.float32, mybir.dt.float32r
    ALU, ACT, AX = mybir.AluOpType, mybir.ActivationFunctionType, mybir.AxisListType
    ctx = ExitStack()
    with ctx:
        base = (nc.sbuf_base + 31) // 32 * 32
        end = nc.sbuf_usable_end
        made = {}

        def at(name, shape, off, dt=f32):
            n = 4
            for s in shape[1:]:
                n *= s
            assert base + off + n <= end, (name, base + off + n - end)
            made[name] = (off, off + n)
            return nc.alloc_sbuf_tensor_at(name, shape, dt, offset=base + off)

        K = 1024
        o = 0

        def seq(name, shape, dt=f32):
            nonlocal o
            t = at(name, shape, o, dt)
            o = (made[name][1] + 31) // 32 * 32
            return t

        w_raw = [seq(f"w_raw{i}", [P, KC, P]) for i in range(RAW)]
        w_hi = [seq(f"w_hi{i}", [P, KC, P], f32r) for i in range(SPL)]
        w_lo = [seq(f"w_lo{i}", [P, KC, P], f32r) for i in range(SPL)]
        x = seq("x", [P, ND, TL])
        vec = seq("vec", [P, NVEC])
        ones = seq("ones", [P, P])
        ident = seq("ident", [P, P])
        ssd_mask = seq("ssd_mask", [P, P])
        mods = seq("mods", [P, 2, 48])
        gains = seq("gains", [P, 2, 4, ND])
        epsv = seq("epsv", [P, 4])
        small = seq("small", [P, 64])
        rstd = seq("rstd", [P, TL])
        o_xc = o
        xc = seq("xc", [P, ND, TC])
        A0 = o
        ps = [ctx.enter_context(nc.psum_tensor(f"ps{i}", [P, 512], f32)) for i in range(8)]

        def V(name, i=0, n=1):
            a, w = VEC[name]
            return vec[:, a + i:a + i + n]

        def C(name):
            a, w = CST[name]
            return cst[:, a:a + w]

        def arena(name, shape, off, dt=f32):
            return at(name, shape, A0 + off, dt)

        h_hi = arena("h_hi", [P, ND, TL], 0, f32r)
        h_lo = arena("h_lo", [P, ND, TL], 16 * K, f32r)
        y = arena("y", [P, ND, TL], 0)
        hid_hi = arena("hid_hi", [P, NH, TL], 32 * K, f32r)
        hid_lo = arena("hid_lo", [P, NH, TL], 76 * K, f32r)
        wk = [arena(f"wk{i}", [P, TL], 120 * K + 2 * K * i) for i in range(4)]
        pad = [at(f"pad{i}", [P, TL + 4], o_xc + 2080 * i) for i in range(2)]
        c_hi = arena("c_hi", [P, ND, TC], 32 * K, f32r)
        c_lo = arena("c_lo", [P, ND, TC], 40 * K, f32r)

        cnt = Counts(lambda n: ctx.enter_context(nc.semaphore(n)))
        raw_ready = [cnt.take(f"raw_ready{i}", 0)[0] for i in range(RAW)]
        split_done = cnt.take("split_done", 0)[0]
        hi_done = cnt.take("hi_done", 0)[0]
        chunk_done = cnt.take("chunk_done", 0)[0]
        mm_free = cnt.take("mm_free", 0)[0]
        const_in = cnt.take("const_in", 0)[0]
        phase_in = cnt.take("phase_in", 0)[0]
        waited = cnt.take("waited", 0)[0]
        act_step = cnt.take("act_step", 0)[0]
        dve_step = cnt.take("dve_step", 0)[0]
        steps = {"act": 0, "dve": 0}

        def astep(ins):
            steps["act"] += 1
            ins.then_inc(act_step, 1)
            nc.scalar.wait_ge(act_step, steps["act"])

        def vstep(ins):
            steps["dve"] += 1
            ins.then_inc(dve_step, 1)
            nc.vector.wait_ge(dve_step, steps["dve"])

        sent = {}

        def sig(eng, ins, taken, n=1):
            sent[taken] = sent.get(taken, 0) + n
            ins.then_inc(taken[0], n)
            eng.wait_ge(*upto(taken, sent[taken]))

        progress = {"chunk": 0, "tile": 0, "phase_in": 0}
        phases = []

        class Phase:
            def __init__(self):
                phases.append(self)

            def sp(self, sp): pass
            def pool(self, pool): pass
            def act(self, act): pass
            def dve(self, dve): pass
            def pe(self, pe): pass

        def loaded(n_dmas):
            progress["phase_in"] += n_dmas
            return 16 * progress["phase_in"]

        class Gemm(Phase):

            def __init__(self, w, tiles, parts, kt, rhs, t=TL, ctx_rhs=None, ctx_from=0, evac_act=None, evac_dve=None,
                         peel=(), signal=None, gate=None):
                super().__init__()
                self.w, self.tiles, self.parts, self.kt, self.rhs, self.t = w, tiles, parts, kt, rhs, t
                self.ctx_rhs, self.ctx_from = ctx_rhs, ctx_from
                self.evac_act, self.evac_dve, self.gate = evac_act, evac_dve, gate
                self.chunk0, self.tile0 = progress["chunk"], progress["tile"]
                progress["chunk"] += tiles * parts
                progress["tile"] += tiles
                self.per = RAW // parts
                self.turns = tiles // self.per
                self.peel = peel
                assert (tiles * parts) % RAW == 0 and self.tile0 % NBANK in (0, 2)

            def loops(self, eng, body):
                bounds = [0, *self.peel, self.turns]
                for a, b in zip(bounds, bounds[1:]):
                    if b - a == 1:
                        body(a, a)
                    else:
                        with eng.Fori(a, b) as i:
                            body(i, a)

            def sp(self, sp):
                def turn(i, a):
                    for j in range(RAW):
                        sp.wait_ge(split_done, self.chunk0 + RAW * i + j + 1)
                        src = self.w[bass.ds(RAW * i + j, 1)].rearrange("o p k f -> (o p) k f")
                        sp.dma_start(w_raw[j][:, 0:self.kt], src).then_inc(raw_ready[j], 16)
                self.loops(sp, turn)

            def pool(self, pool):
                def turn(i, a):
                    for j in range(RAW):
                        s = j % SPL
                        c = self.chunk0 // RAW
                        pool.wait_ge(raw_ready[j], 16 * (c + i + 1))
                        pool.wait_ge(chunk_done, self.chunk0 + RAW * i + j + 1)
                        pool.sem_inc(waited, 1)
                        nc.gpsimd.tensor_scalar(w_hi[s][:, 0:self.kt], w_raw[j][:, 0:self.kt], 1.0, 1.0, ALU.mult, ALU.mult).then_inc(hi_done, 1)
                        pool.wait_ge(hi_done, self.chunk0 + RAW * i + j + 1)
                        nc.gpsimd.tensor_tensor(w_lo[s][:, 0:self.kt], w_raw[j][:, 0:self.kt],
                                                w_hi[s][:, 0:self.kt].bitcast(f32), ALU.subtract).then_inc(split_done, 1)
                self.loops(pool, turn)

            def pe(self, pe):
                pe.wait_ge(mm_free, self.tile0 + NBANK)
                if self.gate:
                    pe.wait_ge(*self.gate)

                def turn(i, a):
                    for n in range(self.per):
                        bank = self.bank(n)
                        pe.wait_ge(mm_free, self.tile0 + self.per * i + n + 1 + NBANK - self.per)
                        both = self.ctx_rhs is not None and self.per * a + n >= self.ctx_from
                        for part in range(self.parts):
                            j = n * self.parts + part
                            s = j % SPL
                            pe.wait_ge(split_done, RAW + self.chunk0 + RAW * i + j + 1)
                            for rhs, dst in ((self.rhs, ps[bank][:, 0:self.t]),) + (
                                    ((self.ctx_rhs, self.ctx_out(n)),) if both else ()):
                                for k in range(self.kt):
                                    kk = part * self.kt + k
                                    hi, lo = rhs(kk)
                                    nc.tensor.matmul(dst, w_hi[s][:, k], hi, start=kk == 0, stop=False)
                                    nc.tensor.matmul(dst, w_hi[s][:, k], lo, start=False, stop=False)
                                    last = nc.tensor.matmul(dst, w_lo[s][:, k], hi, start=False,
                                                            stop=kk == self.parts * self.kt - 1)
                            last.then_inc(chunk_done, 1)
                self.loops(pe, turn)

            def act(self, act):
                if self.evac_act:
                    self.loops(act, lambda i, a: self.evac_act(self, act, i, a))

            def dve(self, dve):
                if self.evac_dve:
                    self.loops(dve, lambda i, a: self.evac_dve(self, dve, i, a))

            def tile(self, i, n):
                return SPL + self.chunk0 + RAW * i + (n + 1) * self.parts

            def bank(self, n):
                return n % NBANK if self.per == NBANK else n % 2

            def out(self, n):
                return ps[self.bank(n)][:, 0:self.t]

            def ctx_out(self, n):
                return ps[4 + n][:, 0:TC]

            @property
            def all_read(self):
                return (mm_free, NBANK + self.tile0 + self.tiles)

        class Rms(Phase):

            def __init__(self, src, nt, t, count, eps, gate, dst=None, bufs=None):
                super().__init__()
                self.src, self.nt, self.t, self.count, self.eps, self.gate = src, nt, t, count, eps, gate
                self.dst = rstd if dst is None else dst
                self.bufs = wk[2:4] if bufs is None else bufs
                self.sq_ready, self.sq_summed = cnt.take("sq_ready", nt), cnt.take("sq_summed", nt)
                self.rstd_ready = cnt.take("rstd_ready", 1)
                self.done = (self.rstd_ready[0], self.rstd_ready[1] + 1)

            def act(self, act):
                s, b = self.sq_summed
                for k in range(self.nt):
                    act.wait_ge(*self.gate(k))
                    if k >= 2:
                        act.wait_ge(s, b + k - 1)
                    sig(nc.scalar, nc.scalar.activation(self.bufs[k % 2][:, 0:self.t], self.src(k), ACT.Square), self.sq_ready)
                act.wait_ge(s, b + self.nt)
                astep(nc.scalar.activation(self.dst[:, 0:self.t], ps[6][:, 0:self.t], ACT.Ln, scale=1.0 / self.count,
                                           bias=epsv[:, self.eps:self.eps + 1]))
                sig(nc.scalar, nc.scalar.activation(self.dst[:, 0:self.t], self.dst[:, 0:self.t], ACT.Exp, scale=-0.5), self.rstd_ready)

            def pe(self, pe):
                for k in range(self.nt):
                    pe.wait_ge(self.sq_ready[0], self.sq_ready[1] + k + 1)
                    nc.tensor.matmul(ps[6][:, 0:self.t], ones[:], self.bufs[k % 2][:, 0:self.t], start=k == 0,
                                     stop=k == self.nt - 1).then_inc(self.sq_summed[0], 1)

        class Apply(Phase):

            def __init__(self, src, nt, t, gain, shift, hi, lo, rms, gate=None):
                super().__init__()
                self.src, self.nt, self.t, self.gain, self.shift, self.hi, self.lo = src, nt, t, gain, shift, hi, lo
                self.rms, self.gate = rms, gate
                self.scaled, self.hi_ready, self.lo_ready = cnt.take("scaled", nt), cnt.take("h_hi_ready", nt), cnt.take("h_lo_ready", nt)
                self.done = (self.lo_ready[0], self.lo_ready[1] + nt)

            def dve(self, dve):
                dve.wait_ge(*self.rms.done)
                if self.gate:
                    dve.wait_ge(*self.gate)
                for k in range(self.nt + 1):
                    if k < self.nt:
                        sig(nc.vector, nc.vector.scalar_tensor_tensor(wk[k % 2][:, 0:self.t], self.src(k), self.gain(k), rstd[:, 0:self.t],
                                                       ALU.mult, ALU.mult), self.scaled)
                    if k >= 1:
                        q = k - 1
                        dve.wait_ge(self.hi_ready[0], self.hi_ready[1] + q + 1)
                        src, hi = wk[q % 2][:, 0:self.t], self.hi(q).bitcast(f32)
                        if self.shift:
                            ins = nc.vector.scalar_tensor_tensor(self.lo(q), src, self.shift(q), hi, ALU.add, ALU.subtract)
                        else:
                            ins = nc.vector.tensor_tensor(self.lo(q), src, hi, ALU.subtract)
                        sig(nc.vector, ins, self.lo_ready)

            def act(self, act):
                for k in range(self.nt):
                    act.wait_ge(self.scaled[0], self.scaled[1] + k + 1)
                    bias = self.shift(k) if self.shift else 0.0
                    sig(nc.scalar, nc.scalar.activation(self.hi(k), wk[k % 2][:, 0:self.t], ACT.Identity, bias=bias), self.hi_ready)

        class Residual(Phase):

            def __init__(self, xt, yt, nt, t, gain, rms, gate=None):
                super().__init__()
                self.x, self.y, self.nt, self.t, self.gain, self.rms, self.gate = xt, yt, nt, t, gain, rms, gate
                self.scaled, self.added = cnt.take("y_scaled", nt), cnt.take("x_added", nt)

            def ready(self, k):
                return (self.added[0], self.added[1] + k + 1)

            def dve(self, dve):
                dve.wait_ge(*(self.rms.done if self.rms else self.gate))
                if not self.rms:
                    for k in range(self.nt):
                        sig(nc.vector, nc.vector.tensor_tensor(self.x(k), self.x(k), self.y(k), ALU.add), self.added)
                    return
                for k in range(self.nt + 1):
                    if k < self.nt:
                        sig(nc.vector, nc.vector.scalar_tensor_tensor(wk[k % 2][:, 0:self.t], self.y(k), self.gain(k), rstd[:, 0:self.t],
                                                       ALU.mult, ALU.mult), self.scaled)
                    if k >= 1:
                        dve.wait_ge(self.scaled[0], self.scaled[1] + k)
                        sig(nc.vector, nc.vector.tensor_tensor(self.x(k - 1), self.x(k - 1), wk[(k - 1) % 2][:, 0:self.t],
                                                ALU.add), self.added)

        a_raw = [arena(f"a_raw{i}", [P, D], 4 * K * i) for i in range(2)]
        a_c = arena("a_c", [P, 2, D], 8 * K)
        a_junk = [arena(f"a_junk{i}", [P, D], (16 + 4 * i) * K) for i in range(2)]

        class Ada(Phase):

            def __init__(self, w, layer, gate):
                super().__init__()
                self.w, self.layer, self.gate = w, layer, gate
                self.arrived = [cnt.take(f"ada_in{i}", 0)[0] for i in range(2)]
                self.base = 24 * layer
                self.c_in = cnt.take("c_in", 1)
                self.c_ready = cnt.take("c_ready", 1)
                self.used = cnt.take("ada_used", 0)[0]
                self.done_c = cnt.take("mods_ready", 1)
                self.done = (self.done_c[0], self.done_c[1] + 1)

            def sp(self, sp):
                if self.gate:
                    sp.wait_ge(*self.gate)
                for v in range(2):
                    sp.dma_start(a_c[:, v], cvec[v:v + 1, :].to_broadcast([P, D])).then_inc(self.c_in[0], 16)
                with sp.Fori(0, 24) as i:
                    for j in range(2):
                        sp.wait_ge(self.used, 4 * (self.base + i) + 2 * j + 2)
                        sp.dma_start(a_raw[j][:], self.w[bass.ds(2 * i + j, 1)].rearrange("o p k -> (o p) k")).then_inc(self.arrived[j], 16)

            def act(self, act):
                act.wait_ge(self.c_in[0], 32 * (self.layer + 1))
                nc.scalar.activation(a_c[:, :], a_c[:, :], ACT.Silu).then_inc(self.c_ready[0], 1)

            def dve(self, dve):
                dve.wait_ge(self.c_ready[0], self.c_ready[1] + 1)
                if self.layer == 0:
                    dve.sem_inc(self.used, 4)
                with dve.Fori(0, 24) as i:
                    for j in range(2):
                        dve.wait_ge(self.arrived[j], 16 * (self.base + i + 1))
                        for v in range(2):
                            dve.wait_ge(self.used, 4 + 4 * (self.base + i) + 2 * j + v - 1)
                            nc.vector.scalar_tensor_tensor(a_junk[v][:], a_raw[j][:], 1.0, a_c[:, v], ALU.mult, ALU.mult,
                                                           accum_out=mods[:, v, bass.ds(2 * i + j, 1)]).then_inc(self.used, 1)
                dve.wait_ge(self.used, 4 + 4 * (self.base + 24))
                l = self.layer
                for v in range(2):
                    last = nc.vector.tensor_tensor(mods[:, v], mods[:, v], V("ada_b", 48 * l, 48), ALU.add)
                vstep(last)
                for v in range(2):
                    for q, (g, m) in enumerate(((0, 8), (1, 16), (2, 32), (3, 40))):
                        ng = V("norm_g", 32 * l + 8 * g, 8)
                        if q % 2 == 0:
                            last = nc.vector.scalar_tensor_tensor(gains[:, v, q], mods[:, v, m:m + 8], 1.0, ng, ALU.add, ALU.mult)
                        else:
                            last = nc.vector.tensor_tensor(gains[:, v, q], mods[:, v, m:m + 8], ng, ALU.mult)
                last.then_inc(self.done_c[0], 1)

        z = arena("z", [P, 24, TA], 48 * K)
        LAT, CTX = slice(TC, TA), slice(0, TC)

        def z_evac_act(g, act, i, a):
            funcs = {0: [ACT.Copy] * 4, 1: [ACT.Silu] * 4}.get(a, [ACT.Silu, ACT.Sigmoid, ACT.Sigmoid, ACT.Copy])
            for n in range(4):
                act.wait_ge(chunk_done, g.tile(i, n))
                dst = z[:, bass.ds(4 * i + n, 1)].rearrange("p o t -> p (o t)")
                nc.scalar.activation(dst[:, LAT], g.out(n), funcs[n])
                nc.scalar.activation(dst[:, CTX], g.ctx_out(n), funcs[n]).then_inc(mm_free, 1)

        m_lev = [arena(f"m_lev{i}", [P, TA], 3 * K * i) for i in range(7)]
        hk, hb, hdq, hdk = (arena(n, [P, TA], (21 + 3 * i) * K) for i, n in enumerate(("hk", "hb", "hdq", "hdk")))
        v_tok = arena("v_tok", [P, NCH, P], 33 * K)
        k_tok = arena("k_tok", [P, NCH, P], 36 * K)
        he = [arena(f"he{i}", [P, TA], (39 + 3 * i) * K) for i in range(2)]
        ho = arena("ho", [P, TA], 45 * K)
        hmask = arena("hmask", [P, 2, 6, P], 120 * K)
        a_tmp = arena("a_tmp", [P, 6, P], 126 * K)
        a_sum = [arena(f"a_sum{i}", [P, P], 129 * K + 512 * i) for i in range(2)]
        h_st = [arena(f"h_st{i}", [P, P], 130 * K + 512 * i) for i in range(2)]
        h_el = small[:, 0:NCH]
        lbv, omlv = small[:, 8:16], small[:, 16:24]
        mix_hi = [arena(f"mix_hi{k}", [P, TA], (48 + 3 * (k if k < 4 else 8 + 4 * (k - 4))) * K, f32r) for k in range(8)]
        mix_lo = [arena(f"mix_lo{k}", [P, TA], (48 + 3 * (4 + k if k < 4 else 9 + 4 * (k - 4))) * K, f32r) for k in range(8)]

        class HgPrep(Phase):

            def __init__(self, gate):
                super().__init__()
                self.gate, self.val = gate, loaded(1)
                self.diff, self.lb = cnt.take("lb_diff", 1), cnt.take("lb_ready", 1)

            def sp(self, sp):
                sp.wait_ge(*self.gate)
                a, w = CST["hg_mask"]
                sp.dma_start(hmask[:, :, :, :].rearrange("p d l t -> p (d l t)"), cst[:, a:a + w]).then_inc(phase_in, 16)

            def dve(self, dve):
                sig(nc.vector, nc.vector.tensor_tensor(small[:, 24:32], V("hg_lower", 0, 8), V("hg_lower", 8, 8), ALU.subtract), self.diff)
                dve.wait_ge(self.lb[0], self.lb[1] + 1)
                vstep(nc.vector.tensor_scalar(omlv, lbv, -1.0, 1.0, ALU.mult, ALU.add))

            def act(self, act):
                act.wait_ge(self.diff[0], self.diff[1] + 1)
                sig(nc.scalar, nc.scalar.activation(lbv, small[:, 24:32], ACT.Sigmoid), self.lb)

        class HgUnit(Phase):

            def __init__(self, head, back, masks, gate):
                super().__init__()
                self.head, self.back, self.masks, self.gate = head, back, masks, gate
                self.order = [1, 0, 5, 4, 3, 2] if back else list(range(NCH))
                self.f_ready, self.lf_ready, self.k_ready = cnt.take("f_ready", 1), cnt.take("lf_ready", 1), cnt.take("k_ready", 1)
                self.b_ready, self.arg_ready, self.exp_ready = cnt.take("b_ready", 1), cnt.take("arg_ready", 7), cnt.take("exp_ready", 7)
                self.level_ready, self.dq_exp, self.dk_arg = cnt.take("level_ready", 7), cnt.take("dq_exp", 1), cnt.take("dk_arg", 1)
                self.dk_exp, self.dq_ready, self.dk_ready = cnt.take("dk_exp", 1), cnt.take("dq_ready", 1), cnt.take("dk_ready", 1)
                self.tok_in_ps, self.tok_read, self.scores_in_ps = cnt.take("tok_in_ps", 4), cnt.take("tok_read", 4), cnt.take("scores_in_ps", 6)
                self.masked, self.o_in_ps, self.state_ready = cnt.take("masked", 6), cnt.take("o_in_ps", 6), cnt.take("state_ready", 7)

            def dve(self, dve):
                h, back = self.head, self.back
                s = z[:, 9 + 4 * h + back]
                d = 4 * back + h
                q = z[:, 8 + 4 * h]
                if self.gate:
                    dve.wait_ge(*self.gate)
                if h == 0 and not back:
                    dve.wait_ge(phase_in, self.masks)
                sig(nc.vector, nc.vector.tensor_scalar(s, s, omlv[:, d:d + 1], lbv[:, d:d + 1], ALU.mult, ALU.add), self.f_ready)
                dve.wait_ge(*upto(self.f_ready, 1))
                sig(nc.vector, nc.vector.tensor_scalar(hk[:], s, -1.0, 1.0, ALU.mult, ALU.add), self.k_ready)
                dve.wait_ge(*upto(self.lf_ready, 1))
                lf = s.rearrange("p (c t) -> p c t", c=NCH)
                b = hb[:, :].rearrange("p (c t) -> p c t", c=NCH)
                for c in range(NCH):
                    src, dst = (lf[:, c, ::-1], b[:, c, ::-1]) if back else (lf[:, c], b[:, c])
                    last = nc.vector.tensor_tensor_scan(dst, ones[:], src, 0.0, ALU.mult, ALU.add)
                sig(nc.vector, last, self.b_ready)
                dve.wait_ge(*upto(self.b_ready, 1))
                end = b[:, :, 0:1] if back else b[:, :, CH - 1:CH]
                sig(nc.vector, nc.vector.tensor_tensor(hdk[:, :].rearrange("p (c t) -> p c t", c=NCH), end.to_broadcast([P, NCH, CH]), b,
                                        ALU.subtract), self.dk_arg)
                qs, ks = (0, 1) if back else (1, 0)
                for l in range(8):
                    if l < 7:
                        half = LEVELS[l]
                        v, w = (a.rearrange("p (n s t) -> p n s t", s=2, t=half) for a in (hb[:, :], he[l % 2][:, :]))
                        n = TA // (2 * half)
                        ref = (v[:, :, 1, 0:1] if back else v[:, :, 0, half - 1:half]).to_broadcast([P, n, half])
                        if l >= 2:
                            dve.wait_ge(*upto(self.level_ready, l - 1))
                        vstep(nc.vector.tensor_tensor(w[:, :, qs], v[:, :, qs], ref, ALU.subtract))
                        sig(nc.vector, nc.vector.tensor_tensor(w[:, :, ks], ref, v[:, :, ks], ALU.subtract), self.arg_ready)
                    if l >= 1:
                        m, half = l - 1, LEVELS[l - 1]
                        e, w, qq, kk = (a.rearrange("p (n s t) -> p n s t", s=2, t=half) for a in (he[m % 2][:, :], m_lev[m][:, :], q, hk[:, :]))
                        dve.wait_ge(*upto(self.exp_ready, m + 1))
                        vstep(nc.vector.tensor_tensor(w[:, :, qs], e[:, :, qs], qq[:, :, qs], ALU.mult))
                        sig(nc.vector, nc.vector.tensor_tensor(w[:, :, ks], e[:, :, ks], kk[:, :, ks], ALU.mult), self.level_ready)
                dve.wait_ge(*upto(self.dq_exp, 1))
                sig(nc.vector, nc.vector.tensor_tensor(hdq[:], hdq[:], q, ALU.mult), self.dq_ready)
                dve.wait_ge(*upto(self.dk_exp, 1))
                sig(nc.vector, nc.vector.tensor_tensor(hdk[:], hdk[:], hk[:], ALU.mult), self.dk_ready)
                sig(nc.vector, nc.vector.memset(h_st[0][:], 0.0), self.state_ready)
                for i, c in enumerate(self.order):
                    bx, by, bo = ps[2 * (i % 2)], ps[2 * (i % 2) + 1], ps[4 + i % 2]
                    dve.wait_ge(*upto(self.scores_in_ps, i + 1))
                    vstep(nc.vector.tensor_tensor(a_tmp[:, 0:4], bx[:, :].rearrange("p (l t) -> p l t", l=4), hmask[:, back, 0:4], ALU.mult))
                    vstep(nc.vector.tensor_tensor(a_tmp[:, 4:6], by[:, 0:256].rearrange("p (l t) -> p l t", l=2), hmask[:, back, 4:6], ALU.mult))
                    sig(nc.vector, nc.vector.tensor_reduce(a_sum[i % 2][:], a_tmp[:, :, :].rearrange("p l t -> p t l"), AX.X, ALU.add), self.masked)
                    dve.wait_ge(*upto(self.o_in_ps, i + 1))
                    dst = ho[:, c * CH:(c + 1) * CH]
                    if back:
                        vstep(nc.vector.tensor_tensor(dst, dst, bo[:, 0:P], ALU.add))
                    else:
                        vstep(nc.vector.tensor_copy(dst, bo[:, 0:P]))
                    dve.wait_ge(*upto(self.state_ready, i + 1))
                    sig(nc.vector, nc.vector.scalar_tensor_tensor(h_st[(i + 1) % 2][:], h_st[i % 2][:], h_el[:, c:c + 1], bo[:, P:2 * P],
                                                   ALU.mult, ALU.add), self.state_ready)

            def act(self, act):
                h, back = self.head, self.back
                s = z[:, 9 + 4 * h + back]
                act.wait_ge(*upto(self.k_ready, 1))
                sig(nc.scalar, nc.scalar.activation(s, s, ACT.Ln), self.lf_ready)
                act.wait_ge(*upto(self.b_ready, 1))
                b = hb[:, :].rearrange("p (c t) -> p c t", c=NCH)
                end = b[:, :, 0] if back else b[:, :, CH - 1]
                astep(nc.scalar.activation(h_el, end, ACT.Exp))
                sig(nc.scalar, nc.scalar.activation(hdq[:], hb[:], ACT.Exp), self.dq_exp)
                act.wait_ge(*upto(self.dk_arg, 1))
                sig(nc.scalar, nc.scalar.activation(hdk[:], hdk[:], ACT.Exp), self.dk_exp)
                for l in range(7):
                    act.wait_ge(*upto(self.arg_ready, l + 1))
                    sig(nc.scalar, nc.scalar.activation(he[l % 2][:], he[l % 2][:], ACT.Exp), self.exp_ready)
                for i, (dst, srcs) in enumerate(((v_tok, (0, 4)), (v_tok, (4, 6)), (k_tok, (0, 4)), (k_tok, (4, 6)))):
                    act.wait_ge(*upto(self.tok_in_ps, i + 1))
                    a, e = srcs
                    sig(nc.scalar, nc.scalar.copy(dst[:, a:e], ps[4 + i][:, 0:(e - a) * P].rearrange("p (c t) -> p c t", c=e - a)), self.tok_read)

            def pe(self, pe):
                h, back = self.head, self.back
                q, v = z[:, 8 + 4 * h], z[:, 11 + 4 * h]
                pe.wait_ge(*upto(self.dq_ready, 1))
                for i, (src, (a, e)) in enumerate(((v, (0, 4)), (v, (4, 6)), (hdk, (0, 4)), (hdk, (4, 6)))):
                    if i == 2:
                        pe.wait_ge(*upto(self.dk_ready, 1))
                    for c in range(a, e):
                        last = nc.tensor.transpose(ps[4 + i][:, (c - a) * P:(c - a + 1) * P], src[:, c * CH:(c + 1) * CH], ident[:])
                    last.then_inc(self.tok_in_ps[0], 1)
                qo, ko = (0, 1) if back else (1, 0)
                for i, c in enumerate(self.order):
                    bx, by, bo = ps[2 * (i % 2)], ps[2 * (i % 2) + 1], ps[4 + i % 2]
                    t0 = c * CH
                    if i >= 2:
                        pe.wait_ge(*upto(self.state_ready, i))
                    nc.tensor.matmul(bx[:, 0:P], hk[:, t0:t0 + CH], q[:, t0:t0 + CH], start=True, stop=True)
                    for l in range(2):
                        half = LEVELS[l]
                        for n in range(CH // (2 * half)):
                            ss, tt = 2 * half * n + half * ko, 2 * half * n + half * qo
                            nc.tensor.matmul(bx[ss:ss + half, tt:tt + half], m_lev[l][:, t0 + ss:t0 + ss + half],
                                             m_lev[l][:, t0 + tt:t0 + tt + half], start=True, stop=True)
                    for l in range(2, 7):
                        dst = bx[:, (l - 1) * P:l * P] if l < 5 else by[:, (l - 5) * P:(l - 4) * P]
                        m = m_lev[l][:, t0:t0 + CH]
                        last = nc.tensor.matmul(dst, m, m, start=True, stop=True)
                    last.then_inc(self.scores_in_ps[0], 1)
                    if i == 0:
                        pe.wait_ge(*upto(self.tok_read, 4))
                    nc.tensor.matmul(bo[:, P:2 * P], k_tok[:, c], v_tok[:, c], start=True, stop=True)
                    pe.wait_ge(*upto(self.state_ready, i + 1))
                    nc.tensor.matmul(bo[:, 0:P], h_st[i % 2][:], hdq[:, t0:t0 + CH], start=True, stop=False)
                    pe.wait_ge(*upto(self.masked, i + 1))
                    nc.tensor.matmul(bo[:, 0:P], v_tok[:, c], a_sum[i % 2][:], start=False, stop=True).then_inc(self.o_in_ps[0], 1)

        class HgOut(Phase):

            def __init__(self, head, unit):
                super().__init__()
                self.head, self.unit = head, unit
                self.hg_sq, self.hg_sum, self.hg_rstd = cnt.take("hg_sq", 1), cnt.take("hg_sum", 1), cnt.take("hg_rstd", 1)
                self.hg_t, self.mix_hi, self.mix_lo = cnt.take("hg_t", 2), cnt.take("mix_hi", 1), cnt.take("mix_lo", 1)

            def act(self, act):
                act.wait_ge(*upto(self.unit.state_ready, 7))
                sig(nc.scalar, nc.scalar.activation(he[0][:], ho[:], ACT.Square), self.hg_sq)
                act.wait_ge(*upto(self.hg_sum, 1))
                astep(nc.scalar.activation(he[1][:, 0:512], ps[6][:, 0:512], ACT.Ln, scale=1.0 / P, bias=epsv[:, 0:1]))
                astep(nc.scalar.activation(he[1][:, 512:TA], ps[7][:, 0:256], ACT.Ln, scale=1.0 / P, bias=epsv[:, 0:1]))
                sig(nc.scalar, nc.scalar.activation(he[1][:], he[1][:], ACT.Exp, scale=-0.5), self.hg_rstd)
                act.wait_ge(*upto(self.hg_t, 2))
                sig(nc.scalar, nc.scalar.copy(mix_hi[4 + self.head][:], ho[:]), self.mix_hi)

            def pe(self, pe):
                pe.wait_ge(*upto(self.hg_sq, 1))
                nc.tensor.matmul(ps[6][:, 0:512], ones[:], he[0][:, 0:512], start=True, stop=True)
                nc.tensor.matmul(ps[7][:, 0:256], ones[:], he[0][:, 512:TA], start=True, stop=True).then_inc(self.hg_sum[0], 1)

            def dve(self, dve):
                dve.wait_ge(*upto(self.hg_rstd, 1))
                sig(nc.vector, nc.vector.scalar_tensor_tensor(ho[:], ho[:], V("onorm"), he[1][:], ALU.mult, ALU.mult), self.hg_t)
                dve.wait_ge(*upto(self.hg_t, 1))
                sig(nc.vector, nc.vector.tensor_tensor(ho[:], ho[:], z[:, 4 + self.head], ALU.mult), self.hg_t)
                dve.wait_ge(*upto(self.mix_hi, 1))
                sig(nc.vector, nc.vector.tensor_tensor(mix_lo[4 + self.head][:], ho[:], mix_hi[4 + self.head][:].bitcast(f32),
                                        ALU.subtract), self.mix_lo)

        PW = 8 + TC + 8 + TL + 8
        p_buf = [arena(f"p_buf{i}", [P, PW], 3200 * i) for i in range(3)]
        p_y = arena("p_y", [P, TA], 9600)
        p_inv = arena("p_inv", [P, 4, TA], 13 * K)
        p_w = arena("p_w", [P, 4, P], 25 * K)

        class Pool(Phase):
            def __init__(self, gate):
                super().__init__()
                self.gate, self.val = gate, loaded(2)
                self.pool_y, self.pool_ps, self.pool_hi = cnt.take("pool_y", 4), cnt.take("pool_ps", 4), cnt.take("pool_hi", 4)
                self.pool_lo = cnt.take("pool_lo", 4)

            def sp(self, sp):
                sp.wait_ge(*self.gate)
                a, w = CST["pool_inv"]
                sp.dma_start(p_inv[:, :, :].rearrange("p g t -> p (g t)"), cst[:, a:a + w]).then_inc(phase_in, 16)
                sp.dma_start(p_w[:, :, :], w_pool).then_inc(phase_in, 16)

            def dve(self, dve):
                dve.wait_ge(*self.gate)
                for i in range(3):
                    last = nc.vector.memset(p_buf[i][:], 0.0)
                vstep(last)
                for g in range(4):
                    u = z[:, g]
                    vstep(nc.vector.tensor_copy(p_buf[2][:, 8:8 + TC], u[:, CTX]))
                    vstep(nc.vector.tensor_copy(p_buf[2][:, 16 + TC:16 + TC + TL], u[:, LAT]))
                    src = 2
                    for j in range(g + 1):
                        step, dst = 1 << j, j % 2
                        n = PW - 2 * step + 1
                        vstep(nc.vector.tensor_tensor(p_buf[dst][:, 0:n], p_buf[src][:, 0:n], p_buf[src][:, step:step + n], ALU.add))
                        src = dst
                    half = 1 << g
                    if g == 0:
                        dve.wait_ge(phase_in, self.val)
                    else:
                        dve.wait_ge(*upto(self.pool_ps, g))
                    s = p_buf[src]
                    vstep(nc.vector.tensor_tensor(p_y[:, CTX], s[:, 8 - half:8 - half + TC], p_inv[:, g, CTX], ALU.mult))
                    vstep(nc.vector.tensor_tensor(p_y[:, LAT], s[:, 16 + TC - half:16 + TC - half + TL], p_inv[:, g, LAT], ALU.mult))
                    sig(nc.vector, nc.vector.tensor_tensor(p_y[:], p_y[:], u, ALU.subtract), self.pool_y)
                    dve.wait_ge(*upto(self.pool_hi, g + 1))
                    for a, e, b in ((0, 512, 0), (512, TA, 1)):
                        last = nc.vector.scalar_tensor_tensor(mix_lo[g][:, a:e], ps[2 * (g % 2) + b][:, 0:e - a], V("pool_scale", g),
                                                              mix_hi[g][:, a:e].bitcast(f32), ALU.mult, ALU.subtract)
                    sig(nc.vector, last, self.pool_lo)

            def pe(self, pe):
                for g in range(4):
                    pe.wait_ge(*upto(self.pool_y, g + 1))
                    if g >= 2:
                        pe.wait_ge(*upto(self.pool_lo, g - 1))
                    nc.tensor.matmul(ps[2 * (g % 2)][:, 0:512], p_w[:, g], p_y[:, 0:512], start=True, stop=True)
                    nc.tensor.matmul(ps[2 * (g % 2) + 1][:, 0:256], p_w[:, g], p_y[:, 512:TA], start=True, stop=True).then_inc(self.pool_ps[0], 1)

            def act(self, act):
                for g in range(4):
                    act.wait_ge(*upto(self.pool_ps, g + 1))
                    astep(nc.scalar.activation(mix_hi[g][:, 0:512], ps[2 * (g % 2)][:, 0:512], ACT.Copy, scale=V("pool_scale", g)))
                    sig(nc.scalar, nc.scalar.activation(mix_hi[g][:, 512:TA], ps[2 * (g % 2) + 1][:, 0:256], ACT.Copy,
                                         scale=V("pool_scale", g)), self.pool_hi)

        yc = arena("yc", [P, ND, TC], 32 * K)
        yc2 = arena("yc2", [P, ND, TC], 0)

        def y_evac(dst, cdst=None):
            def act(g, act, i, a):
                for n in range(g.per):
                    act.wait_ge(chunk_done, g.tile(i, n))
                    ins = nc.scalar.copy(dst[:, bass.ds(g.per * i + n, 1)].rearrange("p o t -> p (o t)"), g.out(n))
                    if cdst is not None:
                        ins = nc.scalar.copy(cdst[:, bass.ds(g.per * i + n, 1)].rearrange("p o t -> p (o t)"), g.ctx_out(n))
                    ins.then_inc(mm_free, 1)
            return act

        class Swiglu:

            def __init__(self, t):
                self.t = t
                self.silu, self.hi, self.lo = cnt.take("silu_ready", NH), cnt.take("hid_hi_ready", NH), cnt.take("hid_lo_ready", NH)
                self.done = upto(self.lo, NH, 2)

            def hid(self, buf, i, q):
                return buf[:, bass.ds(2 * i + q, 1), 0:self.t].rearrange("p o t -> p (o t)")

            def act(self, g, act, i, a):
                for q in range(2):
                    act.wait_ge(chunk_done, g.tile(i, 2 * q))
                    act.wait_ge(self.lo[0], 2 + self.lo[1] + 2 * i + q - 1)
                    nc.scalar.activation(wk[q][:, 0:self.t], g.out(2 * q), ACT.Silu).then_inc(self.silu[0], 1)
                    act.wait_ge(mm_free, NBANK + g.tile0 + 4 * i + 2 * q + 2)
                    nc.scalar.copy(self.hid(hid_hi, i, q), wk[2 + q][:, 0:self.t]).then_inc(self.hi[0], 1)

            def dve(self, g, dve, i, a):
                for q in range(2):
                    dve.wait_ge(chunk_done, g.tile(i, 2 * q + 1))
                    dve.wait_ge(self.silu[0], self.silu[1] + 2 * i + q + 1)
                    nc.vector.tensor_tensor(wk[2 + q][:, 0:self.t], wk[q][:, 0:self.t], g.out(2 * q + 1), ALU.mult).then_inc(mm_free, 2)
                    dve.wait_ge(self.hi[0], self.hi[1] + 2 * i + q + 1)
                    nc.vector.tensor_tensor(self.hid(hid_lo, i, q), wk[2 + q][:, 0:self.t],
                                            self.hid(hid_hi, i, q).bitcast(f32), ALU.subtract).then_inc(self.lo[0], 1)

        r_cos = arena("r_cos", [P, TL], 121 * K)
        r_sin = arena("r_sin", [P, TL], 123 * K)
        r_rot = arena("r_rot", [P, P], 125 * K)
        r_sq = [arena(f"r_sq{i}", [P, TA], (32 + 3 * i) * K) for i in range(2)]
        r_rs = [arena(f"r_rs{i}", [P, TA], (38 + 3 * i) * K) for i in range(2)]
        r_t = [arena(f"r_t{i}", [P, TL], (44 + 2 * i) * K) for i in range(2)]

        class Rope(Phase):

            def __init__(self, tiles, which, gate, temps):
                super().__init__()
                self.tiles, self.which, self.gate, self.val, self.temps = tiles, which, gate, loaded(3), temps
                n = len(tiles)
                self.head_sq, self.head_sum, self.head_rstd = cnt.take("head_sq", n), cnt.take("head_sum", n), cnt.take("head_rstd", n)
                self.head_normed, self.rotated, self.rope_cos = cnt.take("head_normed", n), cnt.take("rotated", n), cnt.take("rope_cos", n)
                self.rope_sin, self.roped = cnt.take("rope_sin", n), cnt.take("roped", n)
                self.done = upto(self.roped, n)

            def sp(self, sp):
                sp.wait_ge(*self.gate)
                for name, dst in (("cos", r_cos), ("sin", r_sin), ("rot", r_rot)):
                    a, w = CST[f"{name}{self.which}"]
                    sp.dma_start(dst[:], cst[:, a:a + w]).then_inc(phase_in, 16)

            def act(self, act):
                act.wait_ge(*self.gate)
                for j, (x_, t, gain) in enumerate(self.tiles):
                    if gain is not None:
                        sig(nc.scalar, nc.scalar.activation(r_sq[j % 2][:, 0:t], x_, ACT.Square), self.head_sq)
                        act.wait_ge(*upto(self.head_sum, j + 1))
                        if j >= 2:
                            act.wait_ge(*upto(self.head_normed, j - 1))
                        r = r_rs[j % 2]
                        if t > TL:
                            astep(nc.scalar.activation(r[:, TL:t], ps[2 * (j % 2) + 1][:, 0:t - TL], ACT.Ln, scale=1.0 / P, bias=epsv[:, 0:1]))
                        astep(nc.scalar.activation(r[:, 0:TL], ps[2 * (j % 2)][:, 0:TL], ACT.Ln, scale=1.0 / P, bias=epsv[:, 0:1]))
                        sig(nc.scalar, nc.scalar.activation(r[:, 0:t], r[:, 0:t], ACT.Exp, scale=-0.5), self.head_rstd)

            def pe(self, pe):
                pe.wait_ge(*self.gate)
                pe.wait_ge(phase_in, self.val)
                for j, (x_, t, gain) in enumerate(self.tiles):
                    if gain is not None:
                        pe.wait_ge(*upto(self.head_sq, j + 1))
                        if t > TL:
                            nc.tensor.matmul(ps[2 * (j % 2) + 1][:, 0:t - TL], ones[:], r_sq[j % 2][:, TL:t], start=True, stop=True)
                        nc.tensor.matmul(ps[2 * (j % 2)][:, 0:TL], ones[:], r_sq[j % 2][:, 0:TL], start=True, stop=True).then_inc(self.head_sum[0], 1)
                        pe.wait_ge(*upto(self.head_normed, j + 1))
                    if j >= 2:
                        pe.wait_ge(*upto(self.rope_sin, j - 1))
                    nc.tensor.matmul(ps[4 + j % 2][:, 0:TL], r_rot[:], x_[:, 0:TL], start=True, stop=True).then_inc(self.rotated[0], 1)

            def dve(self, dve):
                dve.wait_ge(*self.gate)
                dve.wait_ge(phase_in, self.val)
                for j, (x_, t, gain) in enumerate(self.tiles):
                    if gain is not None:
                        dve.wait_ge(*upto(self.head_rstd, j + 1))
                        sig(nc.vector, nc.vector.scalar_tensor_tensor(x_, x_, gain, r_rs[j % 2][:, 0:t], ALU.mult, ALU.mult), self.head_normed)
                    dve.wait_ge(*upto(self.rotated, j + 1))
                    tt = self.temps[j % 2]
                    sig(nc.vector, nc.vector.tensor_tensor(tt[:], r_sin[:], ps[4 + j % 2][:, 0:TL], ALU.mult), self.rope_sin)
                    sig(nc.vector, nc.vector.tensor_tensor(x_[:, 0:TL], x_[:, 0:TL], r_cos[:], ALU.mult), self.rope_cos)
                    dve.wait_ge(*upto(self.rope_cos, j + 1))
                    sig(nc.vector, nc.vector.tensor_tensor(x_[:, 0:TL], x_[:, 0:TL], tt[:], ALU.add), self.roped)

        class Tokens(Phase):

            def __init__(self, pairs, gate):
                super().__init__()
                self.groups = [pairs[i:i + 4] for i in range(0, len(pairs), 4)]
                self.gate = gate
                self.turned, self.copied = cnt.take("turned", len(self.groups)), cnt.take("turned_copied", len(self.groups))
                self.done = upto(self.copied, len(self.groups))

            def pe(self, pe):
                pe.wait_ge(*self.gate)
                for i, g in enumerate(self.groups):
                    if i >= 2:
                        pe.wait_ge(*upto(self.copied, i - 1))
                    for j, (src, _) in enumerate(g):
                        last = nc.tensor.transpose(ps[6 + i % 2][:, j * P:(j + 1) * P], src, ident[:])
                    last.then_inc(self.turned[0], 1)

            def act(self, act):
                for i, g in enumerate(self.groups):
                    act.wait_ge(*upto(self.turned, i + 1))
                    for j, (_, dst) in enumerate(g):
                        ins = nc.scalar.copy(dst, ps[6 + i % 2][:, j * P:(j + 1) * P])
                    sig(nc.scalar, ins, self.copied)

        s_buf = [arena(f"s_buf{i}", [P, 10 * P], 5 * K * i) for i in range(2)]
        p_buf2 = [arena(f"p_buf2{i}", [P, 10 * P], (10 + 5 * i) * K) for i in range(2)]
        pt_buf = [arena(f"pt_buf{i}", [P, 10, P], (20 + 5 * i) * K) for i in range(2)]

        class Attention(Phase):

            def __init__(self, units, gate, masks=()):
                super().__init__()
                self.units, self.gate, self.masks = units, gate, masks
                self.val = loaded(len(masks)) if masks else None
                n = len(units)
                self.groups, total = [], 0
                for u in units:
                    blocks = len(u["values"])
                    self.groups.append((total, (blocks + 3) // 4))
                    total += (blocks + 3) // 4
                self.qk_in_ps, self.qk_copied, self.row_max = cnt.take("qk_in_ps", n), cnt.take("qk_copied", n), cnt.take("row_max", n)
                self.neg_max, self.p_exp, self.p_inv = cnt.take("neg_max", n), cnt.take("p_exp", n), cnt.take("p_inv", n)
                self.p_normed, self.pt_in_ps, self.pt_copied = cnt.take("p_normed", n), cnt.take("pt_in_ps", total), cnt.take("pt_copied", total)
                self.pv_in_ps, self.att_hi, self.att_lo = cnt.take("pv_in_ps", n), cnt.take("att_hi", n), cnt.take("att_lo", n)
                self.done = upto(self.att_lo, n)

            def sp(self, sp):
                if self.masks:
                    sp.wait_ge(*self.gate)
                for name, dst in self.masks:
                    a, w = CST[name]
                    sp.dma_start(dst, cst[:, a:a + w]).then_inc(phase_in, 16)

            def pe(self, pe):
                pe.wait_ge(*self.gate)
                n = len(self.units)
                for u in range(n + 1):
                    if u < n:
                        if u >= 1:
                            pe.wait_ge(*upto(self.qk_copied, u))
                        for b, (keys, w, _) in enumerate(self.units[u]["segs"]):
                            last = nc.tensor.matmul(ps[b][:, 0:w], self.units[u]["q"][b], keys, start=True, stop=True)
                        last.then_inc(self.qk_in_ps[0], 1)
                    if u >= 1:
                        m = u - 1
                        g0, ng = self.groups[m]
                        vals = self.units[m]["values"]
                        pe.wait_ge(*upto(self.p_normed, m + 1))
                        for g in range(ng):
                            if g0 + g >= 2:
                                pe.wait_ge(*upto(self.pt_copied, g0 + g - 1))
                            for j in range(4 * g, min(4 * g + 4, len(vals))):
                                last = nc.tensor.transpose(ps[3 + (g0 + g) % 2][:, (j % 4) * P:(j % 4 + 1) * P],
                                                           p_buf2[m % 2][:, j * P:(j + 1) * P], ident[:])
                            last.then_inc(self.pt_in_ps[0], 1)
                        if m >= 2:
                            pe.wait_ge(*upto(self.att_lo, m - 1))
                        for j, v in enumerate(vals):
                            if j % 4 == 0:
                                pe.wait_ge(*upto(self.pt_copied, g0 + j // 4 + 1))
                            last = nc.tensor.matmul(ps[5 + m % 2][:, 0:P], v, pt_buf[m % 2][:, j], start=j == 0, stop=j == len(vals) - 1)
                        last.then_inc(self.pv_in_ps[0], 1)

            def dve(self, dve):
                if self.masks:
                    dve.wait_ge(phase_in, self.val)
                n = len(self.units)
                for u in range(n + 1):
                    if u < n:
                        mx, nm, sm, rc = (small[:, 32 + 4 * (u % 2) + i:33 + 4 * (u % 2) + i] for i in range(4))
                        un = self.units[u]
                        dve.wait_ge(*upto(self.qk_in_ps, u + 1))
                        off = 0
                        for b, (_, w, mask) in enumerate(un["segs"]):
                            dst = s_buf[u % 2][:, off:off + w]
                            if mask is None:
                                last = nc.vector.tensor_copy(dst, ps[b][:, 0:w])
                            else:
                                last = nc.vector.tensor_tensor(dst, ps[b][:, 0:w], mask, ALU.add)
                            off += w
                        sig(nc.vector, last, self.qk_copied)
                        dve.wait_ge(*upto(self.qk_copied, u + 1))
                        sig(nc.vector, nc.vector.tensor_reduce(mx, s_buf[u % 2][:, 0:off], AX.X, ALU.max), self.row_max)
                        dve.wait_ge(*upto(self.row_max, u + 1))
                        sig(nc.vector, nc.vector.tensor_scalar(nm, mx, -SCALE, None, ALU.mult), self.neg_max)
                        dve.wait_ge(*upto(self.p_exp, u + 1))
                        sig(nc.vector, nc.vector.reciprocal(rc, sm), self.p_inv)
                        dve.wait_ge(*upto(self.p_inv, u + 1))
                        p = p_buf2[u % 2][:, 0:off]
                        sig(nc.vector, nc.vector.tensor_scalar(p, p, rc, None, ALU.mult), self.p_normed)
                    if u >= 1:
                        m = u - 1
                        dve.wait_ge(*upto(self.att_hi, m + 1))
                        sig(nc.vector, nc.vector.tensor_tensor(self.units[m]["lo"], ps[5 + m % 2][:, 0:P], self.units[m]["hi"].bitcast(f32),
                                                ALU.subtract), self.att_lo)

            def act(self, act):
                n = len(self.units)
                for u in range(n + 1):
                    if u < n:
                        nm, sm = (small[:, 33 + 4 * (u % 2) + i:34 + 4 * (u % 2) + i] for i in range(2))
                        w = P * len(self.units[u]["values"])
                        act.wait_ge(*upto(self.neg_max, u + 1))
                        if u >= 2:
                            act.wait_ge(*upto(self.pv_in_ps, u - 1))
                        sig(nc.scalar, nc.scalar.activation(p_buf2[u % 2][:, 0:w], s_buf[u % 2][:, 0:w], ACT.Exp, bias=nm, scale=SCALE,
                                             accum_out=sm), self.p_exp)
                    if u >= 1:
                        m = u - 1
                        g0, ng = self.groups[m]
                        nv = len(self.units[m]["values"])
                        for g in range(ng):
                            e = min(4, nv - 4 * g)
                            act.wait_ge(*upto(self.pt_in_ps, g0 + g + 1))
                            sig(nc.scalar, nc.scalar.copy(pt_buf[m % 2][:, 4 * g:4 * g + e],
                                           ps[3 + (g0 + g) % 2][:, 0:e * P].rearrange("p (j t) -> p j t", j=e)), self.pt_copied)
                        act.wait_ge(*upto(self.pv_in_ps, m + 1))
                        sig(nc.scalar, nc.scalar.copy(self.units[m]["hi"], ps[5 + m % 2][:, 0:P]), self.att_hi)

        zx = arena("zx", [P, 48, TL], 32 * K)
        c_acc = [at("c_acc", [P, TL], o_xc + 4160), rstd]

        class SsmConv:

            def __init__(self):
                self.tap, self.out = cnt.take("conv_tap", 4 * 32), cnt.take("conv_out", 32)

            def act(self, g, act, i, a):
                for n in range(4):
                    act.wait_ge(chunk_done, g.tile(i, n))
                    dst = zx[:, bass.ds(4 * i + n, 1)].rearrange("p o t -> p (o t)")
                    if a < 4:
                        nc.scalar.activation(dst, g.out(n), ACT.Silu).then_inc(mm_free, 1)
                        continue
                    t = 4 * i + n - 16
                    act.wait_ge(self.tap[0], 4 + self.tap[1] + 4 * t)
                    nc.scalar.copy(pad[0][:, 3:3 + TL], g.out(n)).then_inc(mm_free, 1)
                    act.wait_ge(self.tap[0], 4 + self.tap[1] + 4 * t + 4)
                    nc.scalar.activation(dst, c_acc[n % 2][:], ACT.Silu, bias=V("conv_b", t)
                                         if isinstance(t, int) else vec[:, bass.ds(VEC["conv_b"][0] + t, 1)]).then_inc(self.out[0], 1)

            def dve(self, g, dve, i, a):
                if a < 4:
                    return
                for n in range(4):
                    t = 4 * i + n - 16
                    acc = c_acc[n % 2]
                    dve.wait_ge(mm_free, NBANK + g.tile0 + 4 * i + n + 1)
                    dve.wait_ge(self.out[0], 2 + self.out[1] + t - 1)
                    for j in range(4):
                        w = vec[:, bass.ds(VEC["conv_w"][0] + 32 * j + t, 1)]
                        src = pad[0][:, j:j + TL]
                        if j:
                            dve.wait_ge(self.tap[0], 4 + self.tap[1] + 4 * t + j)
                            ins = nc.vector.scalar_tensor_tensor(acc[:], src, w, acc[:], ALU.mult, ALU.add)
                        else:
                            ins = nc.vector.tensor_scalar(acc[:], src, w, None, ALU.mult)
                        ins.then_inc(self.tap[0], 1)

        b_tok = arena("b_tok", [P, 4, P], 0)
        x_dt = arena("x_dt", [P, 4, 256], 2 * K)
        x_dd = arena("x_dd", [P, 4, 256], 6 * K)
        s_cb = arena("s_cb", [P, 4, P], 10 * K)
        s_w = [arena(f"s_w{i}", [P, 4, P], o * K) for i, o in enumerate((12, 14, 22, 129))]
        s_prev = arena("s_prev", [P, 4, 256], 16 * K)
        s_tok = arena("s_tok", [P, 3, 4, NSH], 20 * K)
        s_cd = arena("s_cd", [P, 4, NSH], 21 * K + 512)
        d_dt = arena("d_dt", [NSH, TL], 22 * K)
        d_cs = arena("d_cs", [NSH, TL], 24 * K)
        d_ec = arena("d_ec", [NSH, TL], 26 * K)
        s_y = [arena(f"s_y{i}", [P, TL], (28 + 2 * i) * K) for i in range(2)]
        d_t = [arena(f"d_t{i}", [NSH, TL], (12 + 2 * i) * K) for i in range(3)]
        dtw = arena("dtw", [P, ND, NSH], 128 * K)
        ssm_hi = [arena(f"ssm_hi{k}", [P, TL], (32 + 32 + 2 * k) * K, f32r) for k in range(16)]
        ssm_lo = [arena(f"ssm_lo{k}", [P, TL], (32 + 2 * k) * K, f32r) for k in range(16)]

        class DtPart(Phase):

            def __init__(self, gate):
                super().__init__()
                self.gate, self.val = gate, loaded(2)
                self.dt_in_ps, self.dt_pos, self.dt_act = cnt.take("dt_in_ps", 1), cnt.take("dt_pos", 1), cnt.take("dt_act", 6)
                self.dt_dve, self.dt_turned, self.dt_tok = cnt.take("dt_dve", 6), cnt.take("dt_turned", 2), cnt.take("dt_tok", 2)
                self.done = upto(self.dt_tok, 2)

            def sp(self, sp):
                sp.wait_ge(*self.gate)
                sp.dma_start(dtw[:, :, :], w_dt).then_inc(phase_in, 16)
                a, w = CST["ssd_mask"]
                sp.dma_start(ssd_mask[:], cst[:, a:a + w]).then_inc(phase_in, 16)

            def pe(self, pe):
                pe.wait_ge(phase_in, self.val)
                pe.wait_ge(*self.gate)
                for k in range(ND):
                    for q, h in enumerate((h_hi, h_lo)):
                        last = nc.tensor.matmul(ps[7][0:NSH, :], dtw[:, k], h[:, k].bitcast(f32), start=k == 0 and q == 0,
                                                stop=k == ND - 1 and q == 1)
                last.then_inc(self.dt_in_ps[0], 1)
                pe.wait_ge(*upto(self.dt_dve, 5))
                for q, src in enumerate((d_cs, d_dt, d_t[0])):
                    for c in range(4):
                        nc.tensor.transpose(ps[6][:, (q * 4 + c) * NSH:(q * 4 + c + 1) * NSH], src[:, c * CH:(c + 1) * CH], ident[0:NSH, 0:NSH])
                nc.tensor.matmul(ps[5][:, 0:4 * NSH], ones[0:NSH, :], d_t[1][:, 0:4 * NSH], start=True, stop=True).then_inc(self.dt_turned[0], 2)

            def act(self, act):
                a, w = VEC["dt_bias"]
                bias = vec[0:NSH, a:a + 1]
                act.wait_ge(*upto(self.dt_pos, 1))
                astep(nc.scalar.activation(d_t[0][:], ps[7][0:NSH, :], ACT.Abs, bias=bias))
                astep(nc.scalar.activation(d_t[0][:], d_t[0][:], ACT.Exp, scale=-1.0))
                a, w = VEC["a_log"]
                sig(nc.scalar, nc.scalar.activation(small[0:NSH, 48:49], vec[0:NSH, a:a + 1], ACT.Exp), self.dt_act)
                act.wait_ge(*upto(self.dt_dve, 3))
                sig(nc.scalar, nc.scalar.activation(d_ec[:], d_cs[:], ACT.Exp), self.dt_act)
                act.wait_ge(*upto(self.dt_dve, 4))
                sig(nc.scalar, nc.scalar.activation(d_t[0][:], d_t[0][:], ACT.Exp), self.dt_act)
                act.wait_ge(*upto(self.dt_turned, 2))
                astep(nc.scalar.copy(s_tok[:, :, :, :].rearrange("p q c h -> p (q c h)"), ps[6][:, 0:12 * NSH]))
                sig(nc.scalar, nc.scalar.copy(s_cd[:, :, :].rearrange("p c h -> p (c h)"), ps[5][:, 0:4 * NSH]), self.dt_tok, 2)

            def dve(self, dve):
                a, w = VEC["dt_bias"]
                bias = vec[0:NSH, a:a + 1]
                e, s, u = d_t
                dve.wait_ge(*upto(self.dt_in_ps, 1))
                sig(nc.vector, nc.vector.tensor_scalar(d_dt[:], ps[7][0:NSH, :], bias, 0.0, ALU.add, ALU.max), self.dt_pos)
                dve.wait_ge(*upto(self.dt_act, 1))
                vstep(nc.vector.tensor_scalar(u[:], e[:], 2.0, None, ALU.add))
                vstep(nc.vector.reciprocal(u[:], u[:]))
                vstep(nc.vector.tensor_tensor(s[:], e[:], u[:], ALU.mult))
                vstep(nc.vector.tensor_tensor(u[:], s[:], s[:], ALU.mult))
                vstep(nc.vector.tensor_scalar(e[:], u[:], 2.0 / 17, 2.0 / 15, ALU.mult, ALU.add))
                for c in (13, 11, 9, 7, 5, 3, 1):
                    vstep(nc.vector.tensor_tensor(e[:], e[:], u[:], ALU.mult))
                    vstep(nc.vector.tensor_scalar(e[:], e[:], 2.0 / c, None, ALU.add))
                vstep(nc.vector.tensor_tensor(e[:], e[:], s[:], ALU.mult))
                vstep(nc.vector.tensor_tensor(d_dt[:], d_dt[:], e[:], ALU.add))
                vstep(nc.vector.tensor_scalar(small[0:NSH, 49:50], small[0:NSH, 48:49], -1.0, None, ALU.mult))
                vstep(nc.vector.tensor_scalar(e[:], d_dt[:], small[0:NSH, 49:50], None, ALU.mult))
                for c in range(4):
                    last = nc.vector.tensor_tensor_scan(d_cs[:, c * CH:(c + 1) * CH], ones[0:NSH, :], e[:, c * CH:(c + 1) * CH], 0.0, ALU.mult, ALU.add)
                sig(nc.vector, last, self.dt_dve, 3)
                dve.wait_ge(*upto(self.dt_dve, 3))
                v = d_cs[:, :].rearrange("p (c t) -> p c t", c=4)
                sig(nc.vector, nc.vector.tensor_tensor(e[:, :].rearrange("p (c t) -> p c t", c=4), v[:, :, CH - 1:CH].to_broadcast([NSH, 4, CH]), v,
                                        ALU.subtract), self.dt_dve)
                dve.wait_ge(*upto(self.dt_act, 3))
                for c in range(4):
                    last = nc.vector.tensor_scalar(s[:, c * NSH:(c + 1) * NSH], ident[0:NSH, 0:NSH], d_ec[:, c * CH + CH - 1:c * CH + CH], None, ALU.mult)
                sig(nc.vector, last, self.dt_dve)

        class Ssd(Phase):

            def __init__(self, g, gate, mask_val):
                super().__init__()
                self.g, self.gate, self.mask_val = g, gate, mask_val
                self.ssd_turned, self.ssd_b, self.x_ready = cnt.take("ssd_turned", 1), cnt.take("ssd_b", 1), cnt.take("x_ready", 1)
                self.xd_ready, self.st_in_ps, self.prev_ready = cnt.take("xd_ready", 1), cnt.take("st_in_ps", 3), cnt.take("prev_ready", 4)
                self.row_in_ps, self.seg_ready, self.seg_exp = cnt.take("row_in_ps", 4), cnt.take("seg_ready", 4), cnt.take("seg_exp", 4)
                self.seg_w, self.y_in_ps, self.e_read = cnt.take("seg_w", 4), cnt.take("y_in_ps", 2), cnt.take("e_read", 2)
                self.y_tile, self.y_step, self.y_sq = cnt.take("y_tile", 2), cnt.take("y_step", 8), cnt.take("y_sq", 2)
                self.y_sum, self.y_rstd, self.y_scaled2 = cnt.take("y_sum", 1), cnt.take("y_rstd", 1), cnt.take("y_scaled2", 2)
                self.y_hi, self.y_lo = cnt.take("y_hi", 2), cnt.take("y_lo", 2)
                self.done = upto(self.y_lo, 2)

            def pe(self, pe):
                g = self.g
                pe.wait_ge(*self.gate)
                xs = [zx[:, 16 + 2 * g + t] for t in range(2)]
                bt, ct = zx[:, 32 + g], zx[:, 40 + g]
                for c in range(4):
                    nc.tensor.transpose(ps[0][:, c * P:(c + 1) * P], bt[:, c * CH:(c + 1) * CH], ident[:])
                for c in range(4):
                    for t in range(2):
                        col = (c % 2) * 256 + t * P
                        nc.tensor.transpose(ps[1 + c // 2][:, col:col + P], xs[t][:, c * CH:(c + 1) * CH], ident[:])
                for c in range(4):
                    last = nc.tensor.matmul(ps[3][:, c * P:(c + 1) * P], bt[:, c * CH:(c + 1) * CH], ct[:, c * CH:(c + 1) * CH], start=True, stop=True)
                last.then_inc(self.ssd_turned[0], 1)
                pe.wait_ge(*upto(self.ssd_b, 1))
                pe.wait_ge(*upto(self.xd_ready, 1))
                for c in range(3):
                    nc.tensor.matmul(ps[4 + c // 2][:, (c % 2) * 256:(c % 2 + 1) * 256], b_tok[:, c], x_dd[:, c], start=True, stop=True).then_inc(self.st_in_ps[0], 1)

                for hh in range(4):
                    h = 4 * g + hh
                    if hh >= 1:
                        pe.wait_ge(*upto(self.seg_ready, hh))
                    nc.tensor.matmul(ps[6][:], ident[0:NSH, h:h + 1].to_broadcast([NSH, P]), d_cs[:], start=True, stop=True).then_inc(self.row_in_ps[0], 1)
                for hh in range(4):
                    pe.wait_ge(*upto(self.seg_w, hh + 1))
                    for c in range(4):
                        r = 64 * (hh % 2)
                        nc.tensor.matmul(ps[7 if hh < 2 else 2][r:r + 64, c * P:(c + 1) * P], x_dt[:, c, hh * 64:(hh + 1) * 64], s_w[hh][:, c],
                                         start=True, stop=True)
                for t in range(2):
                    if t == 0:
                        pe.wait_ge(*upto(self.prev_ready, 4))
                    else:
                        pe.wait_ge(*upto(self.y_tile, 1))
                    for c in range(4):
                        nc.tensor.matmul(ps[0][:, c * P:(c + 1) * P], s_prev[:, c, t * P:(t + 1) * P], ct[:, c * CH:(c + 1) * CH], start=True, stop=True)
                    for e in range(2):
                        h = 4 * g + 2 * t + e
                        last = nc.tensor.matmul(ps[1][64 * e:64 * e + 64, :], ident[0:NSH, h:h + 1].to_broadcast([NSH, 64]), d_ec[:],
                                                start=True, stop=True)
                    last.then_inc(self.y_in_ps[0], 1)
                for t in range(2):
                    pe.wait_ge(*upto(self.y_sq, t + 1))
                    last = nc.tensor.matmul(ps[3][:], ones[:], s_w[t][:, :, :].rearrange("p c l -> p (c l)"), start=t == 0, stop=t == 1)
                last.then_inc(self.y_sum[0], 1)

            def act(self, act):
                g = self.g
                act.wait_ge(*upto(self.ssd_turned, 1))
                astep(nc.scalar.copy(b_tok[:, :, :].rearrange("p c l -> p (c l)"), ps[0][:]))
                sig(nc.scalar, nc.scalar.copy(s_cb[:, :, :].rearrange("p c l -> p (c l)"), ps[3][:]), self.ssd_b)
                for hh in range(4):
                    act.wait_ge(*upto(self.seg_ready, hh + 1))
                    w = s_w[hh][:, :, :]
                    sig(nc.scalar, nc.scalar.activation(w, w, ACT.Exp), self.seg_exp)
                for t in range(2):
                    act.wait_ge(*upto(self.y_in_ps, t + 1))
                    sig(nc.scalar, nc.scalar.copy(s_y[0][:], ps[1][:]), self.e_read)
                    act.wait_ge(*upto(self.y_tile, t + 1))
                    sig(nc.scalar, nc.scalar.activation(s_w[t][:, :, :].rearrange("p c l -> p (c l)"), zx[:, 16 + 2 * g + t], ACT.Square), self.y_sq)
                act.wait_ge(*upto(self.y_sum, 1))
                astep(nc.scalar.activation(s_y[0][:], ps[3][:], ACT.Ln, scale=1.0 / 256, bias=epsv[:, 1:2]))
                sig(nc.scalar, nc.scalar.activation(s_y[0][:], s_y[0][:], ACT.Exp, scale=-0.5), self.y_rstd)
                for t in range(2):
                    act.wait_ge(*upto(self.y_scaled2, t + 1))
                    sig(nc.scalar, nc.scalar.copy(ssm_hi[2 * g + t][:], s_y[1][:]), self.y_hi)

            def dve(self, dve):
                g = self.g
                if self.mask_val:
                    dve.wait_ge(phase_in, self.mask_val)
                dve.wait_ge(*self.gate)
                dve.wait_ge(*upto(self.ssd_turned, 1))
                for c2 in range(2):
                    v = lambda a: a[:, 2 * c2:2 * c2 + 2, :].rearrange("p c (h q) -> p c h q", h=4)
                    tok = lambda q: s_tok[:, q, 2 * c2:2 * c2 + 2, 4 * g:4 * g + 4].unsqueeze(3).to_broadcast([P, 2, 4, 64])
                    last = nc.vector.tensor_tensor(v(x_dt), ps[1 + c2][:, :].rearrange("p (c h q) -> p c h q", c=2, h=4), tok(1), ALU.mult)
                sig(nc.vector, last, self.x_ready)
                dve.wait_ge(*upto(self.x_ready, 1))
                for c2 in range(2):
                    v = lambda a: a[:, 2 * c2:2 * c2 + 2, :].rearrange("p c (h q) -> p c h q", h=4)
                    tok = lambda q: s_tok[:, q, 2 * c2:2 * c2 + 2, 4 * g:4 * g + 4].unsqueeze(3).to_broadcast([P, 2, 4, 64])
                    last = nc.vector.tensor_tensor(v(x_dd), v(x_dt), tok(2), ALU.mult)
                sig(nc.vector, last, self.xd_ready)
                sig(nc.vector, nc.vector.memset(s_prev[:, 0], 0.0), self.prev_ready)
                dve.wait_ge(*upto(self.ssd_b, 1))

                def segment(hh):
                    h = 4 * g + hh
                    dve.wait_ge(*upto(self.row_in_ps, hh + 1))
                    for c in range(4):
                        last = nc.vector.scalar_tensor_tensor(s_w[hh][:, c], ps[6][:, c * P:(c + 1) * P], s_tok[:, 0, c, h:h + 1], ssd_mask[:],
                                                              ALU.subtract, ALU.add)
                    sig(nc.vector, last, self.seg_ready)

                for c in range(3):
                    dve.wait_ge(*upto(self.prev_ready, c + 1))
                    dst = s_prev[:, c + 1].rearrange("p (h q) -> p h q", h=4)
                    vstep(nc.vector.tensor_tensor(dst, s_prev[:, c].rearrange("p (h q) -> p h q", h=4),
                                                  s_cd[:, c, 4 * g:4 * g + 4].unsqueeze(2).to_broadcast([P, 4, 64]), ALU.mult))
                    dve.wait_ge(*upto(self.st_in_ps, max(c + 1, 2)))
                    sig(nc.vector, nc.vector.tensor_tensor(s_prev[:, c + 1], s_prev[:, c + 1], ps[4 + c // 2][:, (c % 2) * 256:(c % 2 + 1) * 256],
                                            ALU.add), self.prev_ready)
                for hh in range(5):
                    if hh < 4:
                        segment(hh)
                    if hh >= 1:
                        dve.wait_ge(*upto(self.seg_exp, hh))
                        w = s_w[hh - 1][:, :, :]
                        sig(nc.vector, nc.vector.tensor_tensor(w, w, s_cb[:, :, :], ALU.mult), self.seg_w)
                for t in range(2):
                    x_ = zx[:, 16 + 2 * g + t]
                    a, w = VEC["d_skip"]
                    dve.wait_ge(*upto(self.e_read, t + 1))
                    vstep(nc.vector.tensor_tensor(s_y[1][:], s_y[0][:], ps[0][:], ALU.mult))
                    vstep(nc.vector.tensor_tensor(s_y[1][:], s_y[1][:], ps[7 if t == 0 else 2][:], ALU.add))
                    vstep(nc.vector.scalar_tensor_tensor(s_y[1][:], x_, vec[:, a + 2 * g + t:a + 2 * g + t + 1], s_y[1][:], ALU.mult, ALU.add))
                    sig(nc.vector, nc.vector.tensor_tensor(x_, s_y[1][:], zx[:, 2 * g + t], ALU.mult), self.y_tile)
                dve.wait_ge(*upto(self.y_rstd, 1))
                for t in range(2):
                    sig(nc.vector, nc.vector.scalar_tensor_tensor(s_y[1][:], zx[:, 16 + 2 * g + t], V("ssm_norm", 2 * g + t), s_y[0][:], ALU.mult,
                                                   ALU.mult), self.y_scaled2)
                    dve.wait_ge(*upto(self.y_hi, t + 1))
                    sig(nc.vector, nc.vector.tensor_tensor(ssm_lo[2 * g + t][:], s_y[1][:], ssm_hi[2 * g + t][:].bitcast(f32), ALU.subtract), self.y_lo)

        class ConvFfn:

            def __init__(self, layer):
                self.layer = layer
                self.tap, self.silu, self.gated = cnt.take("ffn_tap", 6 * NH), cnt.take("ffn_silu", NH), cnt.take("ffn_gated", NH)
                self.hi, self.lo = cnt.take("hid_hi_ready", NH), cnt.take("hid_lo_ready", NH)
                self.done = upto(self.lo, NH, 2)

            def hid(self, buf, i, q):
                return buf[:, bass.ds(2 * i + q, 1)].rearrange("p o t -> p (o t)")

            def act(self, g, act, i, a):
                for q in range(2):
                    m = 2 * i + q
                    for s in range(2):
                        act.wait_ge(chunk_done, g.tile(i, 2 * q + s))
                        act.wait_ge(self.tap[0], 6 + self.tap[1] + 6 * m - 3 + 3 * s)
                        nc.scalar.copy(pad[s][:, 2:2 + TL], g.out(2 * q + s)).then_inc(mm_free, 1)
                    act.wait_ge(self.tap[0], 6 + self.tap[1] + 6 * m + 3)
                    nc.scalar.activation(wk[0][:], wk[0][:], ACT.Silu).then_inc(self.silu[0], 1)
                    act.wait_ge(self.gated[0], 1 + self.gated[1] + m + 1)
                    nc.scalar.copy(self.hid(hid_hi, i, q), wk[2][:]).then_inc(self.hi[0], 1)

            def dve(self, g, dve, i, a):
                for q in range(2):
                    m = 2 * i + q
                    dve.wait_ge(self.gated[0], 1 + self.gated[1] + m)
                    for s in range(2):
                        dve.wait_ge(mm_free, NBANK + g.tile0 + 4 * i + 2 * q + s + 1)
                        for j in range(3):
                            w = vec[:, bass.ds(VEC["ffn_conv"][0] + 132 * self.layer + 44 * j + 4 * i + 2 * q + s, 1)]
                            src = pad[s][:, j:j + TL]
                            if j:
                                dve.wait_ge(self.tap[0], 6 + self.tap[1] + 6 * m + 3 * s + j)
                                ins = nc.vector.scalar_tensor_tensor(wk[s][:], src, w, wk[s][:], ALU.mult, ALU.add)
                            else:
                                ins = nc.vector.tensor_scalar(wk[s][:], src, w, None, ALU.mult)
                            ins.then_inc(self.tap[0], 1)
                    dve.wait_ge(self.tap[0], 6 + self.tap[1] + 6 * m + 6)
                    dve.wait_ge(self.lo[0], 2 + self.lo[1] + m)
                    dve.wait_ge(self.silu[0], self.silu[1] + m + 1)
                    nc.vector.tensor_tensor(wk[2][:], wk[0][:], wk[1][:], ALU.mult).then_inc(self.gated[0], 1)
                    dve.wait_ge(self.hi[0], self.hi[1] + m + 1)
                    nc.vector.tensor_tensor(self.hid(hid_lo, i, q), wk[2][:], self.hid(hid_hi, i, q).bitcast(f32), ALU.subtract).then_inc(self.lo[0], 1)

        class Pads(Phase):

            def __init__(self, gate):
                super().__init__()
                self.gate, self.zeroed = gate, cnt.take("pads_zeroed", 2)

            def dve(self, dve):
                dve.wait_ge(*self.gate)
                for i in range(2):
                    sig(nc.vector, nc.vector.memset(pad[i][:], 0.0), self.zeroed)

            def act(self, act):
                act.wait_ge(*upto(self.zeroed, 2))

        class Load(Phase):

            def __init__(self):
                super().__init__()

            def sp(self, sp):
                sp.dma_start(vec[:], vecs).then_inc(const_in, 16)
                a, w = CST["ident"]
                sp.dma_start(ident[:], cst[:, a:a + w]).then_inc(const_in, 16)
                sp.dma_start(x[:, :, :], xT.rearrange("(k p) t -> p k t", p=P)).then_inc(const_in, 16)
                sp.dma_start(xc[:, :, :], ctxT.rearrange("(k p) t -> p k t", p=P)).then_inc(const_in, 16)

            def dve(self, dve):
                nc.vector.memset(ones[:], 1.0)
                nc.vector.memset(epsv[:, 0:1], EPS)
                vstep(nc.vector.memset(epsv[:, 1:2], GEPS))
                for sem_, n in SEEDS:
                    if n and sem_ is not mm_free and sem_ is not chunk_done and sem_ is not split_done:
                        dve.sem_inc(sem_, n)
                dve.wait_ge(const_in, 64)

            def act(self, act):
                act.sem_inc(mm_free, NBANK)
                act.wait_ge(const_in, 64)
                act.wait_ge(dve_step, 1)

            def pool(self, pool):
                pool.sem_inc(split_done, RAW)

            def pe(self, pe):
                pe.sem_inc(chunk_done, SPL)
                pe.wait_ge(dve_step, 1)
                pe.wait_ge(const_in, 64)

        class Store(Phase):
            def __init__(self, rms):
                super().__init__()
                self.rms, self.scaled = rms, cnt.take("out_scaled", ND)

            def dve(self, dve):
                dve.wait_ge(*self.rms.done)
                for k in range(ND):
                    sig(nc.vector, nc.vector.scalar_tensor_tensor(y[:, k], x[:, k], V("final_norm", k), rstd[:], ALU.mult, ALU.mult), self.scaled)

            def sp(self, sp):
                for k in range(ND):
                    sp.wait_ge(*upto(self.scaled, k + 1))
                    sp.dma_start(out[k * P:(k + 1) * P, :], y[:, k]).then_inc(stored, 16)
                sp.wait_ge(stored, 16 * ND)

        stored = cnt.take("stored", 0)[0]
        xt, xct = lambda k: x[:, k], lambda k: xc[:, k]
        yt, yct = lambda k: y[:, k], lambda k: yc[:, k]
        hhi, hlo = lambda k: h_hi[:, k], lambda k: h_lo[:, k]
        hrhs = lambda k: (h_hi[:, k], h_lo[:, k])
        crhs = lambda k: (c_hi[:, k], c_lo[:, k])
        hcrhs = lambda k: (h_hi[:, k, 0:TC], h_lo[:, k, 0:TC])
        always = lambda k: (const_in, 64)
        gain = lambda v, q: lambda k: gains[:, v, q, k:k + 1]
        shift = lambda v, q: lambda k: mods[:, v, 24 * q + k:24 * q + k + 1]
        vgain = lambda name, i=0: lambda k: V(name, i + k)
        same = lambda g: lambda k: g

        Load()
        ada = Ada(ada0, 0, None)
        r = Rms(xt, ND, TL, D, 0, always)
        ap = Apply(xt, ND, TL, gain(0, 0), shift(0, 0), hhi, hlo, r, gate=ada.done)
        r = Rms(xct, ND, TC, D, 0, same(ap.done))
        ap = Apply(xct, ND, TC, gain(1, 0), shift(1, 0), lambda k: c_hi[:, k], lambda k: c_lo[:, k], r)
        gm = Gemm(w_ab_in, 24, 1, 8, hrhs, ctx_rhs=crhs, evac_act=z_evac_act, peel=(1, 2), gate=ap.done)
        hp = HgPrep(gm.all_read)
        u = None
        for head in range(HEADS):
            for back in range(2):
                u = HgUnit(head, back, hp.val, gm.all_read)
            ho_ = HgOut(head, u)
        pl = Pool(upto(ho_.mix_lo, 1))
        gm = Gemm(w_ab_out, 8, 1, 8, lambda k: (mix_hi[k][:, LAT], mix_lo[k][:, LAT]), ctx_rhs=lambda k: (mix_hi[k][:, CTX], mix_lo[k][:, CTX]),
                  evac_act=y_evac(y, yc), gate=upto(pl.pool_lo, 4))
        r = Rms(yt, ND, TL, D, 0, same(gm.all_read))
        re = Residual(xt, yt, ND, TL, gain(0, 1), r)
        r = Rms(yct, ND, TC, D, 0, same(re.ready(ND - 1)))
        rc = Residual(xct, yct, ND, TC, gain(1, 1), r)

        def ffn(up, down, t, rhs, gate, evac, dst):
            g = Gemm(up, 2 * NH, 1, 8, rhs, t=t, evac_act=evac.act, evac_dve=evac.dve, gate=gate)
            return Gemm(down, 8, 2, KC, lambda k: (hid_hi[:, k, 0:t], hid_lo[:, k, 0:t]), t=t, evac_act=y_evac(dst), gate=evac.done)

        r = Rms(xt, ND, TL, D, 0, same(rc.ready(ND - 1)))
        ap = Apply(xt, ND, TL, gain(0, 2), shift(0, 1), hhi, hlo, r)
        gm = ffn(w_f0u, w_f0d, TL, hrhs, ap.done, Swiglu(TL), y)
        r = Rms(yt, ND, TL, D, 0, same(gm.all_read))
        re = Residual(xt, yt, ND, TL, gain(0, 3), r)
        r = Rms(xct, ND, TC, D, 0, same(re.ready(ND - 1)))
        ap = Apply(xct, ND, TC, gain(1, 2), shift(1, 1), lambda k: h_hi[:, k, 0:TC], lambda k: h_lo[:, k, 0:TC], r)
        gm = ffn(w_f0u, w_f0d, TC, hcrhs, ap.done, Swiglu(TC), yc2)
        r = Rms(lambda k: yc2[:, k], ND, TC, D, 0, same(gm.all_read))
        rc = Residual(xct, lambda k: yc2[:, k], ND, TC, gain(1, 3), r)

        z1 = arena("z1", [P, 12, TA], 48 * K)
        v1 = arena("v1", [P, 12, P], 84 * K)
        o1_hi = [arena(f"o1_hi{h}", [P, TL], (48 + 3 * h) * K, f32r) for h in range(8)]
        o1_lo = [arena(f"o1_lo{h}", [P, TL], (90 + 2 * h) * K, f32r) for h in range(8)]

        def z1_evac(g, act, i, a):
            for n in range(4):
                act.wait_ge(chunk_done, g.tile(i, n))
                dst = z1[:, bass.ds(4 * i + n, 1)].rearrange("p o t -> p (o t)")
                ins = nc.scalar.copy(dst[:, 0:TL], g.out(n))
                if a == 2:
                    ins = nc.scalar.copy(dst[:, TL:TA], g.ctx_out(n))
                ins.then_inc(mm_free, 1)

        ada = Ada(ada1, 1, rc.ready(ND - 1))
        r = Rms(xt, ND, TL, D, 0, same(ada.done))
        ap = Apply(xt, ND, TL, gain(0, 0), shift(0, 0), hhi, hlo, r)
        r = Rms(xct, ND, TC, D, 0, same(ap.done))
        ap = Apply(xct, ND, TC, gain(1, 0), shift(1, 0), lambda k: c_hi[:, k], lambda k: c_lo[:, k], r)
        gm = Gemm(w_att_in, 12, 1, 8, hrhs, ctx_rhs=crhs, ctx_from=8, evac_act=z1_evac, peel=(2,), gate=ap.done)
        rp = Rope([(z1[:, j, 0:TL], TL, V("qn")) for j in range(8)] + [(z1[:, 8 + j], TA, V("kn")) for j in range(2)], 1, gm.all_read, r_t)
        tk = Tokens([(z1[:, 10 + v, c * P:(c + 1) * P], v1[:, v * 6 + c]) for v in range(2) for c in range(6)], rp.done)
        at_ = Attention([dict(q=[z1[:, h, n * P:(n + 1) * P]] * 2,
                              segs=[(z1[:, 8 + h // 4, 0:TL], TL, None), (z1[:, 8 + h // 4, TL:TA], TC, None)],
                              values=[v1[:, (h // 4) * 6 + c] for c in range(6)],
                              hi=o1_hi[h][:, n * P:(n + 1) * P], lo=o1_lo[h][:, n * P:(n + 1) * P])
                         for h in range(8) for n in range(4)], tk.done)
        gm = Gemm(w_att_out, 8, 1, 8, lambda k: (o1_hi[k][:], o1_lo[k][:]), evac_act=y_evac(y), gate=at_.done)
        r = Rms(yt, ND, TL, D, 0, same(gm.all_read))
        re = Residual(xt, yt, ND, TL, gain(0, 1), r)
        r = Rms(xt, ND, TL, D, 0, re.ready)
        ap = Apply(xt, ND, TL, gain(0, 2), shift(0, 1), hhi, hlo, r)
        gm = ffn(w_f1u, w_f1d, TL, hrhs, ap.done, Swiglu(TL), y)
        r = Rms(yt, ND, TL, D, 0, same(gm.all_read))
        re = Residual(xt, yt, ND, TL, gain(0, 3), r)

        r = Rms(xt, ND, TL, D, 0, re.ready)
        ap = Apply(xt, ND, TL, vgain("a_norm"), None, hhi, hlo, r)
        Pads(ap.done)
        sc = SsmConv()
        gm = Gemm(w_ssm, 48, 1, 8, hrhs, evac_act=sc.act, evac_dve=sc.dve, peel=(4,), gate=ap.done)
        dt = DtPart(upto(sc.out, 32, 2))
        s = None
        for g in range(NG):
            s = Ssd(g, s.done if s else dt.done, dt.val if g == 0 else None)
        gm = Gemm(w_ssm_out, 8, 2, 8, lambda k: (ssm_hi[k][:], ssm_lo[k][:]), evac_act=y_evac(y), gate=s.done)
        re = Residual(xt, yt, ND, TL, None, None, gate=gm.all_read)

        def conv_ffn(layer, up, down, r, gate_pads):
            ap = Apply(xt, ND, TL, vgain("ffn_norm", 8 * layer), None, hhi, hlo, r)
            Pads(ap.done)
            gm = ffn(up, down, TL, hrhs, ap.done, ConvFfn(layer), y)
            return Residual(xt, yt, ND, TL, None, None, gate=gm.all_read)

        re = conv_ffn(0, w_f2u, w_f2d, Rms(xt, ND, TL, D, 0, re.ready), None)

        kv = arena("kv", [P, 12, TL], 32 * K)
        q2 = arena("q2", [P, 24, TL], 56 * K)
        v2 = arena("v2", [P, 24, P], 104 * K)
        band, dil4, dil16 = arena("band", [P, 256], 116 * K), arena("dil4", [P, 512], 117 * K), arena("dil16", [P, 512], 119 * K)
        o2_hi = [arena(f"o2_hi{h}", [P, TL], (56 + 2 * h) * K, f32r) for h in range(8)]
        o2_lo = [arena(f"o2_lo{h}", [P, TL], (72 + 2 * h) * K, f32r) for h in range(8)]
        r = Rms(xt, ND, TL, D, 0, re.ready)
        ap = Apply(xt, ND, TL, vgain("kv_norm"), None, hhi, hlo, r)
        gm = Gemm(w_kv, 12, 1, 8, hrhs, evac_act=y_evac(kv), gate=ap.done)
        ap = Apply(xt, ND, TL, vgain("b_norm"), None, hhi, hlo, r, gate=gm.all_read)
        gm = Gemm(w_q, 24, 1, 8, hrhs, evac_act=y_evac(q2), gate=ap.done)
        rp = Rope([(kv[:, j], TL, None) for j in range(6)] + [(q2[:, j], TL, None) for j in range(24)], 2, gm.all_read, s_y)
        tk = Tokens([(kv[:, 6 + v, c * P:(c + 1) * P], v2[:, v * 4 + c]) for v in range(6) for c in range(4)], rp.done)

        def dilated(h, n):
            kh = lambda g: kv[:, 2 * g + h // 4]
            first = max(n - 1, 0)
            near = (n + 1 - first) * P
            return dict(q=[q2[:, 8 * g + h, n * P:(n + 1) * P] for g in range(3)],
                        segs=[(kh(0)[:, first * P:(n + 1) * P], near, band[:, 256 - near:256]),
                              (kh(1)[:, 0:(n + 1) * P], (n + 1) * P, dil4[:, (3 - n) * P:512]),
                              (kh(2)[:, 0:(n + 1) * P], (n + 1) * P, dil16[:, (3 - n) * P:512])],
                        values=[v2[:, (h // 4) * 4 + c] for c in range(first, n + 1)]
                        + [v2[:, (2 * g + h // 4) * 4 + c] for g in (1, 2) for c in range(n + 1)],
                        hi=o2_hi[h][:, n * P:(n + 1) * P], lo=o2_lo[h][:, n * P:(n + 1) * P])

        at_ = Attention([dilated(h, n) for h in range(8) for n in range(4)], tk.done,
                        masks=(("band", band[:]), ("dil4", dil4[:]), ("dil16", dil16[:])))
        gm = Gemm(w_o, 8, 1, 8, lambda k: (o2_hi[k][:], o2_lo[k][:]), evac_act=y_evac(y), gate=at_.done)
        re = Residual(xt, yt, ND, TL, None, None, gate=gm.all_read)
        re = conv_ffn(1, w_f3u, w_f3d, Rms(xt, ND, TL, D, 0, re.ready), None)
        r = Rms(xt, ND, TL, D, 0, re.ready)
        Store(r)
        SEEDS = [(cnt.sems[n], v) for n, v in (("hid_lo_ready", 2), ("conv_tap", 4), ("conv_out", 2), ("ffn_tap", 6), ("ffn_gated", 1)) if n in cnt.sems]

        block = ctx.enter_context(nc.Block())

        @block.sync
        def _(sp):
            for ph in phases[:STOP]:
                ph.sp(sp)

        @block.gpsimd
        def _(pool):
            for ph in phases[:STOP]:
                ph.pool(pool)

        @block.scalar
        def _(act):
            for ph in phases[:STOP]:
                ph.act(act)

        @block.vector
        def _(dve):
            for ph in phases[:STOP]:
                ph.dve(dve)

        @block.tensor
        def _(pe):
            for ph in phases[:STOP]:
                ph.pe(pe)


def tables():
    c = np.zeros((P, NCST), np.float32)

    def put(name, v):
        a, w = CST[name]
        c[:v.shape[0], a:a + w] = v.reshape(v.shape[0], w)

    put("ident", np.eye(P))
    t = np.arange(TL)
    inv = 10000.0 ** (-np.arange(32, dtype=np.float32) / np.float32(32))
    pos = [(t // 64).astype(np.float32), (t % 64).astype(np.float32)]
    ang = [p[None, :] * inv.astype(np.float32)[:, None] for p in pos]
    put("cos1", np.concatenate([np.cos(ang[0])] * 2 + [np.cos(ang[1])] * 2))
    put("sin1", np.concatenate([np.sin(ang[0])] * 2 + [np.sin(ang[1])] * 2))
    inv2 = np.power(np.float32(500000.0), -np.arange(0, 32, 2, dtype=np.float32) / np.float32(32))
    a2 = t.astype(np.float32)[None, :] * inv2[:, None]
    put("cos2", np.concatenate([np.cos(a2), np.cos(a2), np.ones((96, TL))]))
    put("sin2", np.concatenate([np.sin(a2), np.sin(a2), np.zeros((96, TL))]))
    for name, halves in (("rot1", [(0, 32), (64, 32)]), ("rot2", [(0, 16)])):
        r = np.zeros((P, P))
        for a, h in halves:
            for i in range(h):
                r[a + h + i, a + i] = -1.0
                r[a + i, a + h + i] = 1.0
        put(name, r)
    m = np.zeros((P, 2, 6, P))
    s_, t_ = np.arange(P)[:, None], np.arange(P)[None, :]
    for back in range(2):
        for l, half in enumerate(LEVELS):
            pair = (s_ // (2 * half) == t_ // (2 * half)) & (s_ // half != t_ // half) & ((s_ > t_) if back else (s_ < t_))
            m[:, back, 0 if l < 2 else l - 1] += pair
        m[:, back, 0] += s_ == t_
    put("hg_mask", m)
    q_, k_ = np.arange(P)[:, None], np.arange(P)[None, :]
    put("band", np.concatenate([np.where(k_ >= q_, 0, NEG), np.where(k_ <= q_, 0, NEG)], 1))
    for name, d in (("dil4", 4), ("dil16", 16)):
        same = (q_ - k_) % d == 0
        put(name, np.concatenate([np.where(same, 0, NEG)] * 3 + [np.where(same & (k_ <= q_), 0, NEG)], 1))
    put("ssd_mask", np.where(s_ <= t_, 0, NEG))
    pi = np.zeros((4, TA))
    for g in range(4):
        w = 2 << g
        for a, n in ((0, TC), (TC, TL)):
            tt = np.arange(n)
            pi[g, a:a + n] = 1.0 / (np.clip(tt - w // 2 + w, 0, n) - np.clip(tt - w // 2, 0, n))
    put("pool_inv", np.broadcast_to(pi.reshape(1, -1), (P, 4 * TA)))
    return c


def kernel(**inp):
    import concourse.bacc as bacc
    from concourse.bass_utils import run_bass_kernel_spmd as run

    inp = {k: np.asarray(v) for k, v in inp.items()}

    def chunks(w, kt, order=None):
        k, f = w.shape
        v = w.reshape(k // (kt * P), kt, P, f // P, P).transpose(3, 0, 2, 1, 4)
        if order is not None:
            v = v[order]
        return np.ascontiguousarray(v.reshape(-1, P, kt, P))

    def cols(v):
        return np.ascontiguousarray(v.reshape(-1, P).T)

    def pairs(n):
        return np.arange(2 * n).reshape(2, n).T.reshape(-1)

    vecs = np.zeros((P, NVEC), np.float32)

    def put(name, v):
        a, w = VEC[name]
        vecs[:v.shape[0], a:a + w] = v

    put("ada_b", cols(inp["ada_b"]))
    put("norm_g", cols(inp["norm_g"]))
    put("pool_scale", cols(inp["pool_scale"]))
    put("hg_lower", cols(inp["hg_lower"]))
    put("onorm", cols(inp["hg_onorm_g"]))
    put("qn", cols(inp["att_qnorm_g"]))
    put("kn", cols(inp["att_knorm_g"]))
    put("a_norm", cols(inp["a_norm_2"]))
    put("conv_w", cols(inp["ssm_conv_w_2"]))
    put("conv_b", cols(inp["ssm_conv_b_2"]))
    put("ssm_norm", cols(inp["ssm_norm_2"]))
    put("d_skip", cols(np.repeat(inp["ssm_d_2"].reshape(-1), 64)))
    put("kv_norm", cols(inp["kv_norm_2"]))
    put("b_norm", cols(inp["b_norm_2"]))
    put("ffn_norm", cols(inp["ffn_norm_2"]))
    fc = inp["ffn_conv_w_2"].reshape(2, 3, 2 * NH, P)[:, :, pairs(NH)]
    put("ffn_conv", cols(fc))
    put("final_norm", cols(inp["final_norm_2"]))
    put("dt_bias", inp["ssm_dt_bias_2"].reshape(NSH, 1))
    put("a_log", inp["ssm_a_log_2"].reshape(NSH, 1))

    head_order = [0, 1, 2, 3, 20, 21, 22, 23] + [4 + 4 * part + h for h in range(4) for part in range(4)]
    ssm = inp["ssm_w_in_2"][0]
    arrays = {
        "xT": np.ascontiguousarray(inp["x"][0].T), "ctxT": np.ascontiguousarray(inp["ctx"][0].T),
        "cvec": np.stack([inp["c"].reshape(-1), inp["c_ctx"].reshape(-1)]), "vecs": vecs, "cst": tables(),
        "ada0": np.ascontiguousarray(inp["ada_w"][0].T.reshape(48, P, D)), "ada1": np.ascontiguousarray(inp["ada_w"][1].T.reshape(48, P, D)),
        "w_ab_in": chunks(inp["ab_w_in"][0], 8, head_order), "w_ab_out": chunks(inp["ab_w_out"][0], 8),
        "w_pool": np.ascontiguousarray(inp["pool_w"][0].transpose(1, 0, 2)),
        "w_f0u": chunks(inp["ffn_w_in"][0], 8, pairs(NH)), "w_f0d": chunks(inp["ffn_w_out"][0], KC),
        "w_att_in": chunks(inp["att_w_in"][0], 8), "w_att_out": chunks(inp["att_w_out"][0], 8),
        "w_f1u": chunks(inp["ffn_w_in"][1], 8, pairs(NH)), "w_f1d": chunks(inp["ffn_w_out"][1], KC),
        "w_ssm": chunks(ssm[:, :6144], 8), "w_dt": np.ascontiguousarray(ssm[:, 6144:].reshape(ND, P, NSH).transpose(1, 0, 2)),
        "w_ssm_out": chunks(inp["ssm_w_out_2"][0], 8), "w_kv": chunks(inp["w_kv_2"], 8), "w_q": chunks(inp["att_w_q_2"][0], 8),
        "w_o": chunks(inp["att_w_o_2"][0], 8),
        "w_f2u": chunks(inp["ffn_w_up_2"][0], 8, pairs(NH)), "w_f2d": chunks(inp["ffn_w_down_2"][0], KC),
        "w_f3u": chunks(inp["ffn_w_up_2"][1], 8, pairs(NH)), "w_f3d": chunks(inp["ffn_w_down_2"][1], KC),
    }
    nc = bacc.Bacc("TRN2", target_bir_lowering=False, num_devices=1)
    args = [nc.dram_tensor(n, a.shape, mybir.dt.from_np(a.dtype), kind="ExternalInput").ap() for n, a in arrays.items()]
    out = nc.dram_tensor("out", (D, TL), mybir.dt.float32, kind="ExternalOutput").ap()
    build(nc, *args, out)
    r = run(nc, [arrays], core_ids=[0])
    return np.ascontiguousarray(r.results[0]["out"].T).reshape(1, TL, D)
```

```python
import numpy as np
import concourse.bass as bass
from concourse import mybir
from contextlib import ExitStack

P = 128
D = 1024
ND = D // P
TL, TC = 512, 256
TA = TL + TC
HID = 2816
NH = HID // P
EPS = 1e-6
GEPS = 1e-5
RAW, SPL = 4, 2
KC = 11
NBANK = 4
CH = 128
NCH = TA // CH
HEADS = 4
LEVELS = (64, 32, 16, 8, 4, 2, 1)
DI = 2048
NG = 8
NSH = 32
SCALE = float(P) ** -0.5
NEG = -1e30

VEC = {}
_n = 0
for _name, _w in (("ada_b", 96), ("norm_g", 64), ("pool_scale", 4), ("hg_lower", 16), ("onorm", 1), ("qn", 1), ("kn", 1),
                  ("a_norm", 8), ("conv_w", 128), ("conv_b", 32), ("ssm_norm", 16), ("d_skip", 16), ("kv_norm", 8),
                  ("b_norm", 8), ("ffn_norm", 16), ("ffn_conv", 264), ("final_norm", 8), ("dt_bias", 1), ("a_log", 1)):
    VEC[_name] = (_n, _w)
    _n += _w
NVEC = _n

CST = {}
_n = 0
for _name, _w in (("ident", 128), ("rot1", 128), ("rot2", 128), ("cos1", TL), ("sin1", TL), ("cos2", TL), ("sin2", TL),
                  ("hg_mask", 2 * 6 * 128), ("band", 256), ("dil4", 512), ("dil16", 512), ("pool_inv", 4 * TA), ("ssd_mask", 128)):
    CST[_name] = (_n, _w)
    _n += _w
NCST = _n


STOP = None


def upto(taken, n, seed=0):
    return taken[0], taken[1] + n + seed


class Counts:

    def __init__(self, make):
        self.make, self.sems, self.at = make, {}, {}

    def take(self, name, n):
        if name not in self.sems:
            self.sems[name], self.at[name] = self.make(name), 0
        base = self.at[name]
        self.at[name] += n
        return self.sems[name], base


def build(nc, xT, ctxT, cvec, vecs, cst, ada0, ada1, w_ab_in, w_ab_out, w_pool, w_f0u, w_f0d, w_att_in, w_att_out,
          w_f1u, w_f1d, w_ssm, w_dt, w_ssm_out, w_kv, w_q, w_o, w_f2u, w_f2d, w_f3u, w_f3d, out):
    f32, f32r = mybir.dt.float32, mybir.dt.float32r
    ALU, ACT, AX = mybir.AluOpType, mybir.ActivationFunctionType, mybir.AxisListType
    ctx = ExitStack()
    with ctx:
        base = (nc.sbuf_base + 31) // 32 * 32
        end = nc.sbuf_usable_end
        made = {}

        def at(name, shape, off, dt=f32):
            n = 4
            for s in shape[1:]:
                n *= s
            assert base + off + n <= end, (name, base + off + n - end)
            made[name] = (off, off + n)
            return nc.alloc_sbuf_tensor_at(name, shape, dt, offset=base + off)

        K = 1024
        o = 0

        def seq(name, shape, dt=f32):
            nonlocal o
            t = at(name, shape, o, dt)
            o = (made[name][1] + 31) // 32 * 32
            return t

        w_raw = [seq(f"w_raw{i}", [P, KC, P]) for i in range(RAW)]
        w_hi = [seq(f"w_hi{i}", [P, KC, P], f32r) for i in range(SPL)]
        w_lo = [seq(f"w_lo{i}", [P, KC, P], f32r) for i in range(SPL)]
        x = seq("x", [P, ND, TL])
        vec = seq("vec", [P, NVEC])
        ones = seq("ones", [P, P])
        ident = seq("ident", [P, P])
        ssd_mask = seq("ssd_mask", [P, P])
        mods = [seq(f"mods{l}", [P, 2, 48]) for l in range(2)]
        gains = [seq(f"gains{l}", [P, 2, 4, ND]) for l in range(2)]
        epsv = seq("epsv", [P, 4])
        small = seq("small", [P, 64])
        rstd = seq("rstd", [P, TL])
        o_xc = o
        xc = seq("xc", [P, ND, TC])
        A0 = o
        ps = [ctx.enter_context(nc.psum_tensor(f"ps{i}", [P, 512], f32)) for i in range(8)]

        def V(name, i=0, n=1):
            a, w = VEC[name]
            return vec[:, a + i:a + i + n]

        def C(name):
            a, w = CST[name]
            return cst[:, a:a + w]

        def arena(name, shape, off, dt=f32):
            return at(name, shape, A0 + off, dt)

        h_hi = arena("h_hi", [P, ND, TL], 0, f32r)
        h_lo = arena("h_lo", [P, ND, TL], 16 * K, f32r)
        y = arena("y", [P, ND, TL], 0)
        hid_hi = arena("hid_hi", [P, NH, TL], 32 * K, f32r)
        hid_lo = arena("hid_lo", [P, NH, TL], 76 * K, f32r)
        hidc_hi = arena("hidc_hi", [P, NH, TC], 32 * K, f32r)
        hidc_lo = arena("hidc_lo", [P, NH, TC], 54 * K, f32r)
        wk = [arena(f"wk{i}", [P, TL], 120 * K + 2 * K * i) for i in range(4)]
        pad = [at(f"pad{i}", [P, TL + 4], o_xc + 2080 * i) for i in range(2)]
        c_hi = arena("c_hi", [P, ND, TC], 32 * K, f32r)
        c_lo = arena("c_lo", [P, ND, TC], 40 * K, f32r)

        cnt = Counts(lambda n: ctx.enter_context(nc.semaphore(n)))
        raw_ready = [cnt.take(f"raw_ready{i}", 0)[0] for i in range(RAW)]
        split_done = cnt.take("split_done", 0)[0]
        hi_done = cnt.take("hi_done", 0)[0]
        chunk_done = cnt.take("chunk_done", 0)[0]
        mm_free = cnt.take("mm_free", 0)[0]
        const_in = cnt.take("const_in", 0)[0]
        phase_in = cnt.take("phase_in", 0)[0]
        waited = cnt.take("waited", 0)[0]
        act_step = cnt.take("act_step", 0)[0]
        dve_step = cnt.take("dve_step", 0)[0]
        steps = {"act": 0, "dve": 0}

        def astep(ins):
            steps["act"] += 1
            ins.then_inc(act_step, 1)
            nc.scalar.wait_ge(act_step, steps["act"])

        def vstep(ins):
            steps["dve"] += 1
            ins.then_inc(dve_step, 1)
            nc.vector.wait_ge(dve_step, steps["dve"])

        sent = {}

        def sig(eng, ins, taken, n=1):
            sent[taken] = sent.get(taken, 0) + n
            ins.then_inc(taken[0], n)
            eng.wait_ge(*upto(taken, sent[taken]))

        progress = {"chunk": 0, "tile": 0, "phase_in": 0}
        phases = []

        class Phase:
            def __init__(self):
                phases.append(self)

            def sp(self, sp): pass
            def pool(self, pool): pass
            def act(self, act): pass
            def dve(self, dve): pass
            def pe(self, pe): pass

        def loaded(n_dmas):
            progress["phase_in"] += n_dmas
            return 16 * progress["phase_in"]

        class Gemm(Phase):

            def __init__(self, w, tiles, parts, kt, rhs, t=TL, ctx_rhs=None, ctx_from=0, evac_act=None, evac_dve=None,
                         peel=(), gate=None, gate_k=None, rows=None):
                super().__init__()
                self.w, self.tiles, self.parts, self.kt, self.rhs, self.t = w, tiles, parts, kt, rhs, t
                self.ctx_rhs, self.ctx_from = ctx_rhs, ctx_from
                self.evac_act, self.evac_dve, self.gate, self.gate_k, self.rows = evac_act, evac_dve, gate, gate_k, rows
                self.chunk0, self.tile0 = progress["chunk"], progress["tile"]
                progress["chunk"] += tiles * parts
                progress["tile"] += tiles
                self.per = RAW // parts
                self.turns = tiles // self.per
                self.peel = tuple(peel)
                self.pe_peel = (1,) + tuple(b for b in peel if b > 1) if gate_k else self.peel
                assert (tiles * parts) % RAW == 0 and self.tile0 % NBANK in (0, 2)

            def loops(self, eng, body, peel=None):
                bounds = [0, *(self.peel if peel is None else peel), self.turns]
                for a, b in zip(bounds, bounds[1:]):
                    if b - a == 1:
                        body(a, a)
                    else:
                        with eng.Fori(a, b) as i:
                            body(i, a)

            def sp(self, sp):
                def turn(i, a):
                    for j in range(RAW):
                        sp.wait_ge(split_done, self.chunk0 + RAW * i + j + 1)
                        src = self.w[bass.ds(RAW * i + j, 1)].rearrange("o p k f -> (o p) k f")
                        sp.dma_start(w_raw[j][:, 0:self.kt], src).then_inc(raw_ready[j], 16)
                        if self.rows:
                            self.rows.sp(sp, i, a, j)
                self.loops(sp, turn)

            def pool(self, pool):
                def turn(i, a):
                    for j in range(RAW):
                        s = j % SPL
                        c = self.chunk0 // RAW
                        pool.wait_ge(raw_ready[j], 16 * (c + i + 1))
                        pool.wait_ge(chunk_done, self.chunk0 + RAW * i + j + 1)
                        pool.sem_inc(waited, 1)
                        nc.gpsimd.tensor_scalar(w_hi[s][:, 0:self.kt], w_raw[j][:, 0:self.kt], 1.0, 1.0, ALU.mult, ALU.mult).then_inc(hi_done, 1)
                        pool.wait_ge(hi_done, self.chunk0 + RAW * i + j + 1)
                        nc.gpsimd.tensor_tensor(w_lo[s][:, 0:self.kt], w_raw[j][:, 0:self.kt],
                                                w_hi[s][:, 0:self.kt].bitcast(f32), ALU.subtract).then_inc(split_done, 1)
                self.loops(pool, turn)

            def pe(self, pe):
                pe.wait_ge(mm_free, self.tile0 + NBANK)
                if self.gate:
                    pe.wait_ge(*self.gate)

                def turn(i, a):
                    for n in range(self.per):
                        bank = self.bank(n)
                        pe.wait_ge(mm_free, self.tile0 + self.per * i + n + 1 + NBANK - self.per)
                        both = self.ctx_rhs is not None and self.per * a + n >= self.ctx_from
                        for part in range(self.parts):
                            j = n * self.parts + part
                            s = j % SPL
                            pe.wait_ge(split_done, RAW + self.chunk0 + RAW * i + j + 1)
                            for rhs, dst in ((self.rhs, ps[bank][:, 0:self.t]),) + (
                                    ((self.ctx_rhs, self.ctx_out(n)),) if both else ()):
                                for k in range(self.kt):
                                    kk = part * self.kt + k
                                    hi, lo = rhs(kk)
                                    if self.gate_k and isinstance(i, int) and n == 0 and rhs is self.rhs:
                                        pe.wait_ge(*self.gate_k(kk))
                                    nc.tensor.matmul(dst, w_hi[s][:, k], hi, start=kk == 0, stop=False)
                                    nc.tensor.matmul(dst, w_hi[s][:, k], lo, start=False, stop=False)
                                    last = nc.tensor.matmul(dst, w_lo[s][:, k], hi, start=False,
                                                            stop=kk == self.parts * self.kt - 1)
                            last.then_inc(chunk_done, 1)
                self.loops(pe, turn, self.pe_peel)

            def act(self, act):
                if self.evac_act:
                    self.loops(act, lambda i, a: self.evac_act(self, act, i, a))

            def dve(self, dve):
                if self.evac_dve:
                    self.loops(dve, lambda i, a: self.evac_dve(self, dve, i, a))
                elif self.rows:
                    self.loops(dve, lambda i, a: self.rows.dve(dve, i, a))

            def tile(self, i, n):
                return SPL + self.chunk0 + RAW * i + (n + 1) * self.parts

            def bank(self, n):
                return n % NBANK if self.per == NBANK else n % 2

            def out(self, n):
                return ps[self.bank(n)][:, 0:self.t]

            def ctx_out(self, n):
                return ps[4 + n][:, 0:TC]

            @property
            def all_read(self):
                return (mm_free, NBANK + self.tile0 + self.tiles)

        class Rms(Phase):

            def __init__(self, src, nt, t, count, eps, gate, dst=None, bufs=None):
                super().__init__()
                self.src, self.nt, self.t, self.count, self.eps, self.gate = src, nt, t, count, eps, gate
                self.dst = rstd if dst is None else dst
                self.bufs = wk[2:4] if bufs is None else bufs
                self.sq_ready, self.sq_summed = cnt.take("sq_ready", nt), cnt.take("sq_summed", nt)
                self.rstd_ready = cnt.take("rstd_ready", 1)
                self.done = (self.rstd_ready[0], self.rstd_ready[1] + 1)

            def act(self, act):
                s, b = self.sq_summed
                for k in range(self.nt):
                    act.wait_ge(*self.gate(k))
                    if k >= 2:
                        act.wait_ge(s, b + k - 1)
                    sig(nc.scalar, nc.scalar.activation(self.bufs[k % 2][:, 0:self.t], self.src(k), ACT.Square), self.sq_ready)
                act.wait_ge(s, b + self.nt)
                astep(nc.scalar.activation(self.dst[:, 0:self.t], ps[6][:, 0:self.t], ACT.Ln, scale=1.0 / self.count,
                                           bias=epsv[:, self.eps:self.eps + 1]))
                sig(nc.scalar, nc.scalar.activation(self.dst[:, 0:self.t], self.dst[:, 0:self.t], ACT.Exp, scale=-0.5), self.rstd_ready)

            def pe(self, pe):
                for k in range(self.nt):
                    pe.wait_ge(self.sq_ready[0], self.sq_ready[1] + k + 1)
                    nc.tensor.matmul(ps[6][:, 0:self.t], ones[:], self.bufs[k % 2][:, 0:self.t], start=k == 0,
                                     stop=k == self.nt - 1).then_inc(self.sq_summed[0], 1)

        class Apply(Phase):

            def __init__(self, src, nt, t, gain, shift, hi, lo, rms, gate=None):
                super().__init__()
                self.src, self.nt, self.t, self.gain, self.shift, self.hi, self.lo = src, nt, t, gain, shift, hi, lo
                self.rms, self.gate = rms, gate
                self.scaled, self.hi_ready, self.lo_ready = cnt.take("scaled", nt), cnt.take("h_hi_ready", nt), cnt.take("h_lo_ready", nt)
                self.done = (self.lo_ready[0], self.lo_ready[1] + nt)

            def tile_ready(self, k):
                return (self.lo_ready[0], self.lo_ready[1] + k + 1)

            def dve(self, dve):
                dve.wait_ge(*self.rms.done)
                if self.gate:
                    dve.wait_ge(*self.gate)
                for k in range(self.nt + 1):
                    if k < self.nt:
                        sig(nc.vector, nc.vector.scalar_tensor_tensor(wk[k % 2][:, 0:self.t], self.src(k), self.gain(k), rstd[:, 0:self.t],
                                                       ALU.mult, ALU.mult), self.scaled)
                    if k >= 1:
                        q = k - 1
                        dve.wait_ge(self.hi_ready[0], self.hi_ready[1] + q + 1)
                        src, hi = wk[q % 2][:, 0:self.t], self.hi(q).bitcast(f32)
                        if self.shift:
                            ins = nc.vector.scalar_tensor_tensor(self.lo(q), src, self.shift(q), hi, ALU.add, ALU.subtract)
                        else:
                            ins = nc.vector.tensor_tensor(self.lo(q), src, hi, ALU.subtract)
                        sig(nc.vector, ins, self.lo_ready)

            def act(self, act):
                for k in range(self.nt):
                    act.wait_ge(self.scaled[0], self.scaled[1] + k + 1)
                    bias = self.shift(k) if self.shift else 0.0
                    sig(nc.scalar, nc.scalar.activation(self.hi(k), wk[k % 2][:, 0:self.t], ACT.Identity, bias=bias), self.hi_ready)

        class Residual(Phase):

            def __init__(self, xt, yt, nt, t, gain, rms, gate=None):
                super().__init__()
                self.x, self.y, self.nt, self.t, self.gain, self.rms, self.gate = xt, yt, nt, t, gain, rms, gate
                self.scaled, self.added = cnt.take("y_scaled", nt), cnt.take("x_added", nt)

            def ready(self, k):
                return (self.added[0], self.added[1] + k + 1)

            def dve(self, dve):
                dve.wait_ge(*(self.rms.done if self.rms else self.gate))
                if not self.rms:
                    for k in range(self.nt):
                        sig(nc.vector, nc.vector.tensor_tensor(self.x(k), self.x(k), self.y(k), ALU.add), self.added)
                    return
                for k in range(self.nt + 1):
                    if k < self.nt:
                        sig(nc.vector, nc.vector.scalar_tensor_tensor(wk[k % 2][:, 0:self.t], self.y(k), self.gain(k), rstd[:, 0:self.t],
                                                       ALU.mult, ALU.mult), self.scaled)
                    if k >= 1:
                        dve.wait_ge(self.scaled[0], self.scaled[1] + k)
                        sig(nc.vector, nc.vector.tensor_tensor(self.x(k - 1), self.x(k - 1), wk[(k - 1) % 2][:, 0:self.t],
                                                ALU.add), self.added)

        ada_used = cnt.take("ada_used", 0)[0]
        ada_in = [cnt.take(f"ada_in{i}", 0)[0] for i in range(2)]

        class AdaBufs:

            def __init__(self, name, off):
                self.raw = [arena(f"{name}_raw{i}", [P, D], off + 4 * K * i) for i in range(2)]
                self.c = arena(f"{name}_c", [P, 2, D], off + 8 * K)
                self.junk = [arena(f"{name}_junk{i}", [P, D], off + (16 + 4 * i) * K) for i in range(2)]

        class AdaC(Phase):

            def __init__(self, bufs, gate):
                super().__init__()
                self.bufs, self.gate = bufs, gate
                self.c_in, self.c_ready = cnt.take("c_in", 32), cnt.take("c_ready", 1)

            def sp(self, sp):
                if self.gate:
                    sp.wait_ge(*self.gate)
                for v in range(2):
                    sp.dma_start(self.bufs.c[:, v], cvec[v:v + 1, :].to_broadcast([P, D])).then_inc(self.c_in[0], 16)

            def act(self, act):
                act.wait_ge(*upto(self.c_in, 32))
                sig(nc.scalar, nc.scalar.activation(self.bufs.c[:, :], self.bufs.c[:, :], ACT.Silu), self.c_ready)

            def dve(self, dve):
                dve.wait_ge(*upto(self.c_ready, 1))

        class AdaRows:

            def __init__(self, w, layer, bufs):
                self.w, self.layer, self.bufs, self.m0 = w, layer, bufs, 48 * layer

            def load(self, sp, n, j):
                sp.wait_ge(ada_used, 2 * (self.m0 + n) + 2)
                sp.dma_start(self.bufs.raw[j][:], self.w[bass.ds(n, 1)].rearrange("o p k -> (o p) k")).then_inc(ada_in[j], 16)

            def chunk(self, dve, n, pairs, j):
                dve.wait_ge(ada_in[j], 16 * (pairs + 1))
                for v in range(2):
                    dve.wait_ge(ada_used, 4 + 2 * (self.m0 + n) + v - 1)
                    nc.vector.scalar_tensor_tensor(self.bufs.junk[v][:], self.bufs.raw[j][:], 1.0, self.bufs.c[:, v], ALU.mult, ALU.mult,
                                                   accum_out=mods[self.layer][:, v, bass.ds(n, 1)]).then_inc(ada_used, 1)

        class AdaTurns:

            def __init__(self, rows, first, per, until):
                self.rows, self.first, self.per, self.until = rows, first, per, until

            def sp(self, sp, i, a, j):
                if a < self.until:
                    for q in range(j * self.per // RAW, (j + 1) * self.per // RAW):
                        self.rows.load(sp, self.first + self.per * i + q, q % 2)

            def dve(self, dve, i, a, part=0, parts=1):
                if a < self.until:
                    for q in range(part * self.per // parts, (part + 1) * self.per // parts):
                        self.rows.chunk(dve, self.first + self.per * i + q, (self.rows.m0 + self.first) // 2 + (self.per // 2) * i + q // 2, q % 2)

        class AdaFirst(Phase):

            def __init__(self, rows, n):
                super().__init__()
                self.rows, self.n = rows, n

            def sp(self, sp):
                with sp.Fori(0, self.n // 2) as i:
                    for j in range(2):
                        self.rows.load(sp, 2 * i + j, j)

            def dve(self, dve):
                with dve.Fori(0, self.n // 2) as i:
                    for j in range(2):
                        self.rows.chunk(dve, 2 * i + j, self.rows.m0 // 2 + i, j)

        class AdaEnd(Phase):

            def __init__(self, rows, a, b, gates):
                super().__init__()
                self.rows, self.a, self.b, self.gates = rows, a, b, gates
                self.ready = cnt.take("mods_ready", 1)
                self.done = upto(self.ready, 1)

            def dve(self, dve):
                l, a, b = self.rows.layer, self.a, self.b
                dve.wait_ge(ada_used, 4 + 2 * (self.rows.m0 + b))
                for v in range(2):
                    vstep(nc.vector.tensor_tensor(mods[l][:, v, a:b], mods[l][:, v, a:b], V("ada_b", 48 * l + a, b - a), ALU.add))
                for v in range(2):
                    for q in self.gates:
                        m = (8, 16, 32, 40)[q]
                        ng = V("norm_g", 32 * l + 8 * q, 8)
                        if q % 2 == 0:
                            last = nc.vector.scalar_tensor_tensor(gains[l][:, v, q], mods[l][:, v, m:m + 8], 1.0, ng, ALU.add, ALU.mult)
                        else:
                            last = nc.vector.tensor_tensor(gains[l][:, v, q], mods[l][:, v, m:m + 8], ng, ALU.mult)
                sig(nc.vector, last, self.ready)

        z = arena("z", [P, 24, TA], 48 * K)
        LAT, CTX = slice(TC, TA), slice(0, TC)

        def z_evac_act(g, act, i, a):
            funcs = {0: [ACT.Copy] * 4, 1: [ACT.Silu] * 4}.get(a, [ACT.Silu, ACT.Sigmoid, ACT.Sigmoid, ACT.Copy])
            if a == 4:
                act.wait_ge(ada_used, 4 + 2 * 48)
            for n in range(4):
                act.wait_ge(chunk_done, g.tile(i, n))
                dst = z[:, bass.ds(4 * i + n, 1)].rearrange("p o t -> p (o t)")
                nc.scalar.activation(dst[:, LAT], g.out(n), funcs[n])
                nc.scalar.activation(dst[:, CTX], g.ctx_out(n), funcs[n]).then_inc(mm_free, 1)

        m_lev = [arena(f"m_lev{i}", [P, TA], 3 * K * i) for i in range(7)]
        hk, hb, hdq, hdk = (arena(n, [P, TA], (21 + 3 * i) * K) for i, n in enumerate(("hk", "hb", "hdq", "hdk")))
        v_tok = arena("v_tok", [P, NCH, P], 33 * K)
        k_tok = arena("k_tok", [P, NCH, P], 36 * K)
        he = [arena(f"he{i}", [P, TA], (39 + 3 * i) * K) for i in range(2)]
        ho = arena("ho", [P, TA], 45 * K)
        hmask = arena("hmask", [P, 2, 6, P], 120 * K)
        a_tmp = arena("a_tmp", [P, 6, P], 126 * K)
        a_sum = [arena(f"a_sum{i}", [P, P], 129 * K + 512 * i) for i in range(2)]
        h_st = [arena(f"h_st{i}", [P, P], 130 * K + 512 * i) for i in range(2)]
        h_el = small[:, 0:NCH]
        lbv, omlv = small[:, 8:16], small[:, 16:24]
        mix_hi = [arena(f"mix_hi{k}", [P, TA], (48 + 3 * (k if k < 4 else 8 + 4 * (k - 4))) * K, f32r) for k in range(8)]
        mix_lo = [arena(f"mix_lo{k}", [P, TA], (48 + 3 * (4 + k if k < 4 else 9 + 4 * (k - 4))) * K, f32r) for k in range(8)]

        class HgPrep(Phase):

            def __init__(self, gate):
                super().__init__()
                self.gate, self.val = gate, loaded(1)
                self.diff, self.lb = cnt.take("lb_diff", 1), cnt.take("lb_ready", 1)

            def sp(self, sp):
                sp.wait_ge(*self.gate)
                a, w = CST["hg_mask"]
                sp.dma_start(hmask[:, :, :, :].rearrange("p d l t -> p (d l t)"), cst[:, a:a + w]).then_inc(phase_in, 16)

            def dve(self, dve):
                sig(nc.vector, nc.vector.tensor_tensor(small[:, 24:32], V("hg_lower", 0, 8), V("hg_lower", 8, 8), ALU.subtract), self.diff)
                dve.wait_ge(self.lb[0], self.lb[1] + 1)
                vstep(nc.vector.tensor_scalar(omlv, lbv, -1.0, 1.0, ALU.mult, ALU.add))

            def act(self, act):
                act.wait_ge(self.diff[0], self.diff[1] + 1)
                sig(nc.scalar, nc.scalar.activation(lbv, small[:, 24:32], ACT.Sigmoid), self.lb)

        class HgUnit(Phase):

            def __init__(self, head, back, masks, gate):
                super().__init__()
                self.head, self.back, self.masks, self.gate = head, back, masks, gate
                self.order = [1, 0, 5, 4, 3, 2] if back else list(range(NCH))
                self.f_ready, self.lf_ready, self.k_ready = cnt.take("f_ready", 1), cnt.take("lf_ready", 1), cnt.take("k_ready", 1)
                self.b_ready, self.arg_ready, self.exp_ready = cnt.take("b_ready", 1), cnt.take("arg_ready", 7), cnt.take("exp_ready", 7)
                self.level_ready, self.dq_exp, self.dk_arg = cnt.take("level_ready", 7), cnt.take("dq_exp", 1), cnt.take("dk_arg", 1)
                self.dk_exp, self.dq_ready, self.dk_ready = cnt.take("dk_exp", 1), cnt.take("dq_ready", 1), cnt.take("dk_ready", 1)
                self.tok_in_ps, self.tok_read, self.scores_in_ps = cnt.take("tok_in_ps", 4), cnt.take("tok_read", 4), cnt.take("scores_in_ps", 6)
                self.masked, self.o_in_ps, self.state_ready = cnt.take("masked", 6), cnt.take("o_in_ps", 6), cnt.take("state_ready", 7)

            def dve(self, dve):
                h, back = self.head, self.back
                s = z[:, 9 + 4 * h + back]
                d = 4 * back + h
                q = z[:, 8 + 4 * h]
                if self.gate:
                    dve.wait_ge(*self.gate)
                if h == 0 and not back:
                    dve.wait_ge(phase_in, self.masks)
                sig(nc.vector, nc.vector.tensor_scalar(s, s, omlv[:, d:d + 1], lbv[:, d:d + 1], ALU.mult, ALU.add), self.f_ready)
                dve.wait_ge(*upto(self.f_ready, 1))
                sig(nc.vector, nc.vector.tensor_scalar(hk[:], s, -1.0, 1.0, ALU.mult, ALU.add), self.k_ready)
                dve.wait_ge(*upto(self.lf_ready, 1))
                lf = s.rearrange("p (c t) -> p c t", c=NCH)
                b = hb[:, :].rearrange("p (c t) -> p c t", c=NCH)
                for c in range(NCH):
                    src, dst = (lf[:, c, ::-1], b[:, c, ::-1]) if back else (lf[:, c], b[:, c])
                    last = nc.vector.tensor_tensor_scan(dst, ones[:], src, 0.0, ALU.mult, ALU.add)
                sig(nc.vector, last, self.b_ready)
                dve.wait_ge(*upto(self.b_ready, 1))
                end = b[:, :, 0:1] if back else b[:, :, CH - 1:CH]
                sig(nc.vector, nc.vector.tensor_tensor(hdk[:, :].rearrange("p (c t) -> p c t", c=NCH), end.to_broadcast([P, NCH, CH]), b,
                                        ALU.subtract), self.dk_arg)
                qs, ks = (0, 1) if back else (1, 0)
                for l in range(8):
                    if l < 7:
                        half = LEVELS[l]
                        v, w = (a.rearrange("p (n s t) -> p n s t", s=2, t=half) for a in (hb[:, :], he[l % 2][:, :]))
                        n = TA // (2 * half)
                        ref = (v[:, :, 1, 0:1] if back else v[:, :, 0, half - 1:half]).to_broadcast([P, n, half])
                        if l >= 2:
                            dve.wait_ge(*upto(self.level_ready, l - 1))
                        vstep(nc.vector.tensor_tensor(w[:, :, qs], v[:, :, qs], ref, ALU.subtract))
                        sig(nc.vector, nc.vector.tensor_tensor(w[:, :, ks], ref, v[:, :, ks], ALU.subtract), self.arg_ready)
                    if l >= 1:
                        m, half = l - 1, LEVELS[l - 1]
                        e, w, qq, kk = (a.rearrange("p (n s t) -> p n s t", s=2, t=half) for a in (he[m % 2][:, :], m_lev[m][:, :], q, hk[:, :]))
                        dve.wait_ge(*upto(self.exp_ready, m + 1))
                        vstep(nc.vector.tensor_tensor(w[:, :, qs], e[:, :, qs], qq[:, :, qs], ALU.mult))
                        sig(nc.vector, nc.vector.tensor_tensor(w[:, :, ks], e[:, :, ks], kk[:, :, ks], ALU.mult), self.level_ready)
                dve.wait_ge(*upto(self.dq_exp, 1))
                sig(nc.vector, nc.vector.tensor_tensor(hdq[:], hdq[:], q, ALU.mult), self.dq_ready)
                dve.wait_ge(*upto(self.dk_exp, 1))
                sig(nc.vector, nc.vector.tensor_tensor(hdk[:], hdk[:], hk[:], ALU.mult), self.dk_ready)
                sig(nc.vector, nc.vector.memset(h_st[0][:], 0.0), self.state_ready)
                for i, c in enumerate(self.order):
                    bx, by, bo = ps[2 * (i % 2)], ps[2 * (i % 2) + 1], ps[4 + i % 2]
                    dve.wait_ge(*upto(self.scores_in_ps, i + 1))
                    vstep(nc.vector.tensor_tensor(a_tmp[:, 0:4], bx[:, :].rearrange("p (l t) -> p l t", l=4), hmask[:, back, 0:4], ALU.mult))
                    vstep(nc.vector.tensor_tensor(a_tmp[:, 4:6], by[:, 0:256].rearrange("p (l t) -> p l t", l=2), hmask[:, back, 4:6], ALU.mult))
                    sig(nc.vector, nc.vector.tensor_reduce(a_sum[i % 2][:], a_tmp[:, :, :].rearrange("p l t -> p t l"), AX.X, ALU.add), self.masked)
                    dve.wait_ge(*upto(self.o_in_ps, i + 1))
                    dst = ho[:, c * CH:(c + 1) * CH]
                    if back:
                        vstep(nc.vector.tensor_tensor(dst, dst, bo[:, 0:P], ALU.add))
                    else:
                        vstep(nc.vector.tensor_copy(dst, bo[:, 0:P]))
                    dve.wait_ge(*upto(self.state_ready, i + 1))
                    sig(nc.vector, nc.vector.scalar_tensor_tensor(h_st[(i + 1) % 2][:], h_st[i % 2][:], h_el[:, c:c + 1], bo[:, P:2 * P],
                                                   ALU.mult, ALU.add), self.state_ready)

            def act(self, act):
                h, back = self.head, self.back
                s = z[:, 9 + 4 * h + back]
                act.wait_ge(*upto(self.k_ready, 1))
                sig(nc.scalar, nc.scalar.activation(s, s, ACT.Ln), self.lf_ready)
                act.wait_ge(*upto(self.b_ready, 1))
                b = hb[:, :].rearrange("p (c t) -> p c t", c=NCH)
                end = b[:, :, 0] if back else b[:, :, CH - 1]
                astep(nc.scalar.activation(h_el, end, ACT.Exp))
                sig(nc.scalar, nc.scalar.activation(hdq[:], hb[:], ACT.Exp), self.dq_exp)
                act.wait_ge(*upto(self.dk_arg, 1))
                sig(nc.scalar, nc.scalar.activation(hdk[:], hdk[:], ACT.Exp), self.dk_exp)
                for l in range(7):
                    act.wait_ge(*upto(self.arg_ready, l + 1))
                    sig(nc.scalar, nc.scalar.activation(he[l % 2][:], he[l % 2][:], ACT.Exp), self.exp_ready)
                for i, (dst, srcs) in enumerate(((v_tok, (0, 4)), (v_tok, (4, 6)), (k_tok, (0, 4)), (k_tok, (4, 6)))):
                    act.wait_ge(*upto(self.tok_in_ps, i + 1))
                    a, e = srcs
                    sig(nc.scalar, nc.scalar.copy(dst[:, a:e], ps[4 + i][:, 0:(e - a) * P].rearrange("p (c t) -> p c t", c=e - a)), self.tok_read)

            def pe(self, pe):
                h, back = self.head, self.back
                q, v = z[:, 8 + 4 * h], z[:, 11 + 4 * h]
                pe.wait_ge(*upto(self.dq_ready, 1))
                for i, (src, (a, e)) in enumerate(((v, (0, 4)), (v, (4, 6)), (hdk, (0, 4)), (hdk, (4, 6)))):
                    if i == 2:
                        pe.wait_ge(*upto(self.dk_ready, 1))
                    for c in range(a, e):
                        last = nc.tensor.transpose(ps[4 + i][:, (c - a) * P:(c - a + 1) * P], src[:, c * CH:(c + 1) * CH], ident[:])
                    last.then_inc(self.tok_in_ps[0], 1)
                qo, ko = (0, 1) if back else (1, 0)
                for i, c in enumerate(self.order):
                    bx, by, bo = ps[2 * (i % 2)], ps[2 * (i % 2) + 1], ps[4 + i % 2]
                    t0 = c * CH
                    if i >= 2:
                        pe.wait_ge(*upto(self.state_ready, i))
                    nc.tensor.matmul(bx[:, 0:P], hk[:, t0:t0 + CH], q[:, t0:t0 + CH], start=True, stop=True)
                    for l in range(2):
                        half = LEVELS[l]
                        for n in range(CH // (2 * half)):
                            ss, tt = 2 * half * n + half * ko, 2 * half * n + half * qo
                            nc.tensor.matmul(bx[ss:ss + half, tt:tt + half], m_lev[l][:, t0 + ss:t0 + ss + half],
                                             m_lev[l][:, t0 + tt:t0 + tt + half], start=True, stop=True)
                    for l in range(2, 7):
                        dst = bx[:, (l - 1) * P:l * P] if l < 5 else by[:, (l - 5) * P:(l - 4) * P]
                        m = m_lev[l][:, t0:t0 + CH]
                        last = nc.tensor.matmul(dst, m, m, start=True, stop=True)
                    last.then_inc(self.scores_in_ps[0], 1)
                    if i == 0:
                        pe.wait_ge(*upto(self.tok_read, 4))
                    nc.tensor.matmul(bo[:, P:2 * P], k_tok[:, c], v_tok[:, c], start=True, stop=True)
                    pe.wait_ge(*upto(self.state_ready, i + 1))
                    nc.tensor.matmul(bo[:, 0:P], h_st[i % 2][:], hdq[:, t0:t0 + CH], start=True, stop=False)
                    pe.wait_ge(*upto(self.masked, i + 1))
                    nc.tensor.matmul(bo[:, 0:P], v_tok[:, c], a_sum[i % 2][:], start=False, stop=True).then_inc(self.o_in_ps[0], 1)

        class HgOut(Phase):

            def __init__(self, head, unit):
                super().__init__()
                self.head, self.unit = head, unit
                self.hg_sq, self.hg_sum, self.hg_rstd = cnt.take("hg_sq", 1), cnt.take("hg_sum", 1), cnt.take("hg_rstd", 1)
                self.hg_t, self.mix_hi, self.mix_lo = cnt.take("hg_t", 2), cnt.take("mix_hi", 1), cnt.take("mix_lo", 1)

            def act(self, act):
                act.wait_ge(*upto(self.unit.state_ready, 7))
                sig(nc.scalar, nc.scalar.activation(he[0][:], ho[:], ACT.Square), self.hg_sq)
                act.wait_ge(*upto(self.hg_sum, 1))
                astep(nc.scalar.activation(he[1][:, 0:512], ps[6][:, 0:512], ACT.Ln, scale=1.0 / P, bias=epsv[:, 0:1]))
                astep(nc.scalar.activation(he[1][:, 512:TA], ps[7][:, 0:256], ACT.Ln, scale=1.0 / P, bias=epsv[:, 0:1]))
                sig(nc.scalar, nc.scalar.activation(he[1][:], he[1][:], ACT.Exp, scale=-0.5), self.hg_rstd)
                act.wait_ge(*upto(self.hg_t, 2))
                sig(nc.scalar, nc.scalar.copy(mix_hi[4 + self.head][:], ho[:]), self.mix_hi)

            def pe(self, pe):
                pe.wait_ge(*upto(self.hg_sq, 1))
                nc.tensor.matmul(ps[6][:, 0:512], ones[:], he[0][:, 0:512], start=True, stop=True)
                nc.tensor.matmul(ps[7][:, 0:256], ones[:], he[0][:, 512:TA], start=True, stop=True).then_inc(self.hg_sum[0], 1)

            def dve(self, dve):
                dve.wait_ge(*upto(self.hg_rstd, 1))
                sig(nc.vector, nc.vector.scalar_tensor_tensor(ho[:], ho[:], V("onorm"), he[1][:], ALU.mult, ALU.mult), self.hg_t)
                dve.wait_ge(*upto(self.hg_t, 1))
                sig(nc.vector, nc.vector.tensor_tensor(ho[:], ho[:], z[:, 4 + self.head], ALU.mult), self.hg_t)
                dve.wait_ge(*upto(self.mix_hi, 1))
                sig(nc.vector, nc.vector.tensor_tensor(mix_lo[4 + self.head][:], ho[:], mix_hi[4 + self.head][:].bitcast(f32),
                                        ALU.subtract), self.mix_lo)

        PW = 8 + TC + 8 + TL + 8
        p_buf = [arena(f"p_buf{i}", [P, PW], 3200 * i) for i in range(3)]
        p_y = arena("p_y", [P, TA], 9600)
        p_inv = arena("p_inv", [P, 4, TA], 13 * K)
        p_w = arena("p_w", [P, 4, P], 25 * K)

        class Pool(Phase):
            def __init__(self, gate):
                super().__init__()
                self.gate, self.val = gate, loaded(2)
                self.pool_y, self.pool_ps, self.pool_hi = cnt.take("pool_y", 4), cnt.take("pool_ps", 4), cnt.take("pool_hi", 4)
                self.pool_lo = cnt.take("pool_lo", 4)

            def sp(self, sp):
                sp.wait_ge(*self.gate)
                a, w = CST["pool_inv"]
                sp.dma_start(p_inv[:, :, :].rearrange("p g t -> p (g t)"), cst[:, a:a + w]).then_inc(phase_in, 16)
                sp.dma_start(p_w[:, :, :], w_pool).then_inc(phase_in, 16)

            def dve(self, dve):
                dve.wait_ge(*self.gate)
                for i in range(3):
                    last = nc.vector.memset(p_buf[i][:], 0.0)
                vstep(last)
                for g in range(4):
                    u = z[:, g]
                    vstep(nc.vector.tensor_copy(p_buf[2][:, 8:8 + TC], u[:, CTX]))
                    vstep(nc.vector.tensor_copy(p_buf[2][:, 16 + TC:16 + TC + TL], u[:, LAT]))
                    src = 2
                    for j in range(g + 1):
                        step, dst = 1 << j, j % 2
                        n = PW - 2 * step + 1
                        vstep(nc.vector.tensor_tensor(p_buf[dst][:, 0:n], p_buf[src][:, 0:n], p_buf[src][:, step:step + n], ALU.add))
                        src = dst
                    half = 1 << g
                    if g == 0:
                        dve.wait_ge(phase_in, self.val)
                    else:
                        dve.wait_ge(*upto(self.pool_ps, g))
                    s = p_buf[src]
                    vstep(nc.vector.tensor_tensor(p_y[:, CTX], s[:, 8 - half:8 - half + TC], p_inv[:, g, CTX], ALU.mult))
                    vstep(nc.vector.tensor_tensor(p_y[:, LAT], s[:, 16 + TC - half:16 + TC - half + TL], p_inv[:, g, LAT], ALU.mult))
                    sig(nc.vector, nc.vector.tensor_tensor(p_y[:], p_y[:], u, ALU.subtract), self.pool_y)
                    dve.wait_ge(*upto(self.pool_hi, g + 1))
                    for a, e, b in ((0, 512, 0), (512, TA, 1)):
                        last = nc.vector.scalar_tensor_tensor(mix_lo[g][:, a:e], ps[2 * (g % 2) + b][:, 0:e - a], V("pool_scale", g),
                                                              mix_hi[g][:, a:e].bitcast(f32), ALU.mult, ALU.subtract)
                    sig(nc.vector, last, self.pool_lo)

            def pe(self, pe):
                for g in range(4):
                    pe.wait_ge(*upto(self.pool_y, g + 1))
                    if g >= 2:
                        pe.wait_ge(*upto(self.pool_lo, g - 1))
                    nc.tensor.matmul(ps[2 * (g % 2)][:, 0:512], p_w[:, g], p_y[:, 0:512], start=True, stop=True)
                    nc.tensor.matmul(ps[2 * (g % 2) + 1][:, 0:256], p_w[:, g], p_y[:, 512:TA], start=True, stop=True).then_inc(self.pool_ps[0], 1)

            def act(self, act):
                for g in range(4):
                    act.wait_ge(*upto(self.pool_ps, g + 1))
                    astep(nc.scalar.activation(mix_hi[g][:, 0:512], ps[2 * (g % 2)][:, 0:512], ACT.Copy, scale=V("pool_scale", g)))
                    sig(nc.scalar, nc.scalar.activation(mix_hi[g][:, 512:TA], ps[2 * (g % 2) + 1][:, 0:256], ACT.Copy,
                                         scale=V("pool_scale", g)), self.pool_hi)

        yc = arena("yc", [P, ND, TC], 32 * K)
        yc2 = arena("yc2", [P, ND, TC], 0)

        def y_evac(dst, cdst=None):
            def act(g, act, i, a):
                for n in range(g.per):
                    act.wait_ge(chunk_done, g.tile(i, n))
                    ins = nc.scalar.copy(dst[:, bass.ds(g.per * i + n, 1)].rearrange("p o t -> p (o t)"), g.out(n))
                    if cdst is not None:
                        ins = nc.scalar.copy(cdst[:, bass.ds(g.per * i + n, 1)].rearrange("p o t -> p (o t)"), g.ctx_out(n))
                    ins.then_inc(mm_free, 1)
            return act

        class Swiglu:

            def __init__(self, t, hi_buf, lo_buf):
                self.t, self.hi_buf, self.lo_buf = t, hi_buf, lo_buf
                self.silu, self.hi, self.lo = cnt.take("silu_ready", NH), cnt.take("hid_hi_ready", NH), cnt.take("hid_lo_ready", NH)
                self.done = upto(self.lo, NH, 2)

            def hid(self, buf, i, q):
                return buf[:, bass.ds(2 * i + q, 1), 0:self.t].rearrange("p o t -> p (o t)")

            def act(self, g, act, i, a):
                for q in range(2):
                    act.wait_ge(chunk_done, g.tile(i, 2 * q))
                    act.wait_ge(self.lo[0], 2 + self.lo[1] + 2 * i + q - 1)
                    nc.scalar.activation(wk[q][:, 0:self.t], g.out(2 * q), ACT.Silu).then_inc(self.silu[0], 1)
                    act.wait_ge(mm_free, NBANK + g.tile0 + 4 * i + 2 * q + 2)
                    nc.scalar.copy(self.hid(self.hi_buf, i, q), wk[2 + q][:, 0:self.t]).then_inc(self.hi[0], 1)

            def dve(self, g, dve, i, a):
                for q in range(2):
                    dve.wait_ge(chunk_done, g.tile(i, 2 * q + 1))
                    dve.wait_ge(self.silu[0], self.silu[1] + 2 * i + q + 1)
                    nc.vector.tensor_tensor(wk[2 + q][:, 0:self.t], wk[q][:, 0:self.t], g.out(2 * q + 1), ALU.mult).then_inc(mm_free, 2)
                    dve.wait_ge(self.hi[0], self.hi[1] + 2 * i + q + 1)
                    nc.vector.tensor_tensor(self.hid(self.lo_buf, i, q), wk[2 + q][:, 0:self.t],
                                            self.hid(self.hi_buf, i, q).bitcast(f32), ALU.subtract).then_inc(self.lo[0], 1)
                    if g.rows:
                        g.rows.dve(dve, i, a, q, 2)

        r_cos = arena("r_cos", [P, TL], 121 * K)
        r_sin = arena("r_sin", [P, TL], 123 * K)
        r_rot = arena("r_rot", [P, P], 125 * K)
        r_sq = [arena(f"r_sq{i}", [P, TA], (32 + 3 * i) * K) for i in range(2)]
        r_rs = [arena(f"r_rs{i}", [P, TA], (38 + 3 * i) * K) for i in range(2)]
        r_t = [arena(f"r_t{i}", [P, TL], (44 + 2 * i) * K) for i in range(2)]

        class Rope(Phase):

            def __init__(self, tiles, which, gate, temps):
                super().__init__()
                self.tiles, self.which, self.gate, self.val, self.temps = tiles, which, gate, loaded(3), temps
                n = len(tiles)
                self.head_sq, self.head_sum, self.head_rstd = cnt.take("head_sq", n), cnt.take("head_sum", n), cnt.take("head_rstd", n)
                self.head_normed, self.rotated, self.rope_cos = cnt.take("head_normed", n), cnt.take("rotated", n), cnt.take("rope_cos", n)
                self.rope_sin, self.roped = cnt.take("rope_sin", n), cnt.take("roped", n)
                self.done = upto(self.roped, n)

            def sp(self, sp):
                sp.wait_ge(*self.gate)
                for name, dst in (("cos", r_cos), ("sin", r_sin), ("rot", r_rot)):
                    a, w = CST[f"{name}{self.which}"]
                    sp.dma_start(dst[:], cst[:, a:a + w]).then_inc(phase_in, 16)

            def act(self, act):
                act.wait_ge(*self.gate)
                for j, (x_, t, gain) in enumerate(self.tiles):
                    if gain is not None:
                        sig(nc.scalar, nc.scalar.activation(r_sq[j % 2][:, 0:t], x_, ACT.Square), self.head_sq)
                        act.wait_ge(*upto(self.head_sum, j + 1))
                        if j >= 2:
                            act.wait_ge(*upto(self.head_normed, j - 1))
                        r = r_rs[j % 2]
                        if t > TL:
                            astep(nc.scalar.activation(r[:, TL:t], ps[2 * (j % 2) + 1][:, 0:t - TL], ACT.Ln, scale=1.0 / P, bias=epsv[:, 0:1]))
                        astep(nc.scalar.activation(r[:, 0:TL], ps[2 * (j % 2)][:, 0:TL], ACT.Ln, scale=1.0 / P, bias=epsv[:, 0:1]))
                        sig(nc.scalar, nc.scalar.activation(r[:, 0:t], r[:, 0:t], ACT.Exp, scale=-0.5), self.head_rstd)

            def pe(self, pe):
                pe.wait_ge(*self.gate)
                pe.wait_ge(phase_in, self.val)
                for j in range(len(self.tiles) + 1):
                    if j < len(self.tiles) and self.tiles[j][2] is not None:
                        t = self.tiles[j][1]
                        pe.wait_ge(*upto(self.head_sq, j + 1))
                        if t > TL:
                            nc.tensor.matmul(ps[2 * (j % 2) + 1][:, 0:t - TL], ones[:], r_sq[j % 2][:, TL:t], start=True, stop=True)
                        nc.tensor.matmul(ps[2 * (j % 2)][:, 0:TL], ones[:], r_sq[j % 2][:, 0:TL], start=True, stop=True).then_inc(self.head_sum[0], 1)
                    if j >= 1:
                        m = j - 1
                        if self.tiles[m][2] is not None:
                            pe.wait_ge(*upto(self.head_normed, m + 1))
                        if m >= 2:
                            pe.wait_ge(*upto(self.rope_sin, m - 1))
                        nc.tensor.matmul(ps[4 + m % 2][:, 0:TL], r_rot[:], self.tiles[m][0][:, 0:TL], start=True, stop=True).then_inc(self.rotated[0], 1)

            def dve(self, dve):
                dve.wait_ge(*self.gate)
                dve.wait_ge(phase_in, self.val)
                for j in range(len(self.tiles) + 1):
                    if j < len(self.tiles) and self.tiles[j][2] is not None:
                        x_, t, gain = self.tiles[j]
                        dve.wait_ge(*upto(self.head_rstd, j + 1))
                        sig(nc.vector, nc.vector.scalar_tensor_tensor(x_, x_, gain, r_rs[j % 2][:, 0:t], ALU.mult, ALU.mult), self.head_normed)
                    if j >= 1:
                        m = j - 1
                        x_, tt = self.tiles[m][0], self.temps[m % 2]
                        dve.wait_ge(*upto(self.rotated, m + 1))
                        sig(nc.vector, nc.vector.tensor_tensor(tt[:], r_sin[:], ps[4 + m % 2][:, 0:TL], ALU.mult), self.rope_sin)
                        sig(nc.vector, nc.vector.tensor_tensor(x_[:, 0:TL], x_[:, 0:TL], r_cos[:], ALU.mult), self.rope_cos)
                        sig(nc.vector, nc.vector.tensor_tensor(x_[:, 0:TL], x_[:, 0:TL], tt[:], ALU.add), self.roped)

        class Tokens(Phase):

            def __init__(self, pairs, gate):
                super().__init__()
                self.groups = [pairs[i:i + 4] for i in range(0, len(pairs), 4)]
                self.gate = gate
                self.turned, self.copied = cnt.take("turned", len(self.groups)), cnt.take("turned_copied", len(self.groups))
                self.done = upto(self.copied, len(self.groups))

            def pe(self, pe):
                pe.wait_ge(*self.gate)
                for i, g in enumerate(self.groups):
                    if i >= 2:
                        pe.wait_ge(*upto(self.copied, i - 1))
                    for j, (src, _) in enumerate(g):
                        last = nc.tensor.transpose(ps[6 + i % 2][:, j * P:(j + 1) * P], src, ident[:])
                    last.then_inc(self.turned[0], 1)

            def act(self, act):
                for i, g in enumerate(self.groups):
                    act.wait_ge(*upto(self.turned, i + 1))
                    for j, (_, dst) in enumerate(g):
                        ins = nc.scalar.copy(dst, ps[6 + i % 2][:, j * P:(j + 1) * P])
                    sig(nc.scalar, ins, self.copied)

        s_buf = [arena(f"s_buf{i}", [P, 10 * P], 5 * K * i) for i in range(4)]
        pt_buf = [arena(f"pt_buf{i}", [P, 10, P], (20 + 5 * i) * K) for i in range(2)]

        class Attention(Phase):

            def __init__(self, units, gate, masks=()):
                super().__init__()
                self.units, self.gate, self.masks = units, gate, masks
                self.val = loaded(len(masks)) if masks else None
                n = len(units)
                self.groups, total = [], 0
                for u in units:
                    blocks = len(u["values"])
                    self.groups.append((total, (blocks + 3) // 4))
                    total += (blocks + 3) // 4
                self.qk_in_ps, self.qk_copied, self.row_max = cnt.take("qk_in_ps", n), cnt.take("qk_copied", n), cnt.take("row_max", n)
                self.neg_max, self.p_exp, self.p_inv = cnt.take("neg_max", n), cnt.take("p_exp", n), cnt.take("p_inv", n)
                self.p_normed, self.pt_in_ps, self.pt_copied = cnt.take("p_normed", n), cnt.take("pt_in_ps", total), cnt.take("pt_copied", total)
                self.pv_in_ps, self.att_hi, self.att_lo = cnt.take("pv_in_ps", n), cnt.take("att_hi", n), cnt.take("att_lo", n)
                self.done = upto(self.att_lo, n)

            def sp(self, sp):
                if self.masks:
                    sp.wait_ge(*self.gate)
                for name, dst in self.masks:
                    a, w = CST[name]
                    sp.dma_start(dst, cst[:, a:a + w]).then_inc(phase_in, 16)

            def pe(self, pe):
                pe.wait_ge(*self.gate)
                n = len(self.units)
                for u in range(n + 3):
                    if u < n:
                        if u >= 1:
                            pe.wait_ge(*upto(self.qk_copied, u))
                        for b, (keys, w, _) in enumerate(self.units[u]["segs"]):
                            last = nc.tensor.matmul(ps[b][:, 0:w], self.units[u]["q"][b], keys, start=True, stop=True)
                        last.then_inc(self.qk_in_ps[0], 1)
                    if 0 <= u - 2 < n:
                        m = u - 2
                        g0, ng = self.groups[m]
                        nv = len(self.units[m]["values"])
                        pe.wait_ge(*upto(self.p_normed, m + 1))
                        for g in range(ng):
                            if g0 + g >= 3:
                                pe.wait_ge(*upto(self.pt_copied, g0 + g - 2))
                            for j in range(4 * g, min(4 * g + 4, nv)):
                                last = nc.tensor.transpose(ps[3 + (g0 + g) % 3][:, (j % 4) * P:(j % 4 + 1) * P],
                                                           s_buf[m % 4][:, j * P:(j + 1) * P], ident[:])
                            last.then_inc(self.pt_in_ps[0], 1)
                    if 0 <= u - 3 < n:
                        m = u - 3
                        g0, ng = self.groups[m]
                        vals = self.units[m]["values"]
                        if m >= 2:
                            pe.wait_ge(*upto(self.att_lo, m - 1))
                        pe.wait_ge(*upto(self.pt_copied, g0 + ng))
                        for j, v in enumerate(vals):
                            last = nc.tensor.matmul(ps[6 + m % 2][:, 0:P], v, pt_buf[m % 2][:, j], start=j == 0, stop=j == len(vals) - 1)
                        last.then_inc(self.pv_in_ps[0], 1)

            def dve(self, dve):
                if self.masks:
                    dve.wait_ge(phase_in, self.val)
                n = len(self.units)
                width = lambda u: P * len(self.units[u]["values"])
                for u in range(n + 4):
                    if u < n:
                        mx, nm = (small[:, 32 + 4 * (u % 4) + i:33 + 4 * (u % 4) + i] for i in range(2))
                        dve.wait_ge(*upto(self.qk_in_ps, u + 1))
                        if u >= 4:
                            g0, ng = self.groups[u - 4]
                            dve.wait_ge(*upto(self.pt_in_ps, g0 + ng))
                        off = 0
                        for b, (_, w, mask) in enumerate(self.units[u]["segs"]):
                            dst = s_buf[u % 4][:, off:off + w]
                            if mask is None:
                                last = nc.vector.tensor_copy(dst, ps[b][:, 0:w])
                            else:
                                last = nc.vector.tensor_tensor(dst, ps[b][:, 0:w], mask, ALU.add)
                            off += w
                        sig(nc.vector, last, self.qk_copied)
                        sig(nc.vector, nc.vector.tensor_reduce(mx, s_buf[u % 4][:, 0:off], AX.X, ALU.max), self.row_max)
                        sig(nc.vector, nc.vector.tensor_scalar(nm, mx, -SCALE, None, ALU.mult), self.neg_max)
                    if 0 <= u - 1 < n:
                        m = u - 1
                        sm, rc = (small[:, 34 + 4 * (m % 4) + i:35 + 4 * (m % 4) + i] for i in range(2))
                        dve.wait_ge(*upto(self.p_exp, m + 1))
                        sig(nc.vector, nc.vector.reciprocal(rc, sm), self.p_inv)
                        p = s_buf[m % 4][:, 0:width(m)]
                        sig(nc.vector, nc.vector.tensor_scalar(p, p, rc, None, ALU.mult), self.p_normed)
                    if 0 <= u - 4 < n:
                        m = u - 4
                        dve.wait_ge(*upto(self.att_hi, m + 1))
                        sig(nc.vector, nc.vector.tensor_tensor(self.units[m]["lo"], ps[6 + m % 2][:, 0:P], self.units[m]["hi"].bitcast(f32),
                                                               ALU.subtract), self.att_lo)

            def act(self, act):
                n = len(self.units)
                for u in range(n + 3):
                    if u < n:
                        nm, sm = (small[:, 33 + 4 * (u % 4) + i:34 + 4 * (u % 4) + i] for i in range(2))
                        w = P * len(self.units[u]["values"])
                        act.wait_ge(*upto(self.neg_max, u + 1))
                        sig(nc.scalar, nc.scalar.activation(s_buf[u % 4][:, 0:w], s_buf[u % 4][:, 0:w], ACT.Exp, bias=nm, scale=SCALE,
                                                            accum_out=sm), self.p_exp)
                    if 0 <= u - 2 < n:
                        m = u - 2
                        g0, ng = self.groups[m]
                        nv = len(self.units[m]["values"])
                        if m >= 2:
                            act.wait_ge(*upto(self.pv_in_ps, m - 1))
                        for g in range(ng):
                            e = min(4, nv - 4 * g)
                            act.wait_ge(*upto(self.pt_in_ps, g0 + g + 1))
                            sig(nc.scalar, nc.scalar.copy(pt_buf[m % 2][:, 4 * g:4 * g + e],
                                                          ps[3 + (g0 + g) % 3][:, 0:e * P].rearrange("p (j t) -> p j t", j=e)), self.pt_copied)
                    if 0 <= u - 3 < n:
                        m = u - 3
                        act.wait_ge(*upto(self.pv_in_ps, m + 1))
                        sig(nc.scalar, nc.scalar.copy(self.units[m]["hi"], ps[6 + m % 2][:, 0:P]), self.att_hi)

        zx = arena("zx", [P, 48, TL], 32 * K)
        c_acc = [at("c_acc", [P, TL], o_xc + 4160), rstd]

        class SsmConv:

            def __init__(self):
                self.tap, self.out = cnt.take("conv_tap", 4 * 32), cnt.take("conv_out", 32)

            def act(self, g, act, i, a):
                for n in range(4):
                    act.wait_ge(chunk_done, g.tile(i, n))
                    dst = zx[:, bass.ds(4 * i + n, 1)].rearrange("p o t -> p (o t)")
                    if a < 4:
                        nc.scalar.activation(dst, g.out(n), ACT.Silu).then_inc(mm_free, 1)
                        continue
                    t = 4 * i + n - 16
                    act.wait_ge(self.tap[0], 4 + self.tap[1] + 4 * t)
                    nc.scalar.copy(pad[0][:, 3:3 + TL], g.out(n)).then_inc(mm_free, 1)
                    act.wait_ge(self.tap[0], 4 + self.tap[1] + 4 * t + 4)
                    nc.scalar.activation(dst, c_acc[n % 2][:], ACT.Silu, bias=V("conv_b", t)
                                         if isinstance(t, int) else vec[:, bass.ds(VEC["conv_b"][0] + t, 1)]).then_inc(self.out[0], 1)

            def dve(self, g, dve, i, a):
                if a < 4:
                    return
                for n in range(4):
                    t = 4 * i + n - 16
                    acc = c_acc[n % 2]
                    dve.wait_ge(mm_free, NBANK + g.tile0 + 4 * i + n + 1)
                    dve.wait_ge(self.out[0], 2 + self.out[1] + t - 1)
                    for j in range(4):
                        w = vec[:, bass.ds(VEC["conv_w"][0] + 32 * j + t, 1)]
                        src = pad[0][:, j:j + TL]
                        if j:
                            dve.wait_ge(self.tap[0], 4 + self.tap[1] + 4 * t + j)
                            ins = nc.vector.scalar_tensor_tensor(acc[:], src, w, acc[:], ALU.mult, ALU.add)
                        else:
                            ins = nc.vector.tensor_scalar(acc[:], src, w, None, ALU.mult)
                        ins.then_inc(self.tap[0], 1)

        b_tok = arena("b_tok", [P, 4, P], 0)
        x_dt = arena("x_dt", [P, 4, 256], 2 * K)
        x_dd = arena("x_dd", [P, 4, 256], 6 * K)
        s_cb = arena("s_cb", [P, 4, P], 10 * K)
        s_w = [arena(f"s_w{i}", [P, 4, P], o * K) for i, o in enumerate((12, 14, 22, 129))]
        s_prev = arena("s_prev", [P, 4, 256], 16 * K)
        s_tok = arena("s_tok", [P, 3, 4, NSH], 20 * K)
        s_cd = arena("s_cd", [P, 4, NSH], 21 * K + 512)
        d_dt = arena("d_dt", [NSH, TL], 22 * K)
        d_cs = arena("d_cs", [NSH, TL], 24 * K)
        d_ec = arena("d_ec", [NSH, TL], 26 * K)
        s_y = [arena(f"s_y{i}", [P, TL], (28 + 2 * i) * K) for i in range(2)]
        d_t = [arena(f"d_t{i}", [NSH, TL], (12 + 2 * i) * K) for i in range(3)]
        dtw = arena("dtw", [P, ND, NSH], 128 * K)
        ssm_hi = [arena(f"ssm_hi{k}", [P, TL], (32 + 32 + 2 * k) * K, f32r) for k in range(16)]
        ssm_lo = [arena(f"ssm_lo{k}", [P, TL], (32 + 2 * k) * K, f32r) for k in range(16)]

        class DtPart(Phase):

            def __init__(self, gate):
                super().__init__()
                self.gate, self.val = gate, loaded(2)
                self.dt_in_ps, self.dt_pos, self.dt_act = cnt.take("dt_in_ps", 1), cnt.take("dt_pos", 1), cnt.take("dt_act", 6)
                self.dt_dve, self.dt_turned, self.dt_tok = cnt.take("dt_dve", 6), cnt.take("dt_turned", 2), cnt.take("dt_tok", 2)
                self.done = upto(self.dt_tok, 2)

            def sp(self, sp):
                sp.wait_ge(*self.gate)
                sp.dma_start(dtw[:, :, :], w_dt).then_inc(phase_in, 16)
                a, w = CST["ssd_mask"]
                sp.dma_start(ssd_mask[:], cst[:, a:a + w]).then_inc(phase_in, 16)

            def pe(self, pe):
                pe.wait_ge(phase_in, self.val)
                pe.wait_ge(*self.gate)
                for k in range(ND):
                    for q, h in enumerate((h_hi, h_lo)):
                        last = nc.tensor.matmul(ps[7][0:NSH, :], dtw[:, k], h[:, k].bitcast(f32), start=k == 0 and q == 0,
                                                stop=k == ND - 1 and q == 1)
                last.then_inc(self.dt_in_ps[0], 1)
                pe.wait_ge(*upto(self.dt_dve, 5))
                for q, src in enumerate((d_cs, d_dt, d_t[0])):
                    for c in range(4):
                        nc.tensor.transpose(ps[6][:, (q * 4 + c) * NSH:(q * 4 + c + 1) * NSH], src[:, c * CH:(c + 1) * CH], ident[0:NSH, 0:NSH])
                nc.tensor.matmul(ps[5][:, 0:4 * NSH], ones[0:NSH, :], d_t[1][:, 0:4 * NSH], start=True, stop=True).then_inc(self.dt_turned[0], 2)

            def act(self, act):
                a, w = VEC["dt_bias"]
                bias = vec[0:NSH, a:a + 1]
                act.wait_ge(*upto(self.dt_pos, 1))
                astep(nc.scalar.activation(d_t[0][:], ps[7][0:NSH, :], ACT.Abs, bias=bias))
                astep(nc.scalar.activation(d_t[0][:], d_t[0][:], ACT.Exp, scale=-1.0))
                a, w = VEC["a_log"]
                sig(nc.scalar, nc.scalar.activation(small[0:NSH, 48:49], vec[0:NSH, a:a + 1], ACT.Exp), self.dt_act)
                act.wait_ge(*upto(self.dt_dve, 3))
                sig(nc.scalar, nc.scalar.activation(d_ec[:], d_cs[:], ACT.Exp), self.dt_act)
                act.wait_ge(*upto(self.dt_dve, 4))
                sig(nc.scalar, nc.scalar.activation(d_t[0][:], d_t[0][:], ACT.Exp), self.dt_act)
                act.wait_ge(*upto(self.dt_turned, 2))
                astep(nc.scalar.copy(s_tok[:, :, :, :].rearrange("p q c h -> p (q c h)"), ps[6][:, 0:12 * NSH]))
                sig(nc.scalar, nc.scalar.copy(s_cd[:, :, :].rearrange("p c h -> p (c h)"), ps[5][:, 0:4 * NSH]), self.dt_tok, 2)

            def dve(self, dve):
                a, w = VEC["dt_bias"]
                bias = vec[0:NSH, a:a + 1]
                e, s, u = d_t
                dve.wait_ge(*upto(self.dt_in_ps, 1))
                sig(nc.vector, nc.vector.tensor_scalar(d_dt[:], ps[7][0:NSH, :], bias, 0.0, ALU.add, ALU.max), self.dt_pos)
                dve.wait_ge(*upto(self.dt_act, 1))
                vstep(nc.vector.tensor_scalar(u[:], e[:], 2.0, None, ALU.add))
                vstep(nc.vector.reciprocal(u[:], u[:]))
                vstep(nc.vector.tensor_tensor(s[:], e[:], u[:], ALU.mult))
                vstep(nc.vector.tensor_tensor(u[:], s[:], s[:], ALU.mult))
                vstep(nc.vector.tensor_scalar(e[:], u[:], 2.0 / 17, 2.0 / 15, ALU.mult, ALU.add))
                for c in (13, 11, 9, 7, 5, 3, 1):
                    vstep(nc.vector.tensor_tensor(e[:], e[:], u[:], ALU.mult))
                    vstep(nc.vector.tensor_scalar(e[:], e[:], 2.0 / c, None, ALU.add))
                vstep(nc.vector.tensor_tensor(e[:], e[:], s[:], ALU.mult))
                vstep(nc.vector.tensor_tensor(d_dt[:], d_dt[:], e[:], ALU.add))
                vstep(nc.vector.tensor_scalar(small[0:NSH, 49:50], small[0:NSH, 48:49], -1.0, None, ALU.mult))
                vstep(nc.vector.tensor_scalar(e[:], d_dt[:], small[0:NSH, 49:50], None, ALU.mult))
                for c in range(4):
                    last = nc.vector.tensor_tensor_scan(d_cs[:, c * CH:(c + 1) * CH], ones[0:NSH, :], e[:, c * CH:(c + 1) * CH], 0.0, ALU.mult, ALU.add)
                sig(nc.vector, last, self.dt_dve, 3)
                dve.wait_ge(*upto(self.dt_dve, 3))
                v = d_cs[:, :].rearrange("p (c t) -> p c t", c=4)
                sig(nc.vector, nc.vector.tensor_tensor(e[:, :].rearrange("p (c t) -> p c t", c=4), v[:, :, CH - 1:CH].to_broadcast([NSH, 4, CH]), v,
                                        ALU.subtract), self.dt_dve)
                dve.wait_ge(*upto(self.dt_act, 3))
                for c in range(4):
                    last = nc.vector.tensor_scalar(s[:, c * NSH:(c + 1) * NSH], ident[0:NSH, 0:NSH], d_ec[:, c * CH + CH - 1:c * CH + CH], None, ALU.mult)
                sig(nc.vector, last, self.dt_dve)

        class Ssd(Phase):

            def __init__(self, g, gate, mask_val):
                super().__init__()
                self.g, self.gate, self.mask_val = g, gate, mask_val
                self.ssd_turned, self.ssd_b, self.x_ready = cnt.take("ssd_turned", 1), cnt.take("ssd_b", 1), cnt.take("x_ready", 1)
                self.xd_ready, self.st_in_ps, self.prev_ready = cnt.take("xd_ready", 1), cnt.take("st_in_ps", 3), cnt.take("prev_ready", 4)
                self.row_in_ps, self.seg_ready, self.seg_exp = cnt.take("row_in_ps", 4), cnt.take("seg_ready", 4), cnt.take("seg_exp", 4)
                self.seg_w, self.y_in_ps, self.e_read = cnt.take("seg_w", 4), cnt.take("y_in_ps", 2), cnt.take("e_read", 2)
                self.y_tile, self.y_step, self.y_sq = cnt.take("y_tile", 2), cnt.take("y_step", 8), cnt.take("y_sq", 2)
                self.y_sum, self.y_rstd, self.y_scaled2 = cnt.take("y_sum", 1), cnt.take("y_rstd", 1), cnt.take("y_scaled2", 2)
                self.y_hi, self.y_lo = cnt.take("y_hi", 2), cnt.take("y_lo", 2)
                self.done = upto(self.y_lo, 2)

            def pe(self, pe):
                g = self.g
                pe.wait_ge(*self.gate)
                xs = [zx[:, 16 + 2 * g + t] for t in range(2)]
                bt, ct = zx[:, 32 + g], zx[:, 40 + g]
                for c in range(4):
                    nc.tensor.transpose(ps[0][:, c * P:(c + 1) * P], bt[:, c * CH:(c + 1) * CH], ident[:])
                for c in range(4):
                    for t in range(2):
                        col = (c % 2) * 256 + t * P
                        nc.tensor.transpose(ps[1 + c // 2][:, col:col + P], xs[t][:, c * CH:(c + 1) * CH], ident[:])
                for c in range(4):
                    last = nc.tensor.matmul(ps[3][:, c * P:(c + 1) * P], bt[:, c * CH:(c + 1) * CH], ct[:, c * CH:(c + 1) * CH], start=True, stop=True)
                last.then_inc(self.ssd_turned[0], 1)
                pe.wait_ge(*upto(self.ssd_b, 1))
                pe.wait_ge(*upto(self.xd_ready, 1))
                for c in range(3):
                    nc.tensor.matmul(ps[4 + c // 2][:, (c % 2) * 256:(c % 2 + 1) * 256], b_tok[:, c], x_dd[:, c], start=True, stop=True).then_inc(self.st_in_ps[0], 1)

                for hh in range(4):
                    h = 4 * g + hh
                    if hh >= 1:
                        pe.wait_ge(*upto(self.seg_ready, hh))
                    nc.tensor.matmul(ps[6][:], ident[0:NSH, h:h + 1].to_broadcast([NSH, P]), d_cs[:], start=True, stop=True).then_inc(self.row_in_ps[0], 1)
                for hh in range(4):
                    pe.wait_ge(*upto(self.seg_w, hh + 1))
                    for c in range(4):
                        r = 64 * (hh % 2)
                        nc.tensor.matmul(ps[7 if hh < 2 else 2][r:r + 64, c * P:(c + 1) * P], x_dt[:, c, hh * 64:(hh + 1) * 64], s_w[hh][:, c],
                                         start=True, stop=True)
                for t in range(2):
                    if t == 0:
                        pe.wait_ge(*upto(self.prev_ready, 4))
                    else:
                        pe.wait_ge(*upto(self.y_tile, 1))
                    for c in range(4):
                        nc.tensor.matmul(ps[0][:, c * P:(c + 1) * P], s_prev[:, c, t * P:(t + 1) * P], ct[:, c * CH:(c + 1) * CH], start=True, stop=True)
                    for e in range(2):
                        h = 4 * g + 2 * t + e
                        last = nc.tensor.matmul(ps[1][64 * e:64 * e + 64, :], ident[0:NSH, h:h + 1].to_broadcast([NSH, 64]), d_ec[:],
                                                start=True, stop=True)
                    last.then_inc(self.y_in_ps[0], 1)
                for t in range(2):
                    pe.wait_ge(*upto(self.y_sq, t + 1))
                    last = nc.tensor.matmul(ps[3][:], ones[:], s_w[t][:, :, :].rearrange("p c l -> p (c l)"), start=t == 0, stop=t == 1)
                last.then_inc(self.y_sum[0], 1)

            def act(self, act):
                g = self.g
                act.wait_ge(*upto(self.ssd_turned, 1))
                astep(nc.scalar.copy(b_tok[:, :, :].rearrange("p c l -> p (c l)"), ps[0][:]))
                sig(nc.scalar, nc.scalar.copy(s_cb[:, :, :].rearrange("p c l -> p (c l)"), ps[3][:]), self.ssd_b)
                for hh in range(4):
                    act.wait_ge(*upto(self.seg_ready, hh + 1))
                    w = s_w[hh][:, :, :]
                    sig(nc.scalar, nc.scalar.activation(w, w, ACT.Exp), self.seg_exp)
                for t in range(2):
                    act.wait_ge(*upto(self.y_in_ps, t + 1))
                    sig(nc.scalar, nc.scalar.copy(s_y[0][:], ps[1][:]), self.e_read)
                    act.wait_ge(*upto(self.y_tile, t + 1))
                    sig(nc.scalar, nc.scalar.activation(s_w[t][:, :, :].rearrange("p c l -> p (c l)"), zx[:, 16 + 2 * g + t], ACT.Square), self.y_sq)
                act.wait_ge(*upto(self.y_sum, 1))
                astep(nc.scalar.activation(s_y[0][:], ps[3][:], ACT.Ln, scale=1.0 / 256, bias=epsv[:, 1:2]))
                sig(nc.scalar, nc.scalar.activation(s_y[0][:], s_y[0][:], ACT.Exp, scale=-0.5), self.y_rstd)
                for t in range(2):
                    act.wait_ge(*upto(self.y_scaled2, t + 1))
                    sig(nc.scalar, nc.scalar.copy(ssm_hi[2 * g + t][:], s_y[1][:]), self.y_hi)

            def dve(self, dve):
                g = self.g
                if self.mask_val:
                    dve.wait_ge(phase_in, self.mask_val)
                dve.wait_ge(*self.gate)
                dve.wait_ge(*upto(self.ssd_turned, 1))
                for c2 in range(2):
                    v = lambda a: a[:, 2 * c2:2 * c2 + 2, :].rearrange("p c (h q) -> p c h q", h=4)
                    tok = lambda q: s_tok[:, q, 2 * c2:2 * c2 + 2, 4 * g:4 * g + 4].unsqueeze(3).to_broadcast([P, 2, 4, 64])
                    last = nc.vector.tensor_tensor(v(x_dt), ps[1 + c2][:, :].rearrange("p (c h q) -> p c h q", c=2, h=4), tok(1), ALU.mult)
                sig(nc.vector, last, self.x_ready)
                dve.wait_ge(*upto(self.x_ready, 1))
                for c2 in range(2):
                    v = lambda a: a[:, 2 * c2:2 * c2 + 2, :].rearrange("p c (h q) -> p c h q", h=4)
                    tok = lambda q: s_tok[:, q, 2 * c2:2 * c2 + 2, 4 * g:4 * g + 4].unsqueeze(3).to_broadcast([P, 2, 4, 64])
                    last = nc.vector.tensor_tensor(v(x_dd), v(x_dt), tok(2), ALU.mult)
                sig(nc.vector, last, self.xd_ready)
                sig(nc.vector, nc.vector.memset(s_prev[:, 0], 0.0), self.prev_ready)
                dve.wait_ge(*upto(self.ssd_b, 1))

                def segment(hh):
                    h = 4 * g + hh
                    dve.wait_ge(*upto(self.row_in_ps, hh + 1))
                    for c in range(4):
                        last = nc.vector.scalar_tensor_tensor(s_w[hh][:, c], ps[6][:, c * P:(c + 1) * P], s_tok[:, 0, c, h:h + 1], ssd_mask[:],
                                                              ALU.subtract, ALU.add)
                    sig(nc.vector, last, self.seg_ready)

                for c in range(3):
                    dve.wait_ge(*upto(self.prev_ready, c + 1))
                    dst = s_prev[:, c + 1].rearrange("p (h q) -> p h q", h=4)
                    vstep(nc.vector.tensor_tensor(dst, s_prev[:, c].rearrange("p (h q) -> p h q", h=4),
                                                  s_cd[:, c, 4 * g:4 * g + 4].unsqueeze(2).to_broadcast([P, 4, 64]), ALU.mult))
                    dve.wait_ge(*upto(self.st_in_ps, max(c + 1, 2)))
                    sig(nc.vector, nc.vector.tensor_tensor(s_prev[:, c + 1], s_prev[:, c + 1], ps[4 + c // 2][:, (c % 2) * 256:(c % 2 + 1) * 256],
                                            ALU.add), self.prev_ready)
                for hh in range(5):
                    if hh < 4:
                        segment(hh)
                    if hh >= 1:
                        dve.wait_ge(*upto(self.seg_exp, hh))
                        w = s_w[hh - 1][:, :, :]
                        sig(nc.vector, nc.vector.tensor_tensor(w, w, s_cb[:, :, :], ALU.mult), self.seg_w)
                for t in range(2):
                    x_ = zx[:, 16 + 2 * g + t]
                    a, w = VEC["d_skip"]
                    dve.wait_ge(*upto(self.e_read, t + 1))
                    vstep(nc.vector.tensor_tensor(s_y[1][:], s_y[0][:], ps[0][:], ALU.mult))
                    vstep(nc.vector.tensor_tensor(s_y[1][:], s_y[1][:], ps[7 if t == 0 else 2][:], ALU.add))
                    vstep(nc.vector.scalar_tensor_tensor(s_y[1][:], x_, vec[:, a + 2 * g + t:a + 2 * g + t + 1], s_y[1][:], ALU.mult, ALU.add))
                    sig(nc.vector, nc.vector.tensor_tensor(x_, s_y[1][:], zx[:, 2 * g + t], ALU.mult), self.y_tile)
                dve.wait_ge(*upto(self.y_rstd, 1))
                for t in range(2):
                    sig(nc.vector, nc.vector.scalar_tensor_tensor(s_y[1][:], zx[:, 16 + 2 * g + t], V("ssm_norm", 2 * g + t), s_y[0][:], ALU.mult,
                                                   ALU.mult), self.y_scaled2)
                    dve.wait_ge(*upto(self.y_hi, t + 1))
                    sig(nc.vector, nc.vector.tensor_tensor(ssm_lo[2 * g + t][:], s_y[1][:], ssm_hi[2 * g + t][:].bitcast(f32), ALU.subtract), self.y_lo)

        class ConvFfn:

            def __init__(self, layer):
                self.layer = layer
                self.tap, self.silu, self.gated = cnt.take("ffn_tap", 6 * NH), cnt.take("ffn_silu", NH), cnt.take("ffn_gated", NH)
                self.hi, self.lo = cnt.take("hid_hi_ready", NH), cnt.take("hid_lo_ready", NH)
                self.done = upto(self.lo, NH, 2)

            def hid(self, buf, i, q):
                return buf[:, bass.ds(2 * i + q, 1)].rearrange("p o t -> p (o t)")

            def act(self, g, act, i, a):
                for q in range(2):
                    m = 2 * i + q
                    for s in range(2):
                        act.wait_ge(chunk_done, g.tile(i, 2 * q + s))
                        act.wait_ge(self.tap[0], 6 + self.tap[1] + 6 * m - 3 + 3 * s)
                        nc.scalar.copy(pad[s][:, 2:2 + TL], g.out(2 * q + s)).then_inc(mm_free, 1)
                    act.wait_ge(self.tap[0], 6 + self.tap[1] + 6 * m + 3)
                    nc.scalar.activation(wk[0][:], wk[0][:], ACT.Silu).then_inc(self.silu[0], 1)
                    act.wait_ge(self.gated[0], 1 + self.gated[1] + m + 1)
                    nc.scalar.copy(self.hid(hid_hi, i, q), wk[2][:]).then_inc(self.hi[0], 1)

            def dve(self, g, dve, i, a):
                for q in range(2):
                    m = 2 * i + q
                    dve.wait_ge(self.gated[0], 1 + self.gated[1] + m)
                    for s in range(2):
                        dve.wait_ge(mm_free, NBANK + g.tile0 + 4 * i + 2 * q + s + 1)
                        for j in range(3):
                            w = vec[:, bass.ds(VEC["ffn_conv"][0] + 132 * self.layer + 44 * j + 4 * i + 2 * q + s, 1)]
                            src = pad[s][:, j:j + TL]
                            if j:
                                dve.wait_ge(self.tap[0], 6 + self.tap[1] + 6 * m + 3 * s + j)
                                ins = nc.vector.scalar_tensor_tensor(wk[s][:], src, w, wk[s][:], ALU.mult, ALU.add)
                            else:
                                ins = nc.vector.tensor_scalar(wk[s][:], src, w, None, ALU.mult)
                            ins.then_inc(self.tap[0], 1)
                    dve.wait_ge(self.tap[0], 6 + self.tap[1] + 6 * m + 6)
                    dve.wait_ge(self.lo[0], 2 + self.lo[1] + m)
                    dve.wait_ge(self.silu[0], self.silu[1] + m + 1)
                    nc.vector.tensor_tensor(wk[2][:], wk[0][:], wk[1][:], ALU.mult).then_inc(self.gated[0], 1)
                    dve.wait_ge(self.hi[0], self.hi[1] + m + 1)
                    nc.vector.tensor_tensor(self.hid(hid_lo, i, q), wk[2][:], self.hid(hid_hi, i, q).bitcast(f32), ALU.subtract).then_inc(self.lo[0], 1)

        class Pads(Phase):

            def __init__(self, gate):
                super().__init__()
                self.gate, self.zeroed = gate, cnt.take("pads_zeroed", 2)

            def dve(self, dve):
                dve.wait_ge(*self.gate)
                for i in range(2):
                    sig(nc.vector, nc.vector.memset(pad[i][:], 0.0), self.zeroed)

            def act(self, act):
                act.wait_ge(*upto(self.zeroed, 2))

        class Load(Phase):

            def __init__(self):
                super().__init__()

            def sp(self, sp):
                sp.dma_start(vec[:], vecs).then_inc(const_in, 16)
                a, w = CST["ident"]
                sp.dma_start(ident[:], cst[:, a:a + w]).then_inc(const_in, 16)
                sp.dma_start(x[:, :, :], xT.rearrange("(k p) t -> p k t", p=P)).then_inc(const_in, 16)
                sp.dma_start(xc[:, :, :], ctxT.rearrange("(k p) t -> p k t", p=P)).then_inc(const_in, 16)

            def dve(self, dve):
                nc.vector.memset(ones[:], 1.0)
                nc.vector.memset(epsv[:, 0:1], EPS)
                vstep(nc.vector.memset(epsv[:, 1:2], GEPS))
                for sem_, n in SEEDS:
                    if n and sem_ is not mm_free and sem_ is not chunk_done and sem_ is not split_done:
                        dve.sem_inc(sem_, n)
                dve.wait_ge(const_in, 64)

            def act(self, act):
                act.sem_inc(mm_free, NBANK)
                act.wait_ge(const_in, 64)
                act.wait_ge(dve_step, 1)

            def pool(self, pool):
                pool.sem_inc(split_done, RAW)

            def pe(self, pe):
                pe.sem_inc(chunk_done, SPL)
                pe.wait_ge(dve_step, 1)
                pe.wait_ge(const_in, 64)

        class Store(Phase):
            def __init__(self, rms):
                super().__init__()
                self.rms, self.scaled = rms, cnt.take("out_scaled", ND)

            def dve(self, dve):
                dve.wait_ge(*self.rms.done)
                for k in range(ND):
                    sig(nc.vector, nc.vector.scalar_tensor_tensor(y[:, k], x[:, k], V("final_norm", k), rstd[:], ALU.mult, ALU.mult), self.scaled)

            def sp(self, sp):
                for k in range(ND):
                    sp.wait_ge(*upto(self.scaled, k + 1))
                    sp.dma_start(out[k * P:(k + 1) * P, :], y[:, k]).then_inc(stored, 16)
                sp.wait_ge(stored, 16 * ND)

        stored = cnt.take("stored", 0)[0]
        xt, xct = lambda k: x[:, k], lambda k: xc[:, k]
        yt, yct = lambda k: y[:, k], lambda k: yc[:, k]
        hhi, hlo = lambda k: h_hi[:, k], lambda k: h_lo[:, k]
        hrhs = lambda k: (h_hi[:, k], h_lo[:, k])
        crhs = lambda k: (c_hi[:, k], c_lo[:, k])
        hcrhs = lambda k: (h_hi[:, k, 0:TC], h_lo[:, k, 0:TC])
        always = lambda k: (const_in, 64)
        gain = lambda v, q, l=0: lambda k: gains[l][:, v, q, k:k + 1]
        shift = lambda v, q, l=0: lambda k: mods[l][:, v, 24 * q + k:24 * q + k + 1]
        vgain = lambda name, i=0: lambda k: V(name, i + k)
        same = lambda g: lambda k: g

        Load()
        ada_bufs0 = AdaBufs("ada0", 96 * K)
        rows0 = AdaRows(ada0, 0, ada_bufs0)
        AdaC(ada_bufs0, None)
        AdaFirst(rows0, 16)
        ada = AdaEnd(rows0, 0, 16, (0,))
        r = Rms(xt, ND, TL, D, 0, always)
        ap = Apply(xt, ND, TL, gain(0, 0), shift(0, 0), hhi, hlo, r, gate=ada.done)
        r = Rms(xct, ND, TC, D, 0, same(ap.done))
        ap = Apply(xct, ND, TC, gain(1, 0), shift(1, 0), lambda k: c_hi[:, k], lambda k: c_lo[:, k], r)
        gm = Gemm(w_ab_in, 24, 1, 8, hrhs, ctx_rhs=crhs, evac_act=z_evac_act, peel=(1, 2, 4), gate=ap.done,
                  rows=AdaTurns(rows0, 16, 8, 4))
        AdaEnd(rows0, 16, 48, (1, 2, 3))
        hp = HgPrep(gm.all_read)
        u = None
        for head in range(HEADS):
            for back in range(2):
                u = HgUnit(head, back, hp.val, gm.all_read)
            ho_ = HgOut(head, u)
        pl = Pool(upto(ho_.mix_lo, 1))
        gm = Gemm(w_ab_out, 8, 1, 8, lambda k: (mix_hi[k][:, LAT], mix_lo[k][:, LAT]), ctx_rhs=lambda k: (mix_hi[k][:, CTX], mix_lo[k][:, CTX]),
                  evac_act=y_evac(y, yc), gate=upto(pl.pool_lo, 4))
        r = Rms(yt, ND, TL, D, 0, same(gm.all_read))
        re = Residual(xt, yt, ND, TL, gain(0, 1), r)
        r = Rms(yct, ND, TC, D, 0, same(re.ready(ND - 1)))
        rc = Residual(xct, yct, ND, TC, gain(1, 1), r)

        def ffn(up, down, t, rhs, ap, evac, dst, hi_buf=hid_hi, lo_buf=hid_lo, rows_up=None, rows_down=None):
            g = Gemm(up, 2 * NH, 1, 8, rhs, t=t, evac_act=evac.act, evac_dve=evac.dve, gate_k=ap.tile_ready, rows=rows_up)
            return Gemm(down, 8, 2, KC, lambda k: (hi_buf[:, k, 0:t], lo_buf[:, k, 0:t]), t=t, evac_act=y_evac(dst), gate=evac.done,
                        peel=(2,) if rows_down else (), rows=rows_down)

        r = Rms(xt, ND, TL, D, 0, same(rc.ready(ND - 1)))
        ap = Apply(xt, ND, TL, gain(0, 2), shift(0, 1), hhi, hlo, r)
        gm = ffn(w_f0u, w_f0d, TL, hrhs, ap, Swiglu(TL, hid_hi, hid_lo), y)
        r = Rms(yt, ND, TL, D, 0, same(gm.all_read))
        re = Residual(xt, yt, ND, TL, gain(0, 3), r)
        r = Rms(xct, ND, TC, D, 0, same(re.ready(ND - 1)))
        ap = Apply(xct, ND, TC, gain(1, 2), shift(1, 1), lambda k: h_hi[:, k, 0:TC], lambda k: h_lo[:, k, 0:TC], r)
        ada_bufs1 = AdaBufs("ada1", 80 * K)
        rows1 = AdaRows(ada1, 1, ada_bufs1)
        AdaC(ada_bufs1, ap.done)
        gm = ffn(w_f0u, w_f0d, TC, hcrhs, ap, Swiglu(TC, hidc_hi, hidc_lo), yc2, hidc_hi, hidc_lo,
                 AdaTurns(rows1, 0, 4, 2 * NH // 4), AdaTurns(rows1, 44, 2, 2))
        ada = AdaEnd(rows1, 0, 48, (0, 1, 2, 3))
        r = Rms(lambda k: yc2[:, k], ND, TC, D, 0, same(gm.all_read))
        rc = Residual(xct, lambda k: yc2[:, k], ND, TC, gain(1, 3), r)

        z1 = arena("z1", [P, 12, TA], 48 * K)
        v1 = arena("v1", [P, 12, P], 84 * K)
        o1_hi = [arena(f"o1_hi{h}", [P, TL], (48 + 3 * h) * K, f32r) for h in range(8)]
        o1_lo = [arena(f"o1_lo{h}", [P, TL], (90 + 2 * h) * K, f32r) for h in range(8)]

        def z1_evac(g, act, i, a):
            for n in range(4):
                act.wait_ge(chunk_done, g.tile(i, n))
                dst = z1[:, bass.ds(4 * i + n, 1)].rearrange("p o t -> p (o t)")
                ins = nc.scalar.copy(dst[:, 0:TL], g.out(n))
                if a == 2:
                    ins = nc.scalar.copy(dst[:, TL:TA], g.ctx_out(n))
                ins.then_inc(mm_free, 1)

        r = Rms(xt, ND, TL, D, 0, same(rc.ready(ND - 1)))
        ap = Apply(xt, ND, TL, gain(0, 0, 1), shift(0, 0, 1), hhi, hlo, r)
        r = Rms(xct, ND, TC, D, 0, same(ap.done))
        ap = Apply(xct, ND, TC, gain(1, 0, 1), shift(1, 0, 1), lambda k: c_hi[:, k], lambda k: c_lo[:, k], r)
        gm = Gemm(w_att_in, 12, 1, 8, hrhs, ctx_rhs=crhs, ctx_from=8, evac_act=z1_evac, peel=(2,), gate=ap.done)
        rp = Rope([(z1[:, j, 0:TL], TL, V("qn")) for j in range(8)] + [(z1[:, 8 + j], TA, V("kn")) for j in range(2)], 1, gm.all_read, r_t)
        tk = Tokens([(z1[:, 10 + v, c * P:(c + 1) * P], v1[:, v * 6 + c]) for v in range(2) for c in range(6)], rp.done)
        at_ = Attention([dict(q=[z1[:, h, n * P:(n + 1) * P]] * 2,
                              segs=[(z1[:, 8 + h // 4, 0:TL], TL, None), (z1[:, 8 + h // 4, TL:TA], TC, None)],
                              values=[v1[:, (h // 4) * 6 + c] for c in range(6)],
                              hi=o1_hi[h][:, n * P:(n + 1) * P], lo=o1_lo[h][:, n * P:(n + 1) * P])
                         for h in range(8) for n in range(4)], tk.done)
        gm = Gemm(w_att_out, 8, 1, 8, lambda k: (o1_hi[k][:], o1_lo[k][:]), evac_act=y_evac(y), gate=at_.done)
        r = Rms(yt, ND, TL, D, 0, same(gm.all_read))
        re = Residual(xt, yt, ND, TL, gain(0, 1, 1), r)
        r = Rms(xt, ND, TL, D, 0, re.ready)
        ap = Apply(xt, ND, TL, gain(0, 2, 1), shift(0, 1, 1), hhi, hlo, r)
        gm = ffn(w_f1u, w_f1d, TL, hrhs, ap, Swiglu(TL, hid_hi, hid_lo), y)
        r = Rms(yt, ND, TL, D, 0, same(gm.all_read))
        re = Residual(xt, yt, ND, TL, gain(0, 3, 1), r)

        r = Rms(xt, ND, TL, D, 0, re.ready)
        ap = Apply(xt, ND, TL, vgain("a_norm"), None, hhi, hlo, r)
        Pads(ap.done)
        sc = SsmConv()
        gm = Gemm(w_ssm, 48, 1, 8, hrhs, evac_act=sc.act, evac_dve=sc.dve, peel=(4,), gate_k=ap.tile_ready)
        dt = DtPart(upto(sc.out, 32, 2))
        s = None
        for g in range(NG):
            s = Ssd(g, s.done if s else dt.done, dt.val if g == 0 else None)
        gm = Gemm(w_ssm_out, 8, 2, 8, lambda k: (ssm_hi[k][:], ssm_lo[k][:]), evac_act=y_evac(y), gate=s.done)
        re = Residual(xt, yt, ND, TL, None, None, gate=gm.all_read)

        def conv_ffn(layer, up, down, r, gate_pads):
            ap = Apply(xt, ND, TL, vgain("ffn_norm", 8 * layer), None, hhi, hlo, r)
            Pads(ap.done)
            gm = ffn(up, down, TL, hrhs, ap, ConvFfn(layer), y)
            return Residual(xt, yt, ND, TL, None, None, gate=gm.all_read)

        re = conv_ffn(0, w_f2u, w_f2d, Rms(xt, ND, TL, D, 0, re.ready), None)

        kv = arena("kv", [P, 12, TL], 32 * K)
        q2 = arena("q2", [P, 24, TL], 56 * K)
        v2 = arena("v2", [P, 24, P], 104 * K)
        band, dil4, dil16 = arena("band", [P, 256], 116 * K), arena("dil4", [P, 512], 117 * K), arena("dil16", [P, 512], 119 * K)
        o2_hi = [arena(f"o2_hi{h}", [P, TL], (56 + 2 * h) * K, f32r) for h in range(8)]
        o2_lo = [arena(f"o2_lo{h}", [P, TL], (72 + 2 * h) * K, f32r) for h in range(8)]
        r = Rms(xt, ND, TL, D, 0, re.ready)
        ap = Apply(xt, ND, TL, vgain("kv_norm"), None, hhi, hlo, r)
        gm = Gemm(w_kv, 12, 1, 8, hrhs, evac_act=y_evac(kv), gate_k=ap.tile_ready)
        ap = Apply(xt, ND, TL, vgain("b_norm"), None, hhi, hlo, r, gate=gm.all_read)
        gm = Gemm(w_q, 24, 1, 8, hrhs, evac_act=y_evac(q2), gate_k=ap.tile_ready)
        rp = Rope([(kv[:, j], TL, None) for j in range(6)] + [(q2[:, j], TL, None) for j in range(24)], 2, gm.all_read, s_y)
        tk = Tokens([(kv[:, 6 + v, c * P:(c + 1) * P], v2[:, v * 4 + c]) for v in range(6) for c in range(4)], rp.done)

        def dilated(h, n):
            kh = lambda g: kv[:, 2 * g + h // 4]
            first = max(n - 1, 0)
            near = (n + 1 - first) * P
            return dict(q=[q2[:, 8 * g + h, n * P:(n + 1) * P] for g in range(3)],
                        segs=[(kh(0)[:, first * P:(n + 1) * P], near, band[:, 256 - near:256]),
                              (kh(1)[:, 0:(n + 1) * P], (n + 1) * P, dil4[:, (3 - n) * P:512]),
                              (kh(2)[:, 0:(n + 1) * P], (n + 1) * P, dil16[:, (3 - n) * P:512])],
                        values=[v2[:, (h // 4) * 4 + c] for c in range(first, n + 1)]
                        + [v2[:, (2 * g + h // 4) * 4 + c] for g in (1, 2) for c in range(n + 1)],
                        hi=o2_hi[h][:, n * P:(n + 1) * P], lo=o2_lo[h][:, n * P:(n + 1) * P])

        at_ = Attention([dilated(h, n) for h in range(8) for n in range(4)], tk.done,
                        masks=(("band", band[:]), ("dil4", dil4[:]), ("dil16", dil16[:])))
        gm = Gemm(w_o, 8, 1, 8, lambda k: (o2_hi[k][:], o2_lo[k][:]), evac_act=y_evac(y), gate=at_.done)
        re = Residual(xt, yt, ND, TL, None, None, gate=gm.all_read)
        re = conv_ffn(1, w_f3u, w_f3d, Rms(xt, ND, TL, D, 0, re.ready), None)
        r = Rms(xt, ND, TL, D, 0, re.ready)
        Store(r)
        SEEDS = [(cnt.sems[n], v) for n, v in (("hid_lo_ready", 2), ("conv_tap", 4), ("conv_out", 2), ("ffn_tap", 6), ("ffn_gated", 1), ("ada_used", 4)) if n in cnt.sems]

        block = ctx.enter_context(nc.Block())

        @block.sync
        def _(sp):
            for ph in phases[:STOP]:
                ph.sp(sp)

        @block.gpsimd
        def _(pool):
            for ph in phases[:STOP]:
                ph.pool(pool)

        @block.scalar
        def _(act):
            for ph in phases[:STOP]:
                ph.act(act)

        @block.vector
        def _(dve):
            for ph in phases[:STOP]:
                ph.dve(dve)

        @block.tensor
        def _(pe):
            for ph in phases[:STOP]:
                ph.pe(pe)


def tables():
    c = np.zeros((P, NCST), np.float32)

    def put(name, v):
        a, w = CST[name]
        c[:v.shape[0], a:a + w] = v.reshape(v.shape[0], w)

    put("ident", np.eye(P))
    t = np.arange(TL)
    inv = 10000.0 ** (-np.arange(32, dtype=np.float32) / np.float32(32))
    pos = [(t // 64).astype(np.float32), (t % 64).astype(np.float32)]
    ang = [p[None, :] * inv.astype(np.float32)[:, None] for p in pos]
    put("cos1", np.concatenate([np.cos(ang[0])] * 2 + [np.cos(ang[1])] * 2))
    put("sin1", np.concatenate([np.sin(ang[0])] * 2 + [np.sin(ang[1])] * 2))
    inv2 = np.power(np.float32(500000.0), -np.arange(0, 32, 2, dtype=np.float32) / np.float32(32))
    a2 = t.astype(np.float32)[None, :] * inv2[:, None]
    put("cos2", np.concatenate([np.cos(a2), np.cos(a2), np.ones((96, TL))]))
    put("sin2", np.concatenate([np.sin(a2), np.sin(a2), np.zeros((96, TL))]))
    for name, halves in (("rot1", [(0, 32), (64, 32)]), ("rot2", [(0, 16)])):
        r = np.zeros((P, P))
        for a, h in halves:
            for i in range(h):
                r[a + h + i, a + i] = -1.0
                r[a + i, a + h + i] = 1.0
        put(name, r)
    m = np.zeros((P, 2, 6, P))
    s_, t_ = np.arange(P)[:, None], np.arange(P)[None, :]
    for back in range(2):
        for l, half in enumerate(LEVELS):
            pair = (s_ // (2 * half) == t_ // (2 * half)) & (s_ // half != t_ // half) & ((s_ > t_) if back else (s_ < t_))
            m[:, back, 0 if l < 2 else l - 1] += pair
        m[:, back, 0] += s_ == t_
    put("hg_mask", m)
    q_, k_ = np.arange(P)[:, None], np.arange(P)[None, :]
    put("band", np.concatenate([np.where(k_ >= q_, 0, NEG), np.where(k_ <= q_, 0, NEG)], 1))
    for name, d in (("dil4", 4), ("dil16", 16)):
        same = (q_ - k_) % d == 0
        put(name, np.concatenate([np.where(same, 0, NEG)] * 3 + [np.where(same & (k_ <= q_), 0, NEG)], 1))
    put("ssd_mask", np.where(s_ <= t_, 0, NEG))
    pi = np.zeros((4, TA))
    for g in range(4):
        w = 2 << g
        for a, n in ((0, TC), (TC, TL)):
            tt = np.arange(n)
            pi[g, a:a + n] = 1.0 / (np.clip(tt - w // 2 + w, 0, n) - np.clip(tt - w // 2, 0, n))
    put("pool_inv", np.broadcast_to(pi.reshape(1, -1), (P, 4 * TA)))
    return c


def kernel(**inp):
    import concourse.bacc as bacc
    from concourse.bass_utils import run_bass_kernel_spmd as run

    inp = {k: np.asarray(v) for k, v in inp.items()}

    def chunks(w, kt, order=None):
        k, f = w.shape
        v = w.reshape(k // (kt * P), kt, P, f // P, P).transpose(3, 0, 2, 1, 4)
        if order is not None:
            v = v[order]
        return np.ascontiguousarray(v.reshape(-1, P, kt, P))

    def cols(v):
        return np.ascontiguousarray(v.reshape(-1, P).T)

    def pairs(n):
        return np.arange(2 * n).reshape(2, n).T.reshape(-1)

    vecs = np.zeros((P, NVEC), np.float32)

    def put(name, v):
        a, w = VEC[name]
        vecs[:v.shape[0], a:a + w] = v

    put("ada_b", cols(inp["ada_b"]))
    put("norm_g", cols(inp["norm_g"]))
    put("pool_scale", cols(inp["pool_scale"]))
    put("hg_lower", cols(inp["hg_lower"]))
    put("onorm", cols(inp["hg_onorm_g"]))
    put("qn", cols(inp["att_qnorm_g"]))
    put("kn", cols(inp["att_knorm_g"]))
    put("a_norm", cols(inp["a_norm_2"]))
    put("conv_w", cols(inp["ssm_conv_w_2"]))
    put("conv_b", cols(inp["ssm_conv_b_2"]))
    put("ssm_norm", cols(inp["ssm_norm_2"]))
    put("d_skip", cols(np.repeat(inp["ssm_d_2"].reshape(-1), 64)))
    put("kv_norm", cols(inp["kv_norm_2"]))
    put("b_norm", cols(inp["b_norm_2"]))
    put("ffn_norm", cols(inp["ffn_norm_2"]))
    fc = inp["ffn_conv_w_2"].reshape(2, 3, 2 * NH, P)[:, :, pairs(NH)]
    put("ffn_conv", cols(fc))
    put("final_norm", cols(inp["final_norm_2"]))
    put("dt_bias", inp["ssm_dt_bias_2"].reshape(NSH, 1))
    put("a_log", inp["ssm_a_log_2"].reshape(NSH, 1))

    head_order = [0, 1, 2, 3, 20, 21, 22, 23] + [4 + 4 * part + h for h in range(4) for part in range(4)]
    ssm = inp["ssm_w_in_2"][0]
    arrays = {
        "xT": np.ascontiguousarray(inp["x"][0].T), "ctxT": np.ascontiguousarray(inp["ctx"][0].T),
        "cvec": np.stack([inp["c"].reshape(-1), inp["c_ctx"].reshape(-1)]), "vecs": vecs, "cst": tables(),
        "ada0": np.ascontiguousarray(inp["ada_w"][0].T.reshape(48, P, D)), "ada1": np.ascontiguousarray(inp["ada_w"][1].T.reshape(48, P, D)),
        "w_ab_in": chunks(inp["ab_w_in"][0], 8, head_order), "w_ab_out": chunks(inp["ab_w_out"][0], 8),
        "w_pool": np.ascontiguousarray(inp["pool_w"][0].transpose(1, 0, 2)),
        "w_f0u": chunks(inp["ffn_w_in"][0], 8, pairs(NH)), "w_f0d": chunks(inp["ffn_w_out"][0], KC),
        "w_att_in": chunks(inp["att_w_in"][0], 8), "w_att_out": chunks(inp["att_w_out"][0], 8),
        "w_f1u": chunks(inp["ffn_w_in"][1], 8, pairs(NH)), "w_f1d": chunks(inp["ffn_w_out"][1], KC),
        "w_ssm": chunks(ssm[:, :6144], 8), "w_dt": np.ascontiguousarray(ssm[:, 6144:].reshape(ND, P, NSH).transpose(1, 0, 2)),
        "w_ssm_out": chunks(inp["ssm_w_out_2"][0], 8), "w_kv": chunks(inp["w_kv_2"], 8), "w_q": chunks(inp["att_w_q_2"][0], 8),
        "w_o": chunks(inp["att_w_o_2"][0], 8),
        "w_f2u": chunks(inp["ffn_w_up_2"][0], 8, pairs(NH)), "w_f2d": chunks(inp["ffn_w_down_2"][0], KC),
        "w_f3u": chunks(inp["ffn_w_up_2"][1], 8, pairs(NH)), "w_f3d": chunks(inp["ffn_w_down_2"][1], KC),
    }
    nc = bacc.Bacc("TRN2", target_bir_lowering=False, num_devices=1)
    args = [nc.dram_tensor(n, a.shape, mybir.dt.from_np(a.dtype), kind="ExternalInput").ap() for n, a in arrays.items()]
    out = nc.dram_tensor("out", (D, TL), mybir.dt.float32, kind="ExternalOutput").ap()
    build(nc, *args, out)
    r = run(nc, [arrays], core_ids=[0])
    return np.ascontiguousarray(r.results[0]["out"].T).reshape(1, TL, D)
```
